# Optimizing a Trainium2 kernel written in Bass

```python
import math
import jax, jax.numpy as jnp
from jax import lax
import numpy as np

D_MODEL = 2048
BATCH = 1
SEQ = 256
DEPTH = 2

D_MIX = D_MODEL
HEAD_DIM = 128
N_HEADS_A = 8
N_HEADS_B = 8
D_A = N_HEADS_A * HEAD_DIM
D_B = N_HEADS_B * HEAD_DIM
IDX_HEADS = 16
IDX_DIM = 64
TOPK_MAX = 256
Q_BLOCK = 128
RET_CHUNK = 128
N_BUCKETS = 32
MAX_EXACT = 16
MAX_DISTANCE = 128
ROPE_BASE = 10000.0
EPS = 1e-6
IN_SIZES = (D_A, HEAD_DIM, HEAD_DIM, D_A, IDX_HEADS * IDX_DIM, IDX_DIM, IDX_HEADS, D_B, D_B, D_B, D_B)
N_IN = 2 * D_A + 2 * HEAD_DIM + IDX_HEADS * IDX_DIM + IDX_DIM + IDX_HEADS + 4 * D_B


def rmsnorm(x, g):
    xf = x.astype(jnp.float32)
    y = xf * lax.rsqrt(jnp.mean(xf * xf, axis=-1, keepdims=True) + EPS)
    return (y * g.astype(jnp.float32)).astype(x.dtype)

def head_groupnorm(x, g):
    xf = x.astype(jnp.float32)
    mu = jnp.mean(xf, axis=-1, keepdims=True)
    var = jnp.mean(jnp.square(xf - mu), axis=-1, keepdims=True)
    y = (xf - mu) * lax.rsqrt(var + EPS)
    B, S, H, D = x.shape
    return (y.reshape(B, S, H * D) * g.astype(jnp.float32)).astype(x.dtype)

def rotary(x, pos):
    half = x.shape[-1] // 2
    inv = ROPE_BASE ** (-jnp.arange(half, dtype=jnp.float32) / half)
    ang = pos.astype(jnp.float32)[..., None] * inv
    cos = jnp.cos(ang)[:, :, None, :]
    sin = jnp.sin(ang)[:, :, None, :]
    xf = x.astype(jnp.float32)
    x1, x2 = xf[..., :half], xf[..., half:]
    return jnp.concatenate([x1 * cos - x2 * sin, x1 * sin + x2 * cos], axis=-1).astype(x.dtype)

def t5_bucket(rel):
    rel = jnp.maximum(rel, 0)
    relf = jnp.maximum(rel, 1).astype(jnp.float32)
    large = MAX_EXACT + (jnp.log(relf / MAX_EXACT) / math.log(MAX_DISTANCE / MAX_EXACT)
                         * (N_BUCKETS - MAX_EXACT)).astype(jnp.int32)
    large = jnp.minimum(large, N_BUCKETS - 1)
    return jnp.where(rel < MAX_EXACT, rel, large)

def sparse_attention(q, k, v, q_idx, k_idx, w_idx, pos, rel_bias):
    B, S, H, Dh = q.shape
    n_blk = S // Q_BLOCK
    top_k = min(TOPK_MAX, S // 4)
    scale = HEAD_DIM ** -0.5
    key_pos = jnp.arange(S)

    def block(xs):
        qb, qib, wb, pb, start = xs
        t = start + jnp.arange(Q_BLOCK)
        dots = jnp.einsum('bqhd,bsd->bqhs', qib, k_idx).astype(jnp.float32)
        I = jnp.einsum('bqh,bqhs->bqs', wb.astype(jnp.float32), jax.nn.relu(dots))
        causal = key_pos[None, :] <= t[:, None]
        I = jnp.where(causal[None], I, -jnp.inf)
        _, sel = lax.top_k(I, top_k)
        valid = sel <= t[None, :, None]
        ks = jax.vmap(lambda kb, ib: kb[ib])(k, sel)
        vs = jax.vmap(lambda vb, ib: vb[ib])(v, sel)
        ps = jax.vmap(lambda pb_, ib: pb_[ib])(pos, sel)
        bias = rel_bias[t5_bucket(pb[:, :, None] - ps)]
        bias = jnp.moveaxis(bias, -1, 2).astype(jnp.float32)
        logits = jnp.einsum('bqhd,bqkd->bqhk', qb, ks).astype(jnp.float32) * scale + bias
        logits = jnp.where(valid[:, :, None, :], logits, -jnp.inf)
        p = jax.nn.softmax(logits, axis=-1).astype(v.dtype)
        return jnp.einsum('bqhk,bqkd->bqhd', p, vs)

    def to_blocks(a):
        return a.reshape((B, n_blk, Q_BLOCK) + a.shape[2:]).swapaxes(0, 1)

    xs = (to_blocks(q), to_blocks(q_idx), to_blocks(w_idx), to_blocks(pos),
          jnp.arange(n_blk) * Q_BLOCK)
    out = lax.map(block, xs)
    return out.swapaxes(0, 1).reshape(B, S, H, Dh)

def retention(q, k, v):
    B, S, H, D = q.shape
    C = RET_CHUNK
    nC = S // C
    log_g = jnp.log1p(-jnp.exp2(-5.0 - jnp.arange(H, dtype=jnp.float32)))
    i = jnp.arange(C, dtype=jnp.float32)
    diff = i[:, None] - i[None, :]
    dmask = jnp.where(diff >= 0, jnp.exp(log_g[:, None, None] * jnp.maximum(diff, 0.0)), 0.0)
    qc = q.astype(jnp.float32).reshape(B, nC, C, H, D)
    kc = k.astype(jnp.float32).reshape(B, nC, C, H, D)
    vc = v.astype(jnp.float32).reshape(B, nC, C, H, D)
    s_in = jnp.einsum('bnihd,bnjhd->bnhij', qc, kc) * dmask
    intra = jnp.einsum('bnhij,bnjhd->bnihd', s_in, vc)
    zeta = jnp.exp(log_g[None, :] * (C - 1.0 - i)[:, None])
    u = jnp.einsum('bnjhd,bnjhe->bnhde', kc * zeta[None, None, :, :, None], vc)
    g_chunk = jnp.exp(log_g * C)[None, :, None, None]

    def step(R, u_n):
        return g_chunk * R + u_n, R

    _, R_prev = lax.scan(step, jnp.zeros((B, H, D, D), jnp.float32), u.swapaxes(0, 1))
    R_prev = R_prev.swapaxes(0, 1)
    xi = jnp.exp(log_g[None, :] * (i + 1.0)[:, None])
    cross = jnp.einsum('bnihd,bnhde->bnihe', qc, R_prev) * xi[None, None, :, :, None]
    return (intra + cross).reshape(B, S, H, D)

def first_inputs(seed: int = 0) -> dict:
    key = jax.random.key(seed)
    ks = jax.random.split(key, 12)
    f32 = jnp.float32
    x = jax.random.normal(ks[0], (BATCH, SEQ, D_MODEL), f32)
    c = jax.random.normal(ks[1], (BATCH, D_MODEL), f32)
    positions = jnp.broadcast_to(jnp.arange(SEQ, dtype=jnp.int32)[None, :], (BATCH, SEQ))
    rel_bias = 0.5 * jax.random.normal(ks[2], (N_BUCKETS, N_HEADS_A), f32)
    norm_gain = 1.0 + 0.05 * jax.random.normal(ks[3], (DEPTH, D_MODEL), f32)
    w_mod = 0.5 * D_MODEL ** -0.5 * jax.random.normal(ks[4], (DEPTH, D_MODEL, 3 * D_MODEL), f32)
    b_mod = 0.02 * jax.random.normal(ks[5], (DEPTH, 3 * D_MODEL), f32)
    w_in = D_MODEL ** -0.5 * jax.random.normal(ks[6], (DEPTH, D_MODEL, N_IN), f32)
    q_norm_gain = 1.0 + 0.05 * jax.random.normal(ks[7], (DEPTH, HEAD_DIM), f32)
    k_norm_gain = 1.0 + 0.05 * jax.random.normal(ks[8], (DEPTH, HEAD_DIM), f32)
    ret_norm_gain = 1.0 + 0.05 * jax.random.normal(ks[9], (DEPTH, D_B), f32)
    w_out = D_MIX ** -0.5 * jax.random.normal(ks[10], (DEPTH, D_MIX, D_MODEL), f32)
    return {"x": x, "c": c, "positions": positions, "rel_bias": rel_bias,
            "norm_gain": norm_gain, "w_mod": w_mod, "b_mod": b_mod, "w_in": w_in,
            "q_norm_gain": q_norm_gain, "k_norm_gain": k_norm_gain,
            "ret_norm_gain": ret_norm_gain, "w_out": w_out}

def first_block(x, c, positions, rel_bias, norm_gain, w_mod, b_mod, w_in,
              q_norm_gain, k_norm_gain, ret_norm_gain, w_out):
    B, S, _ = x.shape
    split_points = [int(p) for p in np.cumsum(IN_SIZES)[:-1]]
    c_act = jax.nn.silu(c)
    for l in range(DEPTH):
        mod = c_act @ w_mod[l] + b_mod[l]
        shift, scale, gate = jnp.split(mod, 3, axis=-1)
        h = rmsnorm(x, norm_gain[l]) * (1.0 + scale[:, None, :]) + shift[:, None, :]
        proj = h @ w_in[l]
        q_a, k_a, v_a, g_a, q_i, k_i, w_i, q_b, k_b, v_b, g_b = jnp.split(proj, split_points, axis=-1)
        q_a = rmsnorm(q_a.reshape(B, S, N_HEADS_A, HEAD_DIM), q_norm_gain[l])
        k_a = rmsnorm(k_a, k_norm_gain[l])
        att = sparse_attention(q_a, k_a, v_a, q_i.reshape(B, S, IDX_HEADS, IDX_DIM), k_i, w_i,
                               positions, rel_bias)
        y_a = att.reshape(B, S, D_A) * jax.nn.silu(g_a)
        q_b = rotary(q_b.reshape(B, S, N_HEADS_B, HEAD_DIM), positions)
        k_b = rotary(k_b.reshape(B, S, N_HEADS_B, HEAD_DIM), positions) * (HEAD_DIM ** -0.5)
        ret = retention(q_b, k_b, v_b.reshape(B, S, N_HEADS_B, HEAD_DIM))
        y_b = head_groupnorm(ret, ret_norm_gain[l]).astype(x.dtype) * jax.nn.silu(g_b)
        y = jnp.concatenate([y_a, y_b], axis=-1) @ w_out[l]
        x = x + gate[:, None, :] * y
    return x


DEPTH_2 = 1

PLE_DIM = 256
D_CONV = D_MODEL // 2
CONV_K = 3
D_REC = D_MODEL // 2
HG_HEAD_DIM = 128
HG_HEADS = D_REC // HG_HEAD_DIM
HG_VDIM = D_REC // HG_HEADS
CHUNK = 64
LB_FLOOR = 1e-30
IN_SPLITS = [D_CONV, D_CONV, D_CONV, D_CONV,
             D_REC, D_REC, D_REC, D_REC,
             D_MODEL, D_MODEL]
IN_COLS = sum(IN_SPLITS)


def rmsnorm_2(x, g):
    xf = x.astype(jnp.float32)
    y = xf * lax.rsqrt(jnp.mean(xf * xf, axis=-1, keepdims=True) + EPS)
    return (y * g.astype(jnp.float32)).astype(x.dtype)

def causal_dwconv3(u, w):
    up = jnp.pad(u, ((0, 0), (CONV_K - 1, 0), (0, 0)))
    s = u.shape[1]
    return up[:, 0:s] * w[0] + up[:, 1:s + 1] * w[1] + up[:, 2:s + 2] * w[2]

def hgrn2_chunked(q, k, v, log_f):
    bn, sn, h, kd = q.shape
    vd = v.shape[-1]
    n = sn // CHUNK

    def to_chunks(t):
        return t.reshape(bn, n, CHUNK, h, t.shape[-1]).transpose(1, 0, 3, 2, 4)

    qc, kc, vc, fc = to_chunks(q), to_chunks(k), to_chunks(v), to_chunks(log_f)
    causal = jnp.tril(jnp.ones((CHUNK, CHUNK), dtype=bool))[:, :, None]
    causal_f = causal.astype(jnp.float32)

    def step(state, inp):
        qn, kn, vn, fn = inp
        b = jnp.cumsum(fn, axis=2)
        inter = jnp.einsum('bhtk,bhkv->bhtv', qn * jnp.exp(b), state)
        diff = b[:, :, :, None, :] - b[:, :, None, :, :]
        decay = jnp.exp(jnp.where(causal, diff, 0.0)) * causal_f
        a = jnp.einsum('bhtk,bhtsk,bhsk->bhts', qn, decay, kn)
        o = inter + jnp.einsum('bhts,bhsv->bhtv', a, vn)
        b_last = b[:, :, -1:, :]
        state = (jnp.exp(b_last[:, :, 0, :])[..., None] * state
                 + jnp.einsum('bhsk,bhsv->bhkv', kn * jnp.exp(b_last - b), vn))
        return state, o

    s0 = jnp.zeros((bn, h, kd, vd), jnp.float32)
    _, o = lax.scan(step, s0, (qc, kc, vc, fc))
    return o.transpose(1, 0, 3, 2, 4).reshape(bn, sn, h, vd)

def second_inputs(seed: int = 0) -> dict:
    key = jax.random.key(seed)
    ks = jax.random.split(key, 16)
    f32 = jnp.float32
    nrm = lambda k, shp: jax.random.normal(k, shp, f32)
    return {
        "x": nrm(ks[0], (BATCH, SEQ, D_MODEL)),
        "p": nrm(ks[1], (DEPTH_2, BATCH, SEQ, PLE_DIM)),
        "norm_mix_g": 1.0 + 0.02 * nrm(ks[2], (DEPTH_2, D_MODEL)),
        "w_in": nrm(ks[3], (DEPTH_2, D_MODEL, IN_COLS)) * D_MODEL ** -0.5,
        "conv_w": nrm(ks[4], (DEPTH_2, CONV_K, D_CONV)) * CONV_K ** -0.5,
        "lb_param": 0.1 * nrm(ks[5], (DEPTH_2, D_REC)),
        "hg_norm_g": 1.0 + 0.02 * nrm(ks[6], (DEPTH_2, D_REC)),
        "w_a_out": nrm(ks[7], (DEPTH_2, D_CONV, D_MODEL)) * D_CONV ** -0.5,
        "w_b_out": nrm(ks[8], (DEPTH_2, D_REC, D_MODEL)) * D_REC ** -0.5,
        "w_o": nrm(ks[9], (DEPTH_2, D_MODEL, D_MODEL)) * D_MODEL ** -0.5,
        "ple_norm_g": 1.0 + 0.02 * nrm(ks[10], (DEPTH_2, D_MODEL)),
        "w_ple_gate": nrm(ks[11], (DEPTH_2, D_MODEL, D_MODEL)) * D_MODEL ** -0.5,
        "w_ple_proj": nrm(ks[12], (DEPTH_2, PLE_DIM, D_MODEL)) * PLE_DIM ** -0.5,
        "final_norm_g": 1.0 + 0.02 * nrm(ks[13], (D_MODEL,)),
    }

def second_block(x, p, norm_mix_g, w_in, conv_w, lb_param, hg_norm_g, w_a_out, w_b_out,
              w_o, ple_norm_g, w_ple_gate, w_ple_proj, final_norm_g):
    dt = x.dtype
    bn, sn, _ = x.shape
    lb_sm = jax.nn.softmax(lb_param.astype(jnp.float32), axis=0)
    lb_all = jnp.cumsum(lb_sm, axis=0) - lb_sm[0]
    split_idx = [int(s) for s in np.cumsum(IN_SPLITS)[:-1]]

    for i in range(DEPTH_2):
        h = rmsnorm_2(x, norm_mix_g[i])
        u = h @ w_in[i]
        c_g, b_g, xa, za, q, fl, iv, og, ga, gb = jnp.split(u, split_idx, axis=-1)

        ya = b_g * causal_dwconv3(c_g * xa, conv_w[i]) * jax.nn.silu(za)

        lb = jnp.clip(lb_all[i], 0.0, 1.0 - 1e-6)
        flf = fl.astype(jnp.float32)
        log_f = jnp.logaddexp(jnp.log(jnp.maximum(lb, LB_FLOOR)),
                              jnp.log1p(-lb) + jax.nn.log_sigmoid(flf))
        kk = (1.0 - lb) * jax.nn.sigmoid(-flf)
        hshape = (bn, sn, HG_HEADS, HG_HEAD_DIM)
        o = hgrn2_chunked(jax.nn.silu(q.astype(jnp.float32)).reshape(hshape),
                          kk.reshape(hshape),
                          iv.astype(jnp.float32).reshape(bn, sn, HG_HEADS, HG_VDIM),
                          log_f.reshape(hshape))
        o = o * lax.rsqrt(jnp.mean(o * o, axis=-1, keepdims=True) + EPS)
        o = o.reshape(bn, sn, D_REC) * hg_norm_g[i].astype(jnp.float32)
        yb = o.astype(dt) * jax.nn.silu(og)

        m = jax.nn.sigmoid(ga) * (ya @ w_a_out[i]) + jax.nn.sigmoid(gb) * (yb @ w_b_out[i])
        x = x + m @ w_o[i]

        gate = jax.nn.sigmoid(rmsnorm_2(x, ple_norm_g[i]) @ w_ple_gate[i])
        x = x + gate * (p[i] @ w_ple_proj[i])

    return rmsnorm_2(x, final_norm_g)


def setup_inputs(seed=0):
    out = dict(first_inputs(seed))
    for name, value in second_inputs(seed + 1).items():
        if name != "x":
            out[name + "_2"] = value
    return out


def reference(
    x, c, positions, rel_bias, norm_gain, w_mod, b_mod, w_in, q_norm_gain, k_norm_gain,
    ret_norm_gain, w_out, p_2, norm_mix_g_2, w_in_2, conv_w_2, lb_param_2, hg_norm_g_2,
    w_a_out_2, w_b_out_2, w_o_2, ple_norm_g_2, w_ple_gate_2, w_ple_proj_2, final_norm_g_2,
):
    x = first_block(
        x, c, positions, rel_bias, norm_gain, w_mod, b_mod, w_in, q_norm_gain, k_norm_gain,
        ret_norm_gain, w_out,
    )
    return second_block(
        x, p_2, norm_mix_g_2, w_in_2, conv_w_2, lb_param_2, hg_norm_g_2, w_a_out_2, w_b_out_2,
        w_o_2, ple_norm_g_2, w_ple_gate_2, w_ple_proj_2, final_norm_g_2,
    )


_drawn_inputs = setup_inputs


def setup_inputs(seed=0):
    import zlib

    import numpy as np

    out = dict(_drawn_inputs(seed))
    spreads = {}
    factors = {'q_norm_gain': 8.0,
     'k_norm_gain': 8.0,
     'ret_norm_gain': 4.968,
     'norm_mix_g_2': 4.236,
     'hg_norm_g_2': 64.0,
     'ple_norm_g_2': 64.0,
     'final_norm_g_2': 7.743,
     'p_2': 8.0,
     'w_ple_gate_2': 8.0,
     'w_ple_proj_2': 8.0}
    for name, (base, spread) in spreads.items():
        noise = np.random.default_rng([zlib.crc32(name.encode()), seed]).standard_normal(out[name].shape)
        drawn = base * np.exp(spread * noise) if base else spread * noise
        out[name] = __import__('jax').numpy.asarray(drawn.astype(out[name].dtype))
    for name, factor in factors.items():
        out[name] = (out[name] * factor).astype(out[name].dtype)
    return out
```

```python
from contextlib import ExitStack, contextmanager
import math

import numpy as np
import concourse.bass as bass
from concourse import mybir

F32 = mybir.dt.float32
F32R = mybir.dt.float32r
I32 = mybir.dt.int32
U8 = mybir.dt.uint8
ALU = mybir.AluOpType
ACT = mybir.ActivationFunctionType
AX = mybir.AxisListType.X
ds = bass.ds

P = 128
D = 2048
S = 256
M = S // P
KT = D // P
DEPTH = 2
HD = 128
NH = 8
DA = NH * HD
IH, ID = 16, 64
TOPK = min(256, S // 4)
NB = 32
EXACT, MAXD = 16, 128
EPS = 1e-6
SCALE = HD ** -0.5
CH = 512

QA = 0
KA = QA + DA
VA = KA + HD
GA = VA + HD
QI = GA + DA
KI = QI + IH * ID
WI = KI + ID
QB = WI + IH
KB = QB + DA
VB = KB + DA
GB = VB + DA
N_IN = GB + DA
NCH = N_IN // CH
TAIL = N_IN - NCH * CH
IN2 = 6 * D

C_ID = 0
C_MASK = C_ID + P
C_INV = C_MASK + 2 * P
C_QG = C_INV + HD // 2
C_KG = C_QG + M * NH
C_B = C_KG + M * NH
C_EPS = C_B + NB
C_HPI = C_EPS + 1
C_PW = C_HPI + 1
C_N = C_PW + 2

V1 = {"b_mod": (0, 96), "norm_gain": (96, 32)}
V2, _at = {}, 0
for _n, _k in (("c", 16), ("norm_mix_g_2", 16), ("hg_norm_g_2", 8), ("ple_norm_g_2", 16), ("conv_w_2", 24),
               ("lb_param_2", 8), ("ret_norm_gain", 16), ("q_norm_gain", 2), ("k_norm_gain", 2)):
    V2[_n] = (_at, _k)
    _at += _k
NV2 = _at
LEVELS = 7

RAW = 4
SPL = 4


def constants():
    k = np.zeros((P, C_N), np.float32)
    k[:, C_ID:C_ID + P] = np.eye(P)
    r = np.arange(P)
    k[:, C_MASK:C_MASK + P] = (r[None, :] >= r[:, None])
    k[:, C_MASK + P:C_MASK + 2 * P] = 1.0
    half = HD // 2
    k[:, C_INV:C_INV + half] = np.float32(10000.0) ** (-np.arange(half, dtype=np.float32) / np.float32(half))
    lg = np.log1p(-np.exp2(-5.0 - np.arange(NH)))
    for m in range(M):
        t = (m * P + r)[:, None]
        k[:, C_QG + m * NH:C_QG + (m + 1) * NH] = np.exp(lg[None, :] * t)
        k[:, C_KG + m * NH:C_KG + (m + 1) * NH] = np.exp(-lg[None, :] * t) * SCALE
    k[:, C_B:C_B + NB] = np.arange(NB)
    k[:, C_EPS] = EPS
    k[:, C_HPI] = math.pi / 2
    k[:, C_PW:C_PW + 2] = -0.5
    lv = np.zeros((P, 5, P), np.float32)
    for n in range(LEVELS):
        b = 64 >> n
        lv[:, max(n - 3, 0)] += ((r[:, None] // (2 * b) == r[None, :] // (2 * b)) & (r[:, None] // b % 2 == 0)
                                 & (r[None, :] // b % 2 == 1))
    lv[:, 4] = np.eye(P)
    return k, lv


class Seen:

    def __init__(self, eng, sem, start=0):
        self.eng, self.sem, self.n, self.i, self.per, self.base = eng, sem, start, None, 0, 0

    def wait(self, more=1):
        self.n += more
        self.eng.wait_ge(self.sem, self.n + self.base if self.i is None else self.i * self.per + (self.base + self.n))

    def skip(self, n):
        self.n += n

    def rest(self, n):
        self.eng.wait_ge(self.sem, self.n + n)


@contextmanager
def loop(eng, turns, per):
    with eng.Fori(0, turns) as i:
        for s, n in per.items():
            s.i, s.per, s.base, s.n = i, n, s.n, 0
        yield i
        for s, n in per.items():
            assert s.n == n, (s.sem, s.n, n)
            s.i, s.n, s.base = None, s.base + turns * n, 0


def bc(ap, n):
    return ap.unsqueeze(len(ap.shape)).broadcast_to([*ap.shape, n])


def build(nc, x, c, positions, rel_bias, norm_gain, w_mod, b_mod, w_in, q_norm_gain, k_norm_gain, ret_norm_gain,
          w_out, p_2, norm_mix_g_2, w_in_2, conv_w_2, lb_param_2, hg_norm_g_2, w_a_out_2, w_b_out_2, w_o_2,
          ple_norm_g_2, w_ple_gate_2, w_ple_proj_2, final_norm_g_2, consts, levels, out):
    ctx = ExitStack()
    with ctx:
        def sb(name, shape, dt=F32):
            return ctx.enter_context(nc.sbuf_tensor(name, shape, dt))

        def sem(name):
            return ctx.enter_context(nc.semaphore(name))

        xres = sb("xres", [P, M, D])
        ht_hi = sb("ht_hi", [P, KT, S], F32R)
        ht_lo = sb("ht_lo", [P, KT, S], F32R)
        proj = sb("proj", [P, M, 8192])
        raw = sb("raw", [P, RAW, 4, CH])
        w_hi = sb("w_hi", [P, SPL, 2, CH], F32R)
        w_lo = sb("w_lo", [P, SPL, 2, CH], F32R)
        scr = sb("scr", [P, 6144])
        kst = sb("kst", [P, C_N])
        lvm = sb("lvm", [P, 5, P], U8)
        vcol = sb("vcol", [P, P + NV2])
        modc = sb("modc", [P, DEPTH * 48])
        acol = sb("acol", [P, DEPTH * KT])
        lbc = sb("lbc", [P, 3 * NH])
        cs = proj[:, 1, N_IN + 384:N_IN + 640].rearrange("p (a m d) -> p a m d", a=2, m=M)
        xn = sb("xn", [P, 2, M, P])
        ktile = proj[:, 0, N_IN:N_IN + S]
        mb = proj[:, 1, N_IN:N_IN + 384]
        st = sb("st", [P, 64])
        tmp8 = proj[:, 0, N_IN + 256:N_IN + 272].rearrange("p (m k) -> p m k", m=M)
        bns = proj[:, 0, N_IN + 272:N_IN + 296].rearrange("p (n k) -> p n k", n=4)
        mv = proj[:, 0, N_IN + 296:N_IN + 304].rearrange("p (n k) -> p n k", n=4)

        ident = kst[:, C_ID:C_ID + P]
        maskt = kst[:, C_MASK:C_MASK + 2 * P]
        eps = kst[:, C_EPS:C_EPS + 1]
        ones = kst[:, C_MASK + P:C_MASK + P + 1]
        ones128 = kst[:, C_MASK + P:C_MASK + 2 * P]

        macc = proj[:, 0, 0:4096].rearrange("p (b e n) -> p b e n", b=2, e=4)
        onehot = proj[:, 1, 0:6144].bitcast(mybir.dt.bfloat16).rearrange("p (b k) -> p b k", b=NB)
        btmp = proj[:, 0, 4096:7168].rearrange("p (h k) -> p h k", h=NH)
        bucket = proj[:, 0, 7168:7552]
        rel = proj[:, 0, 7552:7936]
        prow_i = proj[:, 1, 6144:6400].bitcast(I32)
        prow = proj[:, 1, 6400:6656]
        rbt = proj[:, 1, 6656:6912]
        pcol_i = proj[:, 1, 6912:6914].bitcast(I32)
        pcol = proj[:, 1, 6914:6916]
        ang = proj[:, 1, 6916:7044].rearrange("p (m d) -> p m d", m=M)
        ang_n = proj[:, 1, 7044:7172].rearrange("p (m d) -> p m d", m=M)
        lb_t = proj[:, 1, 7172:7188].rearrange("p (a h) -> p a h", a=2)

        def v1(n, i=0, k=1):
            return vcol[:, V1[n][0] + i:V1[n][0] + i + k]

        def v2(n, i=0, k=1):
            return vcol[:, P + V2[n][0] + i:P + V2[n][0] + i + k]

        bias = scr[:, 0:3072].rearrange("p (h k) -> p h k", h=NH)
        lb_s = scr[:, 3072:3840].rearrange("p (b k) -> p b k", b=2)
        lg = scr[:, 3840:4608].rearrange("p (b k) -> p b k", b=2)
        pt = scr[:, 4608:5376].rearrange("p (b k) -> p b k", b=2)
        qt = scr[:, 5376:5888].rearrange("p (b k) -> p b k", b=2)
        ttmp = scr[:, 5888:6144]
        ttmp2 = scr[:, 5632:6144].rearrange("p (b t) -> p b t", b=2)
        idx = scr[:, 3840:4224]
        kit = scr[:, 4608:4864]
        rqk = scr[:, 3072:4096].rearrange("p (b w m d) -> p b w m d", b=2, w=2, m=M)
        rqt = scr[:, 4096:5120].rearrange("p (b w t) -> p b w t", b=2, w=2)
        rst = scr[:, 5120:5888].rearrange("p (b k) -> p b k", b=2)
        ro = proj[:, 0, 0:512].rearrange("p (b m d) -> p b m d", b=2, m=M)
        rtmp = proj[:, 1, 0:1024].rearrange("p (a w d) -> p a w d", a=4, w=4)
        wk = scr[:, 0:2048].rearrange("p (n t) -> p n t", t=S)
        wq = scr[:, 2048:4096].rearrange("p (n t) -> p n t", t=S)
        hq = scr[:, 4096:4352]
        hk = scr[:, 4352:4608]
        hs = scr[:, 4608:5120]
        hb = scr[:, 5120:5376]
        hat = scr[:, 5376:5632].rearrange("p (m t) -> p m t", m=M)
        hax = scr[:, 5632:5760]
        hy = scr[:, 5888:6144].rearrange("p (m d) -> p m d", m=M)
        cg2 = scr[:, 0:2048].rearrange("p (m n) -> p m n", m=M)
        ut = scr[:, 2048:2048 + 2 * 258].rearrange("p (b t) -> p b t", b=2)
        ct = scr[:, 2560 + 8:2560 + 8 + 512].rearrange("p (b t) -> p b t", b=2)

        def level_views(dst, src):
            for n in range(LEVELS):
                h = 64 >> n
                dv, sv = (a.rearrange("p (n two t) -> p n two t", two=2, t=h) for a in (dst[:, n, :], src))
                yield (n, (dv[:, :, 0, :], sv[:, :, 0, :]), (dv[:, :, 1, :], sv[:, :, 1, :]),
                       sv[:, :, 0, h - 1:h].broadcast_to([P, S // (2 * h), h]))

        acc = ctx.enter_context(nc.psum_tensor("acc", [P, 2, M, CH], F32))
        tps = ctx.enter_context(nc.psum_tensor("tps", [P, 2, CH], F32))
        sps = ctx.enter_context(nc.psum_tensor("sps", [P, 2, CH], F32))

        gates = nc.dram_tensor("gates", (DEPTH * KT, P), F32, kind="Internal").ap()

        s_const = sem("s_const")
        s_x = sem("s_x")
        s_vec = sem("s_vec")
        s_pos = sem("s_pos")
        s_rb = sem("s_rb")
        vec_turned = sem("vec_turned")
        vec_ready = sem("vec_ready")
        c_ready = sem("c_ready")
        raw_landed = [sem(f"raw_landed{j}") for j in range(RAW)]
        hi_ready = sem("hi_ready")
        raw_read = sem("raw_read")
        split_used = sem("split_used")
        acc_taken = sem("acc_taken")
        dve_link = sem("dve_link")
        dve_passed = sem("dve_passed")
        act_link = sem("act_link")
        pool_link = sem("pool_link")
        mod_summed = sem("mod_summed")
        mod_taken = sem("mod_taken")
        mod_ready = sem("mod_ready")
        gate_turned = sem("gate_turned")
        gate_rows = sem("gate_rows")
        gate_out = sem("gate_out")
        gate_bc = sem("gate_bc")
        onehot_ready = sem("onehot_ready")
        onehot_used = sem("onehot_used")
        rot_ready = sem("rot_ready")
        sums_ready = sem("sums_ready")
        root_ready = sem("root_ready")
        rstd_ready = sem("rstd_ready")
        turn_in = sem("turn_in")
        turned = sem("turned")
        turn_hi = sem("turn_hi")
        turn_lo = sem("turn_lo")
        proj_ready = sem("proj_ready")
        x_ready = sem("x_ready")
        k_ready = sem("k_ready")
        k_turned = sem("k_turned")
        kt_ready = sem("kt_ready")
        qi_ready = sem("qi_ready")
        qi_turned = sem("qi_turned")
        qit_ready = sem("qit_ready")
        dots_ready = sem("dots_ready")
        relu_ready = sem("relu_ready")
        dots_used = sem("dots_used")
        idx_ready = sem("idx_ready")
        idx_causal = sem("idx_causal")
        sel_ready = sem("sel_ready")
        mb_ready = sem("mb_ready")
        qn_ready = sem("qn_ready")
        qn_turned = sem("qn_turned")
        qt_ready = sem("qt_ready")
        lb_ready = sem("lb_ready")
        scores_ready = sem("scores_ready")
        logits_ready = sem("logits_ready")
        max_ready = sem("max_ready")
        probs_ready = sem("probs_ready")
        probs_turned = sem("probs_turned")
        pt_ready = sem("pt_ready")
        heads_out = sem("heads_out")
        y_ready = sem("y_ready")
        ga_ready = sem("ga_ready")
        rot_done = sem("rot_done")
        rqk_turned = sem("rqk_turned")
        rqt_ready = sem("rqt_ready")
        rs_ready = sem("rs_ready")
        rst_ready = sem("rst_ready")
        ret_out = sem("ret_out")
        ret_taken = sem("ret_taken")
        ret_var = sem("ret_var")
        ret_root = sem("ret_root")
        yb_ready = sem("yb_ready")
        act_acc = sem("act_acc")
        lb_stats = sem("lb_stats")
        lb_exp = sem("lb_exp")
        lbc_ready = sem("lbc_ready")
        hg_in = sem("hg_in")
        hg_turned = sem("hg_turned")
        hg_sig = sem("hg_sig")
        hg_f = sem("hg_f")
        hg_ln = sem("hg_ln")
        hg_w = sem("hg_w")
        hg_b = sem("hg_b")
        hg_d1 = sem("hg_d1")
        hg_d2 = sem("hg_d2")
        hg_x1 = sem("hg_x1")
        hg_x2 = sem("hg_x2")
        hg_rstd = sem("hg_rstd")
        hg_a = sem("hg_a")
        hg_at = sem("hg_at")
        hg_axr = sem("hg_axr")
        hg_o = sem("hg_o")
        hg_ss = sem("hg_ss")
        hg_y = sem("hg_y")
        cv_in = sem("cv_in")
        cv_turned = sem("cv_turned")
        cv_u = sem("cv_u")
        cv_c = sem("cv_c")
        cv_y = sem("cv_y")
        cv_hi = sem("cv_hi")
        cv_lo = sem("cv_lo")
        p_landed = sem("p_landed")
        fin_g = sem("fin_g")
        fin_ready = sem("fin_ready")
        s_out = sem("s_out")

        x_rows = x[0].rearrange("(m p) d -> p m d", p=P)
        out_rows = out[0].rearrange("(m p) d -> p m d", p=P)

        def ktiles(w):
            return w.rearrange("(k p) n -> p k n", p=P)

        wm = [ktiles(w_mod[l]) for l in range(DEPTH)]
        wi = [ktiles(w_in[l]) for l in range(DEPTH)]
        wo = [ktiles(w_out[l]) for l in range(DEPTH)]
        wi2 = ktiles(w_in_2[0])
        wa2, wb2, wo2 = ktiles(w_a_out_2[0]), ktiles(w_b_out_2[0]), ktiles(w_o_2[0])
        wg2, wp2 = ktiles(w_ple_gate_2[0]), ktiles(w_ple_proj_2[0])

        def full(w):
            return lambda j, col, n: w[:, 4 * j:4 * j + 4, ds(col, n)]

        def two(j, col, n):
            return (wa2 if j < 2 else wb2)[:, 4 * (j % 2):4 * (j % 2) + 4, ds(col, n)]

        REC, GATES, CONV = 4096, 8192, 0
        W2_PARTS = [(REC, 8), (GATES, 8), (CONV, 2), (CONV + 1024, 6)]

        block = ctx.enter_context(nc.Block())

        @block.sync
        def _(sp):
            free = Seen(sp, raw_read)

            sp.dma_start(vcol[0:96, 0:P], b_mod.rearrange("l (k p) -> (l k) p", p=P)).then_inc(s_vec, 16)
            sp.dma_start(vcol[96:128, 0:P], norm_gain.rearrange("l (k p) -> (l k) p", p=P)).then_inc(s_vec, 16)
            for name, ap in (("c", c), ("norm_mix_g_2", norm_mix_g_2), ("hg_norm_g_2", hg_norm_g_2),
                             ("ple_norm_g_2", ple_norm_g_2), ("lb_param_2", lb_param_2),
                             ("ret_norm_gain", ret_norm_gain), ("q_norm_gain", q_norm_gain),
                             ("k_norm_gain", k_norm_gain)):
                o, k = V2[name]
                sp.dma_start(xn[o:o + k, 0, 0, :], ap.rearrange("l (k p) -> (l k) p", p=P)).then_inc(s_vec, 16)
            o, k = V2["conv_w_2"]
            sp.dma_start(xn[o:o + k, 0, 0, :], conv_w_2[0].rearrange("t (k p) -> (t k) p", p=P)).then_inc(s_vec, 16)
            sp.dma_start(kst[:, :], consts).then_inc(s_const, 16)
            sp.dma_start(scr[:, 3072:3712], levels.rearrange("p n t -> p (n t)")).then_inc(s_const, 16)

            def pieces(src, col, n, width=CH, kts=4):
                for j in range(RAW):
                    free.wait(2)
                    sp.dma_start(raw[:, j, 0:kts, 0:width], src(j, col, width)).then_inc(raw_landed[j], 16)

            for l in range(DEPTH):
                with loop(sp, 12, {free: 8}) as i:
                    pieces(full(wm[l]), i * CH, CH)
                if l == 0:
                    sp.dma_start(xres[:, :, :], x_rows).then_inc(s_x, 16)
            sp.wait_ge(gate_rows, 1)
            sp.dma_start(gates.rearrange("(l k) p -> k l p", l=DEPTH),
                         ttmp[0:KT, 0:DEPTH * P].rearrange("k (l p) -> k l p", l=DEPTH)).then_inc(gate_out, 16)
            sp.wait_ge(gate_out, 16)
            for l in range(DEPTH):
                with loop(sp, NCH, {free: 8}) as i:
                    pieces(full(wi[l]), i * CH, CH)
                pieces(full(wi[l]), NCH * CH, CH, width=TAIL)
                with loop(sp, 4, {free: 8}) as i:
                    pieces(full(wo[l]), i * CH, CH)
            for col, n in W2_PARTS:
                with loop(sp, n, {free: 8}) as i:
                    pieces(full(wi2), col + i * CH, CH)
            with loop(sp, 4, {free: 8}) as i:
                pieces(two, i * CH, CH)
            with loop(sp, 4, {free: 8}) as i:
                pieces(full(wo2), i * CH, CH)
            with loop(sp, 4, {free: 8}) as i:
                pieces(full(wg2), i * CH, CH)
            for j in range(RAW):
                free.wait(2)
                sp.dma_start(raw[:, j, 0:2, :], wp2[:, :, j * CH:(j + 1) * CH]).then_inc(raw_landed[j], 16)
            sp.wait_ge(fin_ready, 2)
            sp.dma_start(out_rows, proj[:, :, 0:D]).then_inc(s_out, 16)
            sp.wait_ge(s_out, 16)

        @block.tensor
        def _(pe):
            pe.sem_inc(split_used, SPL)
            pe.sem_inc(turned, 2)
            pe.sem_inc(mod_summed, 2)
            pe.sem_inc(qi_turned, 2)
            pe.sem_inc(qn_turned, 2)
            pe.sem_inc(rqk_turned, 2)
            pe.sem_inc(hg_turned, 1)
            pe.sem_inc(cv_turned, 2)
            lo = Seen(pe, raw_read, 8 + 8 * 12 * DEPTH)
            taken = Seen(pe, acc_taken)
            t_in, t_lo = Seen(pe, turn_in), Seen(pe, turn_lo)

            def gemm(turns, halves, group, width=CH, side=None, side_per=None):
                def body(t, first):
                    for x, (slot, kts) in enumerate(halves):
                        buf = x // group % 2
                        if x % group == 0:
                            taken.wait()
                        lo.wait()
                        for u, kt in enumerate(kts):
                            for m in range(M):
                                hi_m, lo_m = (a[:, kt, m * P:(m + 1) * P] for a in (ht_hi, ht_lo))
                                start, stop = x % group == 0 and u == 0, x % group == group - 1 and u == len(kts) - 1
                                o = acc[:, buf, m, 0:width]
                                pe.matmul(o, hi_m, w_hi[:, slot, u, 0:width], start=start, stop=False)
                                pe.matmul(o, hi_m, w_lo[:, slot, u, 0:width], start=False, stop=False)
                                mm = pe.matmul(o, lo_m, w_hi[:, slot, u, 0:width], start=False, stop=stop)
                        mm.then_inc(split_used, 1)
                        if side:
                            side(t, x, first)
                taken.rest(2)
                per = {taken: len(halves) // group, lo: len(halves)}
                if side:
                    body(0, True)
                    with loop(pe, turns - 1, {**per, **side_per}) as i:
                        body(i + 1, False)
                elif turns == 1:
                    body(0, True)
                else:
                    with loop(pe, turns, per) as i:
                        body(i, False)

            def chunk_halves(n):
                return [(h % SPL, (2 * h, 2 * h + 1)) for h in range(8)] * n

            def turn(n):
                with loop(pe, n, {t_in: 2, t_lo: 2}):
                    for b in range(2):
                        t_in.wait()
                        t_lo.wait()
                        for m in range(M):
                            tr = pe.transpose(tps[:, b, m * P:(m + 1) * P], xn[:, b, m, :], ident)
                        tr.then_inc(turned, 1)

            pe.wait_ge(s_vec, 16 * 11)
            pe.wait_ge(s_const, 32)
            pe.transpose(tps[:, 0, 0:P], vcol[:, 0:P], ident)
            pe.transpose(tps[:, 0, P:P + NV2], xn[0:NV2, 0, 0, :], ident[0:NV2, 0:NV2]).then_inc(vec_turned, 1)

            m_sum, m_taken = Seen(pe, raw_read, 8), Seen(pe, mod_taken)
            for l in range(DEPTH):
                with loop(pe, 6, {m_sum: 16, m_taken: 2}):
                    for b in range(2):
                        m_sum.wait(8)
                        m_taken.wait()
                        for j in range(4):
                            for e in range(4):
                                mm = pe.matmul(tps[:, b, j:j + 1], macc[:, b, e, j * P:(j + 1) * P], ones,
                                               start=e == 0, stop=e == 3)
                        mm.then_inc(mod_summed, 1)
            pe.wait_ge(mod_ready, 1)
            for l in range(DEPTH):
                tr = pe.transpose(tps[0:KT, 0, l * P:(l + 1) * P], modc[:, l * 48 + 32:l * 48 + 48], ident)
            tr.then_inc(gate_turned, 1)
            pe.wait_ge(gate_rows, 1)

            ktt, dots = Seen(pe, kt_ready), Seen(pe, dots_used, 0)
            qin, qit = Seen(pe, qi_ready), Seen(pe, qit_ready)
            qn, qtr, prb, ptr, yr = (Seen(pe, s) for s in (qn_ready, qt_ready, probs_ready, pt_ready, y_ready))
            rq, rs, rt = (Seen(pe, s) for s in (rqt_ready, rst_ready, ret_taken))
            rd = Seen(pe, rot_done, 2)
            kr = Seen(pe, k_ready)

            def sparse_keys():
                taken.rest(2)
                kr.wait(2)
                for m in range(M):
                    pe.transpose(tps[:, 0, m * P:(m + 1) * P], xn[:, 0, m, :], ident)
                    tr = pe.transpose(tps[:, 0, S + m * P:S + (m + 1) * P], xn[:, 1, m, :], ident)
                tr.then_inc(k_turned, 1)

            def index_scores():
                ktt.wait()
                with loop(pe, 4, {qin: 2, qit: 1, dots: 4}):
                    for b in range(2):
                        qin.wait()
                        for m in range(M):
                            tr = pe.transpose(tps[:, 0, b * S + m * P:b * S + (m + 1) * P], xn[:, b, m, :], ident)
                        tr.then_inc(qi_turned, 1)
                    qit.wait()
                    for b in range(2):
                        for e in range(2):
                            dots.wait()
                            r = slice(64 * e, 64 * e + 64)
                            pe.matmul(sps[:, e, 0:P], qt[r, b, 0:P], kit[r, 0:P], start=True, stop=True)
                            pe.matmul(sps[:, e, P:P + S], qt[r, b, P:S], kit[r, :], start=True,
                                      stop=True).then_inc(dots_ready, 1)

            def sparse_heads():
                with loop(pe, 4, {qn: 2, qtr: 2, prb: 2, ptr: 2, yr: 2}):
                    for b in range(2):
                        qn.wait()
                        for m in range(M):
                            tr = pe.transpose(tps[:, b, m * P:(m + 1) * P], xn[:, b, m, :], ident)
                        tr.then_inc(qn_turned, 1)
                    for b in range(2):
                        qtr.wait()
                        yr.wait()
                        pe.matmul(sps[:, b, 0:P], qt[:, b, 0:P], ktile[:, 0:P], start=True, stop=True)
                        pe.matmul(sps[:, b, P:P + S], qt[:, b, P:S], ktile, start=True,
                                  stop=True).then_inc(scores_ready, 1)
                    for b in range(2):
                        prb.wait()
                        for n in range(3):
                            tr = pe.transpose(tps[:, b, n * P:(n + 1) * P], lg[:, b, n * P:(n + 1) * P], ident)
                        tr.then_inc(probs_turned, 1)
                    for b in range(2):
                        ptr.wait()
                        v = [proj[:, m, VA:VA + HD] for m in range(M)]
                        pe.matmul(sps[:, b, 0:P], pt[:, b, 0:P], v[0], start=True, stop=True)
                        pe.matmul(sps[:, b, P:S], pt[:, b, P:S], v[0], start=True, stop=False)
                        pe.matmul(sps[:, b, P:S], pt[:, b, S:S + P], v[1], start=False,
                                  stop=True).then_inc(heads_out, 1)

            def retention():
                with loop(pe, 4, {rd: 2, rq: 2, rs: 2, rt: 2}) as i:
                    for b in range(2):
                        rd.wait()
                        for w in range(2):
                            for m in range(M):
                                tr = pe.transpose(tps[:, b, w * S + m * P:w * S + (m + 1) * P], rqk[:, b, w, m, :], ident)
                        tr.then_inc(rqk_turned, 1)
                    for b in range(2):
                        rq.wait()
                        rt.wait()
                        pe.matmul(sps[:, b, 0:S], rqt[:, b, 1, 0:P], rqt[:, b, 0, :], start=True, stop=True)
                        pe.matmul(sps[:, b, S:S + P], rqt[:, b, 1, P:S], rqt[:, b, 0, P:S], start=True,
                                  stop=True).then_inc(rs_ready, 1)
                    for b in range(2):
                        rs.wait()
                        v = [proj[:, m, ds(VB + (2 * i + b) * HD, HD)] for m in range(M)]
                        pe.matmul(sps[:, b, 0:P], rst[:, b, 0:P], v[0], start=True, stop=True)
                        pe.matmul(sps[:, b, P:S], rst[:, b, P:S], v[0], start=True, stop=False)
                        pe.matmul(sps[:, b, P:S], rst[:, b, S:S + P], v[1], start=False,
                                  stop=True).then_inc(ret_out, 1)

            for l in range(DEPTH):
                turn(KT // 2)
                t_lo.rest(2)
                gemm(NCH // 2, chunk_halves(2), 8)
                gemm(1, chunk_halves(1), 8, width=TAIL)
                sparse_keys()
                index_scores()
                sparse_heads()
                retention()
                rt.rest(2)
                turn(KT // 2)
                t_lo.rest(2)
                gemm(2, chunk_halves(2), 8)

            hin, hx1, hx2, hat_r, haxr, hyr = (Seen(pe, s) for s in (hg_in, hg_x1, hg_x2, hg_at, hg_axr, hg_y))

            def hgrn_scores():
                hx1.wait()
                hx2.wait()
                hyr.wait()
                for m in range(M):
                    c0 = m * P

                    def score(lv, s0, t0, h, o):
                        return pe.matmul(o, wk[:, lv, c0 + s0:c0 + s0 + h], wk[:, lv, c0 + t0:c0 + t0 + h],
                                         start=True, stop=True)
                    region = [sps[:, r // 2, (r % 2 * 2 + m) * P:(r % 2 * 2 + m + 1) * P] for r in range(4)]
                    for r in range(4):
                        score(3 + r, 0, 0, P, region[r])
                    for lv in range(3):
                        h = 64 >> lv
                        for s0 in range(0, P, 2 * h):
                            score(lv, s0, s0 + h, h, region[0][s0:s0 + h, s0 + h:s0 + 2 * h])
                    pe.matmul(tps[:, 1, c0:c0 + P], hk[:, c0:c0 + P], hq[:, c0:c0 + P], start=True, stop=True)
                pe.matmul(tps[:, 0, 0:P], wk[:, LEVELS, 0:P], wk[:, LEVELS, P:S], start=True,
                          stop=True).then_inc(hg_a, 1)

            def hgrn_out(g):
                hat_r.wait()
                v = [proj[:, m, ds(2048 + g * HD, HD)] for m in range(M)]
                pe.matmul(tps[:, 1, S:S + P], hat[:, 0, :], v[0], start=True, stop=True)
                pe.matmul(tps[:, 1, S + P:2 * S], hat[:, 1, :], v[1], start=True, stop=False)
                pe.matmul(tps[:, 1, S + P:2 * S], hax, v[0], start=False, stop=True).then_inc(hg_o, 1)

            def hgrn(t, x, first):
                g, n = 2 * t + x // 8, x % 8
                begin = first and x < 8
                if n == 0 and not begin:
                    hgrn_scores()
                if n == 1:
                    if not begin:
                        haxr.wait()
                    hin.wait()
                    for b in range(2):
                        for m in range(M):
                            tr = pe.transpose(tps[:, 0, b * S + m * P:b * S + (m + 1) * P], xn[:, b, m, :], ident)
                    tr.then_inc(hg_turned, 1)
                if n == 4 and not begin:
                    hgrn_out(g - 1)
            cin, cy = Seen(pe, cv_in), Seen(pe, cv_y)

            def conv():
                with loop(pe, 4, {cin: 2, cy: 2}):
                    for b in range(2):
                        cin.wait()
                        cy.wait()
                        for m in range(M):
                            pe.transpose(tps[:, b, m * P:(m + 1) * P], xn[:, b, m, :], ident)
                            tr = pe.transpose(tps[:, b, S + m * P:S + (m + 1) * P], lgc[:, b, m, :], ident)
                        tr.then_inc(cv_turned, 1)

            lgc = scr[:, 3584:4096].rearrange("p (b m d) -> p b m d", b=2, m=M)

            turn(KT // 2)
            t_lo.rest(2)
            for col, n in W2_PARTS:
                if col == GATES:
                    gemm(n // 2, chunk_halves(2), 8, side=hgrn,
                         side_per={s: 2 for s in (hin, hx1, hx2, hat_r, haxr, hyr)})
                    hgrn_scores()
                    haxr.wait()
                    hgrn_out(NH - 1)
                else:
                    gemm(n // 2, chunk_halves(2), 8)
            conv()
            cy.rest(2)
            turn(NH // 2)
            t_lo.rest(2)
            pe.wait_ge(cv_lo, 2 + 8)
            gemm(4, chunk_halves(1), 4)
            turn(KT // 2)
            t_lo.rest(2)
            gemm(2, chunk_halves(2), 8)
            turn(KT // 2)
            t_lo.rest(2)
            gemm(2, chunk_halves(2), 8)
            turn(1)
            t_lo.rest(2)
            gemm(1, [(j, (0, 1)) for j in range(4)], 1)


        @block.scalar
        def _(act):
            act.sem_inc(acc_taken, 2)
            act.sem_inc(mod_taken, 2)
            act.sem_inc(ret_taken, 2)
            act.dma_start(prow_i, positions.partition_broadcast(P)).then_inc(s_pos, 16)
            for m in range(M):
                act.dma_start(pcol_i[:, m:m + 1], positions[0].rearrange("(m p o) -> m p o", p=P, o=1)[m])\
                   .then_inc(s_pos, 16)
            act.dma_start(rbt, rel_bias.rearrange("b h -> (b h)").partition_broadcast(P)).then_inc(s_rb, 16)

            landed = [Seen(act, s, 16 * 12 * DEPTH) for s in raw_landed]
            slot_free = Seen(act, split_used)
            results = Seen(act, split_used, SPL)
            t_out = Seen(act, turned, 2)

            def link(ins):
                ins.then_inc(act_link, 1)
                linked.wait()

            linked = Seen(act, act_link)

            def split(turns, nh, group, width=CH, halves=2, evac=None, side=None, side_per=None):
                gb = nh // group

                def take(g, b):
                    results.wait(group)
                    evac(g, b)

                def body(t, first):
                    for x in range(nh):
                        j = x // halves % RAW
                        if x % halves == 0:
                            landed[j].wait(16)
                        slot_free.wait()
                        act.activation(w_hi[:, x % SPL, :, 0:width],
                                       raw[:, j, 2 * (x % halves):2 * (x % halves) + 2, 0:width],
                                       ACT.Copy).then_inc(hi_ready, 1)
                        if evac and x % group == min(3, group - 1) and not (first and x < group):
                            g = x // group - 1
                            take(t * gb + g, g % 2)
                        if side:
                            side(t, x, first)

                body(0, True)
                if turns > 1:
                    per = {slot_free: nh, results: nh if evac else 0, **(side_per or {})}
                    per.update({s: 16 * nh // (RAW * halves) for s in landed})
                    with loop(act, turns - 1, per) as i:
                        body(i + 1, False)
                if evac:
                    take(turns * gb - 1, (turns * gb - 1) % 2)
                else:
                    results.skip(turns * nh)

            def turn(n, kt0=0, scale=None, bias=None):
                with loop(act, n, {t_out: 2}) as i:
                    for b in range(2):
                        t_out.wait()
                        o = ht_hi[:, ds(kt0 + 2 * i + b, 1), :].rearrange("p a t -> p (a t)")
                        kw = {}
                        if scale is not None:
                            kw["scale"] = scale[:, ds(2 * i + b, 1)]
                        if bias is not None:
                            kw["bias"] = bias[:, ds(2 * i + b, 1)]
                        act.activation(o, tps[:, b, 0:S], ACT.Copy if bias is None else ACT.Identity,
                                       **kw).then_inc(turn_hi, 1)

            xr = Seen(act, x_ready, 2)

            def row_sums(n_x):
                for m in range(M):
                    act.activation(proj[:, m, 0:D], xres[:, m, :], ACT.Square, accum_out=st[:, m:m + 1])\
                       .then_inc(act_link, 1)
                linked.wait(2)
                act.activation(st[:, 2:4], st[:, 0:2], ACT.Sqrt, bias=eps, scale=1.0 / D).then_inc(root_ready, 1)

            act.wait_ge(vec_turned, 1)
            link(act.activation(vcol[:, :], tps[:, 0, 0:P + NV2], ACT.Copy))
            act.activation(v2("c", 0, KT), v2("c", 0, KT), ACT.Silu).then_inc(vec_ready, 1)
            act.wait_ge(rot_ready, 1)
            act.activation(cs[:, 1, :, :], ang, ACT.Sin).then_inc(rot_done, 1)
            act.activation(cs[:, 0, :, :], ang_n, ACT.Sin, bias=kst[:, C_HPI:C_HPI + 1]).then_inc(rot_done, 1)
            act.wait_ge(lb_stats, 1)
            act.activation(lb_t[:, 1, :], lb_t[:, 0, :], ACT.Exp).then_inc(lb_exp, 1)

            m_sum = Seen(act, mod_summed, 2)
            for l in range(DEPTH):
                with loop(act, 6, {m_sum: 2}) as i:
                    for b in range(2):
                        m_sum.wait()
                        act.activation(modc[:, ds(l * 48 + 8 * i + 4 * b, 4)], tps[:, b, 0:4], ACT.Copy)\
                           .then_inc(mod_taken, 1)
            act.wait_ge(gate_turned, 1)
            act.activation(ttmp[0:KT, :], tps[0:KT, 0, 0:DEPTH * P], ACT.Copy).then_inc(gate_rows, 1)

            rr, ktn, qtn, dr = (Seen(act, s) for s in (sums_ready, k_turned, qi_turned, dots_ready))
            qtn.skip(2)
            qnt, mx, pbt = Seen(act, qn_turned, 2), Seen(act, max_ready), Seen(act, probs_turned)
            rqt_t, rout, rvar = Seen(act, rqk_turned, 2), Seen(act, ret_out), Seen(act, ret_var)

            def to_proj(width=CH, col0=0, func=ACT.Copy, base=0):
                def evac(g, b):
                    act.activation(proj[:, :, ds(base + g * CH, width)], acc[:, b, :, 0:width], func)\
                       .then_inc(acc_taken, 1)
                return evac

            for l in range(DEPTH):
                if l == 0:
                    act.wait_ge(s_x, 16)
                    act.wait_ge(mod_ready, 1)
                    act.wait_ge(gate_out, 16)
                else:
                    xr.wait(4)
                row_sums(l)
                turn(KT // 2, scale=acol[:, l * KT:(l + 1) * KT], bias=modc[:, l * 48:l * 48 + KT])
                split(NCH // 2, 16, 8, evac=to_proj())
                split(1, 8, 8, width=TAIL, evac=to_proj(TAIL, base=NCH * CH))
                linked.skip(0)
                act.wait_ge(acc_taken, 2 + (NCH + 1 + 4) * l + NCH + 1)
                act.activation(proj[:, :, GA:GA + DA], proj[:, :, GA:GA + DA], ACT.Silu).then_inc(ga_ready, 1)
                act.activation(proj[:, :, GB:GB + DA], proj[:, :, GB:GB + DA], ACT.Silu).then_inc(ga_ready, 1)
                rr.wait()
                act.activation(st[:, 24:42], st[:, 4:22], ACT.Sqrt, bias=eps, scale=1.0 / HD).then_inc(root_ready, 1)
                ktn.wait()
                act.activation(kit, tps[:, 0, 0:S], ACT.Copy)
                act.activation(ktile, tps[:, 0, S:2 * S], ACT.Copy, scale=v2("k_norm_gain", l)).then_inc(kt_ready, 1)
                with loop(act, 4, {qtn: 2, dr: 4}):
                    qtn.wait(2)
                    act.activation(qt, tps[:, 0, :].rearrange("p (b t) -> p b t", b=2), ACT.Copy).then_inc(qit_ready, 1)
                    for b in range(2):
                        for e in range(2):
                            dr.wait()
                            act.activation(sps[:, e, 0:384], sps[:, e, 0:384], ACT.Relu).then_inc(relu_ready, 1)
                with loop(act, 4, {qnt: 2, mx: 2, pbt: 2}):
                    for b in range(2):
                        qnt.wait()
                        act.activation(qt[:, b, :], tps[:, b, 0:S], ACT.Copy, scale=v2("q_norm_gain", l))\
                           .then_inc(qt_ready, 1)
                    for b in range(2):
                        mx.wait()
                        act.activation(lg[:, b, 0:P], lg[:, b, 0:P], ACT.Exp, bias=st[:, 44 + 2 * b:45 + 2 * b],
                                       accum_out=st[:, 48 + 2 * b:49 + 2 * b])
                        act.activation(lg[:, b, P:384], lg[:, b, P:384], ACT.Exp, bias=st[:, 45 + 2 * b:46 + 2 * b],
                                       accum_out=st[:, 49 + 2 * b:50 + 2 * b]).then_inc(probs_ready, 1)
                    for b in range(2):
                        pbt.wait()
                        act.activation(pt[:, b, :], tps[:, b, 0:384], ACT.Copy).then_inc(pt_ready, 1)
                with loop(act, 4, {rqt_t: 2, rout: 2, rvar: 1}) as i:
                    for b in range(2):
                        rqt_t.wait()
                        act.activation(rqt[:, b, :, :], tps[:, b, :].rearrange("p (w t) -> p w t", w=2), ACT.Copy)\
                           .then_inc(rqt_ready, 1)
                    for b in range(2):
                        rout.wait()
                        for m in range(M):
                            r = act.activation(ro[:, b, m, :], sps[:, b, m * P:(m + 1) * P], ACT.Copy,
                                               scale=kst[:, ds(C_QG + m * NH + 2 * i + b, 1)])
                        r.then_inc(ret_taken, 1)
                    rvar.wait()
                    act.activation(st[:, 0:4], mv[:, :, 1], ACT.Sqrt, bias=eps).then_inc(ret_root, 1)
                turn(NH // 2)
                turn(NH // 2, kt0=NH, scale=v2("ret_norm_gain", l * NH, NH))
                act.dma_start(proj[:, 0, 0:D], gates[l * KT:(l + 1) * KT, :].rearrange("k p -> (k p)")
                              .partition_broadcast(P)).then_inc(gate_bc, 16)
                split(2, 16, 8)

            xr.wait(4)
            row_sums(2)
            turn(KT // 2, scale=v2("norm_mix_g_2", 0, KT))
            hgt, hgf, hgd1, hgd2, hga, hgo = (Seen(act, s) for s in (hg_turned, hg_f, hg_d1, hg_d2, hg_a, hg_o))
            hgt.skip(1)

            def hgrn_cross():
                hga.wait()
                act.activation(hax, tps[:, 0, 0:P], ACT.Copy).then_inc(hg_axr, 1)

            def hgrn_squares():
                hgo.wait()
                for m in range(M):
                    act.activation(hy[:, m, :], tps[:, 1, S + m * P:S + (m + 1) * P], ACT.Square,
                                   scale=HD ** -0.5, accum_out=st[:, m:m + 1]).then_inc(hg_ss, 1)

            def hgrn(t, x, first):
                n = x % 8
                begin = first and x < 8
                if n == 2 and not begin:
                    hgrn_cross()
                if n == 3:
                    hgt.wait()
                    act.activation(hs[:, 0:S], tps[:, 0, S:2 * S], ACT.Sigmoid)
                    act.activation(hk, tps[:, 0, S:2 * S], ACT.Sigmoid, scale=-1.0)
                    act.activation(hq, tps[:, 0, 0:S], ACT.Copy).then_inc(hg_sig, 1)
                if n == 4:
                    hgf.wait()
                    act.activation(hs, hs, ACT.Ln).then_inc(hg_ln, 1)
                if n == 5:
                    hgd1.wait()
                    hgd2.wait()
                    act.activation(wk, wk, ACT.Exp).then_inc(hg_w, 1)
                if n == 6 and not begin:
                    hgrn_squares()
            ngroups = 2 + DEPTH * (NCH + 1 + 4)
            for col, n in W2_PARTS:
                if col == CONV:
                    def evac(g, b):
                        act.activation(cg2[:, :, ds(g * CH, CH)], acc[:, b, :, :], ACT.Copy).then_inc(acc_taken, 1)
                else:
                    evac = to_proj(func=ACT.Sigmoid if col == GATES else ACT.Copy, base=4096 if col == GATES else 0)
                if col == GATES:
                    split(n // 2, 16, 8, evac=evac, side=hgrn, side_per={s: 2 for s in (hgt, hgf, hgd1, hgd2, hga, hgo)})
                    hgrn_cross()
                    hgrn_squares()
                else:
                    split(n // 2, 16, 8, evac=evac)
                ngroups += n
                if col == REC:
                    act.wait_ge(acc_taken, ngroups)
                    act.activation(proj[:, :, 0:1024], proj[:, :, 0:1024], ACT.Silu).then_inc(ga_ready, 1)
                    act.activation(proj[:, :, 3072:4096], proj[:, :, 3072:4096], ACT.Silu).then_inc(ga_ready, 1)
            act.wait_ge(acc_taken, ngroups)
            act.activation(proj[:, :, 2048:3072], proj[:, :, 2048:3072], ACT.Silu).then_inc(ga_ready, 1)
            cvt, cvc = Seen(act, cv_turned, 2), Seen(act, cv_y, 2)
            act.wait_ge(cv_hi, 1)
            with loop(act, 4, {cvt: 2, cvc: 2}) as i:
                for b in range(2):
                    cvt.wait()
                    act.activation(ut[:, b, 2:258], tps[:, b, 0:S], ACT.Copy).then_inc(cv_u, 1)
                for b in range(2):
                    cvc.wait()
                    act.activation(ht_hi[:, ds(2 * i + b, 1), :].rearrange("p a t -> p (a t)"), ct[:, b, :],
                                   ACT.Copy).then_inc(cv_hi, 1)
            turn(NH // 2, kt0=NH, scale=v2("hg_norm_g_2", 0, NH))
            split(4, 8, 4)
            turn(KT // 2)
            act.dma_start(proj[:, :, 6144:6400], p_2[0, 0].rearrange("(m p) d -> p m d", p=P)).then_inc(p_landed, 16)
            act.dma_start(proj[:, 0, 4096:6144], final_norm_g_2.partition_broadcast(P)).then_inc(fin_g, 16)
            split(2, 16, 8)
            act.wait_ge(acc_taken, ngroups + 8 + 4)
            row_sums(3)
            turn(KT // 2, scale=v2("ple_norm_g_2", 0, KT))
            split(2, 16, 8, evac=to_proj(func=ACT.Sigmoid))
            turn(1)
            split(1, 4, 1, halves=1, evac=to_proj(base=2048))
            act.wait_ge(x_ready, 2 + 8 + 1)
            for m in range(M):
                act.activation(proj[:, m, 0:D], xres[:, m, :], ACT.Square, accum_out=st[:, m:m + 1]).then_inc(act_link, 1)
            linked.wait(2)
            act.activation(st[:, 2:4], st[:, 0:2], ACT.Sqrt, bias=eps, scale=1.0 / D).then_inc(root_ready, 1)

        @block.vector
        def _(dve):
            dve.sem_inc(raw_read, 8)
            dve.sem_inc(turn_lo, 2)
            dve.sem_inc(dots_used, 2)
            dve.sem_inc(y_ready, 2)
            dve.sem_inc(logits_ready, 2)
            dve.sem_inc(yb_ready, 2)
            dve.sem_inc(hg_y, 1)
            dve.sem_inc(cv_y, 2)
            dve.sem_inc(cv_lo, 2)
            linked = Seen(dve, dve_link)

            def link(ins):
                ins.then_inc(dve_link, 1)
                linked.wait()

            hi = Seen(dve, hi_ready)
            results = Seen(dve, split_used, SPL)
            t_hi, t_lo = Seen(dve, turn_hi), Seen(dve, turn_lo)

            def split(turns, nh, group, width=CH, halves=2, evac=None, side=None, side_per=None):
                gb = nh // group

                def take(g, b):
                    results.wait(group)
                    evac(g, b)

                def body(t, first):
                    for x in range(nh):
                        j = x // halves % RAW
                        hi.wait()
                        inc = 2 // halves
                        dve.tensor_tensor(w_lo[:, x % SPL, :, 0:width],
                                          raw[:, j, 2 * (x % halves):2 * (x % halves) + 2, 0:width],
                                          w_hi[:, x % SPL, :, 0:width].bitcast(F32), ALU.subtract).then_inc(raw_read, 1)
                        if evac and x % group == min(3, group - 1) and not (first and x < group):
                            g = x // group - 1
                            take(t * gb + g, g % 2)
                        if side:
                            side(t, x, first)

                body(0, True)
                if turns > 1:
                    per = {hi: nh, results: nh if evac else 0, **(side_per or {})}
                    if evac in owners:
                        per.update(owners[evac])
                    with loop(dve, turns - 1, per) as i:
                        body(i + 1, False)
                if evac:
                    take(turns * gb - 1, (turns * gb - 1) % 2)
                else:
                    results.skip(turns * nh)

            owners = {}

            def turn(n, kt0=0, scale=None, bias=None):
                per = {t_hi: 2}
                if bias is not None:
                    per.update({linked: 2, t_lo: 2})
                else:
                    t_lo.skip(2 * n)
                with loop(dve, n, per) as i:
                    for b in range(2):
                        t_hi.wait()
                        at = ds(kt0 + 2 * i + b, 1)
                        h = ht_hi[:, at, :].rearrange("p a t -> p (a t)").bitcast(F32)
                        o = ht_lo[:, at, :].rearrange("p a t -> p (a t)")
                        if bias is not None:
                            t_lo.wait()
                            link(dve.tensor_scalar(ttmp2[:, b, :], tps[:, b, 0:S], scale[:, ds(2 * i + b, 1)],
                                                   bias[:, ds(2 * i + b, 1)], ALU.mult, ALU.add))
                            r = dve.tensor_tensor(o, ttmp2[:, b, :], h, ALU.subtract)
                        elif scale is not None:
                            r = dve.scalar_tensor_tensor(o, tps[:, b, 0:S], scale[:, ds(2 * i + b, 1)], h,
                                                         ALU.mult, ALU.subtract)
                        else:
                            r = dve.tensor_tensor(o, tps[:, b, 0:S], h, ALU.subtract)
                        r.then_inc(turn_lo, 1)

            dve.wait_ge(s_pos, 48)
            dve.wait_ge(s_const, 32)
            dve.tensor_copy(lvm[:, :, :], scr[:, 3072:3712].rearrange("p (n t) -> p n t", t=P))
            dve.tensor_copy(prow, prow_i)
            link(dve.tensor_copy(pcol, pcol_i))
            for m in range(M):
                r = dve.tensor_scalar(ang[:, m, :], kst[:, C_INV:C_INV + HD // 2], pcol[:, m:m + 1], None, ALU.mult)
            link(r)
            big = 1.5 * 2 ** 23
            link(dve.tensor_scalar(ang_n, ang, 1.0 / (2 * math.pi), big, ALU.mult, ALU.add))
            link(dve.tensor_scalar(ang_n, ang_n, -big, None, ALU.add))
            c1 = 6.28125
            c2 = float(np.float32(2 * math.pi - c1).view(np.uint32) & np.uint32(0xfffff000))
            c2 = float(np.uint32(np.float32(2 * math.pi - c1).view(np.uint32) & np.uint32(0xfffff000)).view(np.float32))
            c3 = 2 * math.pi - c1 - c2
            for cc in (c1, c2, c3):
                link(dve.scalar_tensor_tensor(ang, ang_n, -cc, ang, ALU.mult, ALU.add))
            link(dve.tensor_scalar(ang, ang, 3.1415925, -3.1415925, ALU.min, ALU.max))
            link(dve.tensor_scalar(ang_n, ang, -1.0, None, ALU.mult))
            dve.tensor_tensor(ang_n, ang, ang_n, ALU.min).then_inc(rot_ready, 1)
            for m in range(M):
                o = slice(0, P) if m == 0 else slice(P, 384)
                r = dve.tensor_scalar(rel[:, o], prow[:, 0:(m + 1) * P], pcol[:, m:m + 1], -1.0, ALU.subtract, ALU.mult)
            link(r)
            link(dve.tensor_scalar(bucket, rel, 0.0, float(EXACT), ALU.max, ALU.min))
            for j in range(1, NB - EXACT):
                thr = math.ceil(EXACT * (MAXD / EXACT) ** (j / (NB - EXACT)))
                link(dve.scalar_tensor_tensor(bucket, rel, float(thr), bucket, ALU.is_ge, ALU.add))
            with loop(dve, NB, {}) as i:
                dve.tensor_tensor(onehot[:, ds(i, 1), :].rearrange("p a k -> p (a k)"), bucket,
                                  kst[:, ds(C_B + i, 1)].broadcast_to([P, 384]), ALU.is_equal).then_inc(onehot_ready, 1)
            dve.wait_ge(vec_ready, 1)
            lp = v2("lb_param_2", 0, NH)
            dve.tensor_tensor(lb_t[:, 0, :], lp, lp, ALU.subtract).then_inc(lb_stats, 1)
            dve.wait_ge(lb_exp, 1)
            link(dve.reciprocal(lb_t[:, 0, :], lb_t[:, 1, :]))
            link(dve.tensor_tensor(lb_t[:, 0, :], lb_t[:, 0, :], lb_t[:, 1, :], ALU.mult))
            link(dve.tensor_tensor(lb_t[:, 1, :], lb_t[:, 0, :], lb_t[:, 0, :], ALU.subtract))
            link(dve.tensor_scalar(lb_t[:, 1, :], lb_t[:, 1, :], 0.0, 1.0 - 1e-6, ALU.max, ALU.min))
            dve.tensor_scalar(lbc[:, 0:NH], lb_t[:, 1, :], -1.0, 1.0, ALU.mult, ALU.add)
            link(dve.tensor_scalar(lbc[:, NH:2 * NH], lb_t[:, 1, :], 1e-30, None, ALU.max))

            m_free = Seen(dve, mod_summed)
            m_land = [Seen(dve, s) for s in raw_landed]
            m_prev = Seen(dve, raw_read, 7)
            for l in range(DEPTH):
                per = {m_free: 2, m_prev: 16}
                per.update({s: 32 for s in m_land})
                with loop(dve, 6, per):
                    for b in range(2):
                        m_free.wait()
                        for j in range(RAW):
                            m_land[j].wait(16)
                            for u in range(2):
                                m_prev.wait()
                                for e in (2 * u, 2 * u + 1):
                                    kt = 4 * j + e
                                    ck = v2("c", kt)
                                    if j == 0:
                                        r = dve.tensor_scalar(macc[:, b, e, :], raw[:, j, e, :], ck, None, ALU.mult)
                                    else:
                                        r = dve.scalar_tensor_tensor(macc[:, b, e, :], raw[:, j, e, :], ck,
                                                                     macc[:, b, e, :], ALU.mult, ALU.add)
                                r.then_inc(raw_read, 1)
            dve.wait_ge(mod_ready, 1)
            for l in range(DEPTH):
                r = dve.scalar_tensor_tensor(acol[:, l * KT:(l + 1) * KT], modc[:, l * 48 + KT:l * 48 + 2 * KT], 1.0,
                                             v1("norm_gain", l * KT, KT), ALU.add, ALU.mult)
            link(r)

            root, accs = Seen(dve, root_ready), Seen(dve, acc_taken, 2)
            rl, sc, lbr, prb, ho = (Seen(dve, s) for s in (relu_ready, scores_ready, lb_ready, probs_ready, heads_out))
            du, rsr, rtk, rrt = Seen(dve, dots_used, 1), Seen(dve, rs_ready), Seen(dve, ret_taken, 2), Seen(dve, ret_root)
            gar, xfree, mbr = Seen(dve, ga_ready), Seen(dve, x_ready), Seen(dve, idx_causal)
            mbd = Seen(dve, mb_ready)

            def row_scale():
                root.wait()
                dve.reciprocal(st[:, 22:24], st[:, 2:4]).then_inc(rstd_ready, 1)

            for l in range(DEPTH):
                row_scale()
                turn(KT // 2, scale=acol[:, l * KT:(l + 1) * KT], bias=modc[:, l * 48:l * 48 + KT])
                split(NCH // 2, 16, 8)
                split(1, 8, 8, width=TAIL)
                accs.wait(NCH + 1)
                sq = scr[:, 3840:3840 + DA + HD]
                for m in range(M):
                    link(dve.tensor_tensor(sq, proj[:, m, 0:DA + HD], proj[:, m, 0:DA + HD], ALU.mult))
                    r = dve.tensor_reduce(st[:, 4 + 9 * m:13 + 9 * m], sq.rearrange("p (h d) -> p h d", d=HD), AX, ALU.add)
                    if m == 0:
                        link(r)
                r.then_inc(sums_ready, 1)
                root.wait()
                link(dve.reciprocal(st[:, 4:22], st[:, 24:42]))
                dve.memset(idx, 0.0).then_inc(rstd_ready, 1)
                with loop(dve, 4, {rl: 4, du: 4}) as i:
                    for b in range(2):
                        for e in range(2):
                            rl.wait()
                            du.wait()
                            for m in range(M):
                                o = slice(0, P) if m == 0 else slice(P, 384)
                                r = dve.scalar_tensor_tensor(idx[:, o], sps[:, e, o],
                                                             proj[:, m, ds(WI + 4 * i + 2 * b + e, 1)], idx[:, o],
                                                             ALU.mult, ALU.add)
                            r.then_inc(dots_used, 1)
                du.rest(1)
                dve.sem_inc(idx_ready, 1)
                mbr.wait(2)
                tiles = [idx[:, 0:P], idx[:, P:384]]
                for n in range(TOPK // 8):
                    for m in range(M):
                        r = dve.max(tmp8[:, m, :], tiles[m])
                    link(r)
                    for m in range(M):
                        r = dve.match_replace(tiles[m], tmp8[:, m, :], tiles[m], -3.4e38)
                    link(r)
                dve.tensor_scalar(mb, idx, -3.2e38, -1e30, ALU.is_ge, ALU.mult).then_inc(sel_ready, 1)
                gar.wait(2)
                with loop(dve, 4, {sc: 2, lbr: 2, prb: 2, ho: 2, linked: 4}) as i:
                    for b in range(2):
                        sc.wait()
                        lbr.wait()
                        link(dve.scalar_tensor_tensor(lg[:, b, :], sps[:, b, 0:384], SCALE, lb_s[:, b, :],
                                                      ALU.mult, ALU.add))
                        dve.tensor_reduce(st[:, 44 + 2 * b:45 + 2 * b], lg[:, b, 0:P], AX, ALU.max, negate=True)\
                           .then_inc(logits_ready, 1)
                        dve.tensor_reduce(st[:, 45 + 2 * b:46 + 2 * b], lg[:, b, P:384], AX, ALU.max, negate=True)\
                           .then_inc(max_ready, 1)
                    for b in range(2):
                        prb.wait()
                        link(dve.reciprocal(st[:, 52 + 2 * b:54 + 2 * b], st[:, 48 + 2 * b:50 + 2 * b]))
                        ho.wait()
                        for m in range(M):
                            g = proj[:, m, ds(GA + (2 * i + b) * HD, HD)]
                            r = dve.scalar_tensor_tensor(g, sps[:, b, m * P:(m + 1) * P], st[:, 52 + 2 * b + m:53 + 2 * b + m],
                                                         g, ALU.mult, ALU.mult)
                        r.then_inc(y_ready, 1)
                with loop(dve, 4, {rsr: 2, rtk: 2, rrt: 1, linked: 3}) as i:
                    for b in range(2):
                        rsr.wait()
                        dve.scalar_tensor_tensor(rst[:, b, 0:S], sps[:, b, 0:S], kst[:, ds(C_KG + 2 * i + b, 1)], maskt,
                                                 ALU.mult, ALU.mult)
                        dve.scalar_tensor_tensor(rst[:, b, S:S + P], sps[:, b, S:S + P], kst[:, ds(C_KG + NH + 2 * i + b, 1)],
                                                 maskt[:, 0:P], ALU.mult, ALU.mult).then_inc(rst_ready, 1)
                    for b in range(2):
                        rtk.wait()
                        for m in range(M):
                            r = dve.bn_stats(bns[:, 2 * b + m, :], ro[:, b, m, :])
                    link(r)
                    dve.sem_inc(dve_passed, 1)
                    for n in range(4):
                        r = dve.bn_aggr(mv[:, n, :], bns[:, n, :])
                    r.then_inc(ret_var, 1)
                    rrt.wait()
                    link(dve.reciprocal(st[:, 4:8], st[:, 0:4]))
                    for n in range(4):
                        r = dve.tensor_scalar(ro[:, n // 2, n % 2, :], ro[:, n // 2, n % 2, :], mv[:, n, 0:1],
                                              st[:, 4 + n:5 + n], ALU.subtract, ALU.mult)
                    link(r)
                    for b in range(2):
                        g = proj[:, :, ds(GB + (2 * i + b) * HD, HD)]
                        r = dve.tensor_tensor(g, g, ro[:, b, :, :], ALU.mult)
                        r.then_inc(yb_ready, 1)
                turn(NH // 2)
                turn(NH // 2, kt0=NH, scale=v2("ret_norm_gain", l * NH, NH))
                dve.wait_ge(gate_bc, 16 * (l + 1))

                def gated(g, b):
                    xfree.wait()
                    dve.tensor_tensor(proj[:, 1, b * 1024:(b + 1) * 1024].rearrange("p (m n) -> p m n", m=M),
                                      acc[:, b, :, :],
                                      proj[:, 0, ds(g * CH, CH)].unsqueeze(1).broadcast_to([P, M, CH]),
                                      ALU.mult).then_inc(acc_taken, 1)
                owners[gated] = {xfree: 2}
                split(2, 16, 8, evac=gated)
                accs.skip(4)

            row_scale()
            turn(KT // 2, scale=v2("norm_mix_g_2", 0, KT))
            hsg, hln, hwr, har, hrt = (Seen(dve, s) for s in (hg_sig, hg_ln, hg_w, hg_a, hg_rstd))
            bsc = hb.rearrange("p (m t) -> p m t", m=M)
            lfs = hs[:, 0:S].rearrange("p (m t) -> p m t", m=M)

            def hgrn_merge():
                har.wait()
                for r in range(5):
                    dve.sem_inc(dve_passed, 1)
                    src = (sps[:, r // 2, r % 2 * S:(r % 2 + 1) * S] if r < 4 else tps[:, 1, 0:S])\
                        .rearrange("p (m t) -> p m t", m=M)
                    o = dve.copy_predicated(hat, lvm[:, r, :].unsqueeze(1).broadcast_to([P, M, P]), src)
                    if r < 4:
                        link(o)
                o.then_inc(hg_at, 1)

            def hgrn_y(g):
                hrt.wait()
                for m in range(M):
                    og = proj[:, m, ds(3072 + g * HD, HD)]
                    r = dve.scalar_tensor_tensor(og, tps[:, 1, S + m * P:S + (m + 1) * P], st[:, 4 + m:5 + m], og,
                                                 ALU.mult, ALU.mult)
                r.then_inc(hg_y, 1)

            def hgrn(t, x, first):
                g, n = 2 * t + x // 8, x % 8
                begin = first and x < 8
                if n == 2 and not begin:
                    hgrn_merge()
                if n == 3:
                    hsg.wait()
                    one_lb, floor = lbc[:, ds(g, 1)], lbc[:, ds(NH + g, 1)]
                    dve.tensor_scalar(hk, hk, one_lb, None, ALU.mult)
                    link(dve.tensor_scalar(hb, hs[:, 0:S], one_lb, floor, ALU.mult, ALU.add))
                    dve.tensor_scalar(hs[:, 0:S], hb, 2.0 ** -60, None, ALU.max)
                    dve.tensor_scalar(hs[:, S:2 * S], hb, 2.0 ** -60, 2.0 ** 60, ALU.min, ALU.mult).then_inc(hg_f, 1)
                if n == 4:
                    hln.wait()
                    link(dve.tensor_tensor(hs[:, 0:S], hs[:, 0:S], hs[:, S:2 * S], ALU.add))
                    for m in range(M):
                        r = dve.tensor_tensor_scan(bsc[:, m, :], ones128, lfs[:, m, :], 0.0, ALU.mult, ALU.add)
                    r.then_inc(hg_b, 1)
                    hbd.wait()
                    for _, first_half, second, mid in level_views(wk, hb):
                        dve.tensor_tensor(second[0], second[1], mid, ALU.subtract)
                    dve.tensor_copy(wk[:, LEVELS, P:S], hb[:, P:S]).then_inc(hg_d2, 1)
                if n == 6:
                    hwr.wait()
                    for _, first_half, second, mid in level_views(wk, hq):
                        dve.tensor_tensor(second[0], second[0], second[1], ALU.mult)
                    dve.tensor_tensor(wk[:, LEVELS, P:S], wk[:, LEVELS, P:S], hq[:, P:S], ALU.mult).then_inc(hg_x2, 1)
                if n == 7 and not begin:
                    hgrn_y(g - 1)

            hbd = Seen(dve, hg_b)
            for col, n in W2_PARTS:
                accs.skip(n)
                if col == GATES:
                    gar.wait(2)
                    link(dve.memset(hat, 0.0))
                    split(n // 2, 16, 8, side=hgrn,
                          side_per={hsg: 2, hln: 2, hwr: 2, har: 2, hrt: 2, hbd: 2, linked: 12})
                    hgrn_merge()
                    hgrn_y(NH - 1)
                else:
                    split(n // 2, 16, 8)
            dve.memset(ut, 0.0).then_inc(cv_hi, 1)
            cuu, chh, cll = Seen(dve, cv_u), Seen(dve, cv_hi, 1), Seen(dve, cv_lo)
            cw = v2("conv_w_2", 0, 24)
            with loop(dve, 4, {cuu: 2, chh: 2, cll: 2, linked: 6}) as i:
                for b in range(2):
                    cll.wait()
                    cuu.wait()
                    k = 2 * i + b
                    link(dve.tensor_scalar(ct[:, b, :], ut[:, b, 2:258], cw[:, ds(16 + k, 1)], None, ALU.mult))
                    link(dve.scalar_tensor_tensor(ct[:, b, :], ut[:, b, 1:257], cw[:, ds(8 + k, 1)], ct[:, b, :],
                                                  ALU.mult, ALU.add))
                    link(dve.scalar_tensor_tensor(ct[:, b, :], ut[:, b, 0:256], cw[:, ds(k, 1)], ct[:, b, :],
                                                  ALU.mult, ALU.add))
                    dve.tensor_tensor(ct[:, b, :], ct[:, b, :], tps[:, b, S:2 * S], ALU.mult).then_inc(cv_y, 1)
                for b in range(2):
                    chh.wait()
                    at = ds(2 * i + b, 1)
                    dve.tensor_tensor(ht_lo[:, at, :].rearrange("p a t -> p (a t)"), ct[:, b, :],
                                      ht_hi[:, at, :].rearrange("p a t -> p (a t)").bitcast(F32),
                                      ALU.subtract).then_inc(cv_lo, 1)
            turn(NH // 2, kt0=NH, scale=v2("hg_norm_g_2", 0, NH))

            def merge(g, b):
                gt = proj[:, :, ds(4096 + b * 2048 + (g - b) * (CH // 2), CH)]
                dve.tensor_tensor(gt, acc[:, b, :, :], gt, ALU.mult).then_inc(acc_taken, 1)
            split(4, 8, 4, evac=merge)
            turn(KT // 2)

            def add_x(g, b):
                xs = xres[:, :, ds(g * CH, CH)]
                dve.tensor_tensor(xs, acc[:, b, :, :], xs, ALU.add).then_inc(acc_taken, 1)
            split(2, 16, 8, evac=add_x)
            row_scale()
            turn(KT // 2, scale=v2("ple_norm_g_2", 0, KT))
            accs.skip(8 + 4)
            split(2, 16, 8)
            turn(1)
            split(1, 4, 1, halves=1)
            accs.wait(8)
            link(dve.tensor_tensor(proj[:, :, 0:D], proj[:, :, 0:D], proj[:, :, D:2 * D], ALU.mult))
            dve.tensor_tensor(xres[:, :, :], xres[:, :, :], proj[:, :, 0:D], ALU.add).then_inc(x_ready, 1)
            root.wait()
            link(dve.reciprocal(st[:, 22:24], st[:, 2:4]))
            dve.wait_ge(fin_g, 16)
            for m in range(M):
                dve.scalar_tensor_tensor(proj[:, m, 0:D], xres[:, m, :], st[:, 22 + m:23 + m], proj[:, 0, 4096:6144],
                                         ALU.mult, ALU.mult).then_inc(fin_ready, 1)

        @block.gpsimd
        def _(pool):
            pool.sem_inc(x_ready, 2)
            linked = Seen(pool, pool_link)

            def link(ins):
                ins.then_inc(pool_link, 1)
                linked.wait()

            link(pool.memset(scr[:, 0:3072], 0.0))
            pool.wait_ge(s_rb, 16)
            oh = Seen(pool, onehot_ready)
            with loop(pool, NB, {oh: 1, linked: 2}) as i:
                oh.wait()
                link(pool.tensor_tensor(btmp, onehot[:, ds(i, 1), :].broadcast_to([P, NH, 384]),
                                        bc(rbt[:, ds(i * NH, NH)], 384), ALU.mult))
                link(pool.tensor_tensor(bias, bias, btmp, ALU.add))
            pool.wait_ge(mod_taken, 2 + 12 * DEPTH)
            pool.tensor_tensor(modc[:, :], modc[:, :], v1("b_mod", 0, 96), ALU.add).then_inc(mod_ready, 1)

            xfree = Seen(pool, turned)
            rstd, accs = Seen(pool, rstd_ready), Seen(pool, acc_taken, 2)
            qif, qnf, lbf, rqf = (Seen(pool, s) for s in (qi_turned, qn_turned, logits_ready, rqk_turned))
            idr, slr, yr, ybr = Seen(pool, idx_ready), Seen(pool, sel_ready), Seen(pool, y_ready, 2), Seen(pool, yb_ready, 2)
            rdone = Seen(pool, rot_done, 2)
            mbr = Seen(pool, mb_ready)
            ktn = Seen(pool, k_turned)

            def turn(n, make):
                with loop(pool, n, {xfree: 2}) as i:
                    for b in range(2):
                        xfree.wait()
                        make(xn[:, b, :, :], 2 * i + b).then_inc(turn_in, 1)

            def x_tile(o, k):
                return pool.tensor_tensor(o, xres[:, :, ds(k * P, P)], bc(st[:, 22:24], P), ALU.mult)

            def proj_tile(col):
                return lambda o, k: pool.tensor_copy(o, proj[:, :, ds(col + k * P, P)])

            def causal(t, fill, done):
                for m in range(M):
                    o = t[:, 0:P] if m == 0 else t[:, P:384]
                    pool.affine_select(out=o, in_=o, compare_op=ALU.is_ge, fill=fill, base=m * P,
                                       pattern=[[-1, (m + 1) * P]], channel_multiplier=1).then_inc(done, 1)

            xs = Seen(pool, acc_taken, 2)
            for l in range(DEPTH):
                rstd.wait()
                turn(KT // 2, x_tile)
                accs.wait(NCH + 1)
                xfree.rest(2)
                for e in range(2):
                    r = pool.tensor_copy(xn[:, 0, :, 64 * e:64 * e + 64], proj[:, :, KI:KI + ID])
                r.then_inc(k_ready, 1)
                rstd.wait()
                rs9 = st[:, 4:22].rearrange("p (m h) -> p m h", m=M)
                pool.tensor_tensor(xn[:, 1, :, :], proj[:, :, KA:KA + HD], bc(rs9[:, :, 8], HD), ALU.mult)\
                    .then_inc(k_ready, 1)
                ktn.wait()
                with loop(pool, 4, {qif: 2}) as i:
                    for b in range(2):
                        qif.wait()
                        pool.tensor_copy(xn[:, b, :, :], proj[:, :, ds(QI + (2 * i + b) * P, P)]).then_inc(qi_ready, 1)
                idr.wait()
                causal(idx, -3e38, idx_causal)
                slr.wait()
                causal(mb, -1e30, mb_ready)
                mbr.wait(2)
                qif.rest(2)
                with loop(pool, 4, {qnf: 2, lbf: 2}) as i:
                    for b in range(2):
                        h = 2 * i + b
                        qnf.wait()
                        pool.tensor_tensor(xn[:, b, :, :], proj[:, :, ds(QA + h * HD, HD)],
                                           rs9[:, :, ds(h, 1)].broadcast_to([P, M, HD]), ALU.mult).then_inc(qn_ready, 1)
                        lbf.wait()
                        pool.tensor_tensor(lb_s[:, b, :], bias[:, ds(h, 1), :].rearrange("p a k -> p (a k)"), mb,
                                           ALU.add).then_inc(lb_ready, 1)
                yr.wait(8)
                t4 = [rtmp[:, a, :, :].rearrange("p (w m) d -> p w m d", w=2) for a in range(4)]
                qk = proj[:, :, QB:QB + 2 * DA].rearrange("p m (w n) -> p w m n", w=2)
                cos, sin = (cs[:, a, :, :].unsqueeze(1).broadcast_to([P, 2, M, HD // 2]) for a in range(2))
                half = HD // 2
                with loop(pool, 4, {rqf: 2, linked: 2, rdone: 2}) as i:
                    for b in range(2):
                        h = 2 * i + b
                        rqf.wait()
                        x1, x2 = qk[:, :, :, ds(h * HD, half)], qk[:, :, :, ds(h * HD + half, half)]
                        pool.tensor_tensor(t4[0], x1, cos, ALU.mult)
                        pool.tensor_tensor(t4[1], x2, sin, ALU.mult)
                        pool.tensor_tensor(t4[2], x1, sin, ALU.mult)
                        link(pool.tensor_tensor(t4[3], x2, cos, ALU.mult))
                        pool.tensor_tensor(rqk[:, b, :, :, 0:half], t4[0], t4[1], ALU.subtract)
                        pool.tensor_tensor(rqk[:, b, :, :, half:HD], t4[2], t4[3], ALU.add).then_inc(rot_done, 1)
                        rdone.wait()
                ybr.wait(8)
                turn(NH // 2, proj_tile(GA))
                turn(NH // 2, proj_tile(GB))
                for g in range(4):
                    accs.wait()
                    b = g % 2
                    t = xres[:, :, g * CH:(g + 1) * CH]
                    pool.tensor_tensor(t, t, proj[:, 1, b * 1024:(b + 1) * 1024].rearrange("p (m n) -> p m n", m=M),
                                       ALU.add).then_inc(x_ready, 1)

            rstd.wait()
            turn(KT // 2, x_tile)
            hin, hbr, hwr, hss = (Seen(pool, s) for s in (hg_turned, hg_b, hg_w, hg_ss))
            accs.skip(16)
            pool.wait_ge(ga_ready, 2 * DEPTH + 2)

            def hgrn_scale():
                hss.wait(2)
                link(pool.tensor_tensor(st[:, 2:4], st[:, 0:2], eps.broadcast_to([P, M]), ALU.add))
                pool.tensor_tensor(st[:, 4:6], st[:, 2:4], kst[:, C_PW:C_PW + 2], ALU.pow).then_inc(hg_rstd, 1)

            def hgrn(g, first):
                hin.wait()
                pool.tensor_copy(xn[:, 0, :, :], proj[:, :, ds(g * HD, HD)])
                pool.tensor_copy(xn[:, 1, :, :], proj[:, :, ds(1024 + g * HD, HD)]).then_inc(hg_in, 1)
                hbr.wait()
                for _, first_half, second, mid in level_views(wk, hb):
                    pool.tensor_tensor(first_half[0], mid, first_half[1], ALU.subtract)
                pool.tensor_tensor(wk[:, LEVELS, 0:P], hb[:, P - 1:P].broadcast_to([P, P]), hb[:, 0:P],
                                   ALU.subtract).then_inc(hg_d1, 1)
                hwr.wait()
                for _, first_half, second, mid in level_views(wk, hk):
                    pool.tensor_tensor(first_half[0], first_half[0], first_half[1], ALU.mult)
                pool.tensor_tensor(wk[:, LEVELS, 0:P], wk[:, LEVELS, 0:P], hk[:, 0:P], ALU.mult).then_inc(hg_x1, 1)
                if not first:
                    hgrn_scale()

            hgrn(0, True)
            with loop(pool, NH - 1, {hin: 1, hbr: 1, hwr: 1, hss: 2, linked: 1}) as i:
                hgrn(i + 1, False)
            hgrn_scale()
            accs.skip(8)
            pool.wait_ge(ga_ready, 2 * DEPTH + 3)
            cvf = Seen(pool, cv_turned)
            lgc = scr[:, 3584:4096].rearrange("p (b m d) -> p b m d", b=2, m=M)
            with loop(pool, 4, {cvf: 2}) as i:
                for b in range(2):
                    k = 2 * i + b
                    cvf.wait()
                    pool.tensor_tensor(xn[:, b, :, :], cg2[:, :, ds(k * P, P)], proj[:, :, ds(1024 + k * P, P)], ALU.mult)
                    pool.tensor_tensor(lgc[:, b, :, :], proj[:, :, ds(k * P, P)], proj[:, :, ds(2048 + k * P, P)],
                                       ALU.mult).then_inc(cv_in, 1)
            cvf.rest(2)
            turn(NH // 2, proj_tile(3072))
            accs.wait(8)
            turn(KT // 2, lambda o, k: pool.tensor_tensor(o, proj[:, :, ds(4096 + k * P, P)], proj[:, :, ds(6144 + k * P, P)],
                                                          ALU.add))
            rstd.wait()
            turn(KT // 2, x_tile)
            pool.wait_ge(p_landed, 16)
            turn(1, proj_tile(6144))


_INS = ["x", "c", "positions", "rel_bias", "norm_gain", "w_mod", "b_mod", "w_in", "q_norm_gain", "k_norm_gain",
        "ret_norm_gain", "w_out", "p_2", "norm_mix_g_2", "w_in_2", "conv_w_2", "lb_param_2", "hg_norm_g_2",
        "w_a_out_2", "w_b_out_2", "w_o_2", "ple_norm_g_2", "w_ple_gate_2", "w_ple_proj_2", "final_norm_g_2"]


def kernel(**inputs):
    import concourse.bacc as bacc
    from concourse.bass_utils import run_bass_kernel_spmd

    nc = bacc.Bacc("TRN2", target_bir_lowering=False, num_devices=1)
    arrays, args = {}, []
    consts, levels = constants()
    for name, a in [(n, np.ascontiguousarray(inputs[n])) for n in _INS] + [("consts", consts), ("levels", levels)]:
        arrays["in_" + name] = a
        args.append(nc.dram_tensor("in_" + name, a.shape, mybir.dt.from_np(a.dtype), kind="ExternalInput").ap())
    out = nc.dram_tensor("out_0", (1, S, D), F32, kind="ExternalOutput").ap()
    build(nc, *args, out)
    r = run_bass_kernel_spmd(nc, [arrays], core_ids=[0])
    return r.results[0]["out_0"]
```

```python
from contextlib import ExitStack, contextmanager
import math

import numpy as np
import concourse.bass as bass
from concourse import mybir

F32 = mybir.dt.float32
F32R = mybir.dt.float32r
I32 = mybir.dt.int32
U8 = mybir.dt.uint8
ALU = mybir.AluOpType
ACT = mybir.ActivationFunctionType
AX = mybir.AxisListType.X
ds = bass.ds

P = 128
D = 2048
S = 256
M = S // P
KT = D // P
DEPTH = 2
HD = 128
NH = 8
DA = NH * HD
IH, ID = 16, 64
TOPK = min(256, S // 4)
NB = 32
EXACT, MAXD = 16, 128
EPS = 1e-6
SCALE = HD ** -0.5
CH = 512

QA = 0
KA = QA + DA
VA = KA + HD
GA = VA + HD
QI = GA + DA
KI = QI + IH * ID
WI = KI + ID
QB = WI + IH
KB = QB + DA
VB = KB + DA
GB = VB + DA
N_IN = GB + DA
NCH = N_IN // CH
TAIL = N_IN - NCH * CH
IN2 = 6 * D

C_ID = 0
C_MASK = C_ID + P
C_INV = C_MASK + 2 * P
C_QG = C_INV + HD // 2
C_KG = C_QG + M * NH
C_B = C_KG + M * NH
C_EPS = C_B + NB
C_HPI = C_EPS + 1
C_PW = C_HPI + 1
C_N = C_PW + 2

V1 = {"b_mod": (0, 96), "norm_gain": (96, 32)}
V2, _at = {}, 0
for _n, _k in (("c", 16), ("norm_mix_g_2", 16), ("hg_norm_g_2", 8), ("ple_norm_g_2", 16), ("conv_w_2", 24),
               ("lb_param_2", 8), ("ret_norm_gain", 16), ("q_norm_gain", 2), ("k_norm_gain", 2)):
    V2[_n] = (_at, _k)
    _at += _k
NV2 = _at
LEVELS = 7

B_BESIDE = 12
RAW = 4
B_FIRST = 15
SPL = 4


def constants():
    k = np.zeros((P, C_N), np.float32)
    k[:, C_ID:C_ID + P] = np.eye(P)
    r = np.arange(P)
    k[:, C_MASK:C_MASK + P] = (r[None, :] >= r[:, None])
    k[:, C_MASK + P:C_MASK + 2 * P] = 1.0
    half = HD // 2
    k[:, C_INV:C_INV + half] = np.float32(10000.0) ** (-np.arange(half, dtype=np.float32) / np.float32(half))
    lg = np.log1p(-np.exp2(-5.0 - np.arange(NH)))
    for m in range(M):
        t = (m * P + r)[:, None]
        k[:, C_QG + m * NH:C_QG + (m + 1) * NH] = np.exp(lg[None, :] * t)
        k[:, C_KG + m * NH:C_KG + (m + 1) * NH] = np.exp(-lg[None, :] * t) * SCALE
    k[:, C_B:C_B + NB] = np.arange(NB)
    k[:, C_EPS] = EPS
    k[:, C_HPI] = math.pi / 2
    k[:, C_PW:C_PW + 2] = -0.5
    lv = np.zeros((P, 5, P), np.float32)
    for n in range(LEVELS):
        b = 64 >> n
        lv[:, max(n - 3, 0)] += ((r[:, None] // (2 * b) == r[None, :] // (2 * b)) & (r[:, None] // b % 2 == 0)
                                 & (r[None, :] // b % 2 == 1))
    lv[:, 4] = np.eye(P)
    return k, lv


class Seen:

    def __init__(self, eng, sem, start=0):
        self.eng, self.sem, self.n, self.i, self.per, self.base = eng, sem, start, None, 0, 0

    def next(self, more=1):
        self.n += more
        return self.n + self.base if self.i is None else self.i * self.per + (self.base + self.n)

    def skip(self, n):
        self.n += n

    def ahead(self, n):
        v = self.next(n)
        self.n -= n
        return v


@contextmanager
def loop(eng, turns, per):
    with eng.Fori(0, turns) as i:
        for s, n in per.items():
            s.i, s.per, s.base, s.n = i, n, s.n, 0
        yield i
        for s, n in per.items():
            assert s.n == n, (s.sem, s.n, n)
            s.i, s.n, s.base = None, s.base + turns * n, 0


def bc(ap, n):
    return ap.unsqueeze(len(ap.shape)).broadcast_to([*ap.shape, n])


def build(nc, x, c, positions, rel_bias, norm_gain, w_mod, b_mod, w_in, q_norm_gain, k_norm_gain, ret_norm_gain,
          w_out, p_2, norm_mix_g_2, w_in_2, conv_w_2, lb_param_2, hg_norm_g_2, w_a_out_2, w_b_out_2, w_o_2,
          ple_norm_g_2, w_ple_gate_2, w_ple_proj_2, final_norm_g_2, consts, levels, out):
    ctx = ExitStack()
    with ctx:
        def sb(name, shape, dt=F32):
            return ctx.enter_context(nc.sbuf_tensor(name, shape, dt))

        def sem(name):
            return ctx.enter_context(nc.semaphore(name))

        xres = sb("xres", [P, M, D])
        ht_hi = sb("ht_hi", [P, KT, S], F32R)
        ht_lo = sb("ht_lo", [P, KT, S], F32R)
        proj = sb("proj", [P, M, 8192])
        raw = sb("raw", [P, RAW, 4, CH])
        w_hi = sb("w_hi", [P, SPL, 2, CH], F32R)
        w_lo = sb("w_lo", [P, SPL, 2, CH], F32R)
        scr = sb("scr", [P, 6144])
        kst = sb("kst", [P, C_N])
        lvm = sb("lvm", [P, 5, P], U8)
        vcol = sb("vcol", [P, P + NV2])
        modc = sb("modc", [P, DEPTH * 48])
        acol = sb("acol", [P, DEPTH * KT])
        lbc = sb("lbc", [P, 3 * NH])
        cs = proj[:, 1, N_IN + 384:N_IN + 640].rearrange("p (a m d) -> p a m d", a=2, m=M)
        xn = sb("xn", [P, 2, M, P])
        ktile = proj[:, 0, N_IN:N_IN + S]
        mb = proj[:, 1, N_IN:N_IN + 384]
        st = sb("st", [P, 64])
        tmp8 = proj[:, 0, N_IN + 256:N_IN + 272].rearrange("p (m k) -> p m k", m=M)
        bns = proj[:, 0, N_IN + 272:N_IN + 296].rearrange("p (n k) -> p n k", n=4)
        mv = proj[:, 0, N_IN + 296:N_IN + 304].rearrange("p (n k) -> p n k", n=4)

        ident = kst[:, C_ID:C_ID + P]
        maskt = kst[:, C_MASK:C_MASK + 2 * P]
        eps = kst[:, C_EPS:C_EPS + 1]
        ones = kst[:, C_MASK + P:C_MASK + P + 1]
        ones128 = kst[:, C_MASK + P:C_MASK + 2 * P]

        macc = scr[:, 3072:5120].rearrange("p (b e n) -> p b e n", b=2, e=2)
        rbt = scr[:, 5120:5376]
        onehot = proj[:, 1, QB + 1024:N_IN].bitcast(U8).rearrange("p (b k) -> p b k", b=NB)
        btmp = proj[:, 0, QB + 1024:N_IN].rearrange("p (b h k) -> p b h k", b=2, h=NH // 2)
        bucket = proj[:, 0, 2048:2432]
        rel = proj[:, 0, 2432:2816]
        prow_i = proj[:, 1, 2048:2304].bitcast(I32)
        prow = proj[:, 1, 2304:2560]
        pcol_i = proj[:, 1, 2560:2562].bitcast(I32)
        pcol = proj[:, 1, 2562:2564]
        ang = proj[:, 1, 2564:2692].rearrange("p (m d) -> p m d", m=M)
        ang_n = proj[:, 1, 2692:2820].rearrange("p (m d) -> p m d", m=M)
        lb_t = proj[:, 1, 2820:2836].rearrange("p (a h) -> p a h", a=2)

        def v1(n, i=0, k=1):
            return vcol[:, V1[n][0] + i:V1[n][0] + i + k]

        def v2(n, i=0, k=1):
            return vcol[:, P + V2[n][0] + i:P + V2[n][0] + i + k]

        bias = scr[:, 0:3072].rearrange("p (h k) -> p h k", h=NH)
        lb_s = scr[:, 3072:3840].rearrange("p (b k) -> p b k", b=2)
        lg = scr[:, 3840:4608].rearrange("p (b k) -> p b k", b=2)
        pt = scr[:, 4608:5376].rearrange("p (b k) -> p b k", b=2)
        qt = scr[:, 5376:5888].rearrange("p (b k) -> p b k", b=2)
        ttmp = scr[:, 5888:6144]
        ttmp2 = scr[:, 5632:6144].rearrange("p (b t) -> p b t", b=2)
        idx = proj[:, 0, N_IN + 304:N_IN + 688]
        kit = scr[:, 5888:6144]
        sq = scr[:, 3840:3840 + 640]
        rqk = scr[:, 3072:4096].rearrange("p (b w m d) -> p b w m d", b=2, w=2, m=M)
        rqt = scr[:, 4096:5120].rearrange("p (b w t) -> p b w t", b=2, w=2)
        rst = scr[:, 5120:5888].rearrange("p (b k) -> p b k", b=2)
        ro = proj[:, 0, 0:512].rearrange("p (b m d) -> p b m d", b=2, m=M)
        rtmp = proj[:, 1, 0:1024].rearrange("p (a w d) -> p a w d", a=4, w=4)
        wk = scr[:, 0:2048].rearrange("p (n t) -> p n t", t=S)
        wq = scr[:, 2048:4096].rearrange("p (n t) -> p n t", t=S)
        hq = scr[:, 4096:4352]
        hk = scr[:, 4352:4608]
        hs = scr[:, 4608:5120]
        hb = scr[:, 5120:5376]
        hat = scr[:, 5376:5632].rearrange("p (m t) -> p m t", m=M)
        hax = scr[:, 5632:5760]
        hy = scr[:, 5888:6144].rearrange("p (m d) -> p m d", m=M)
        cg2 = scr[:, 0:2048].rearrange("p (m n) -> p m n", m=M)
        ut = scr[:, 2048:2048 + 2 * 258].rearrange("p (b t) -> p b t", b=2)
        ct = scr[:, 2560 + 8:2560 + 8 + 512].rearrange("p (b t) -> p b t", b=2)

        def level_views(dst, src):
            for n in range(LEVELS):
                h = 64 >> n
                dv, sv = (a.rearrange("p (n two t) -> p n two t", two=2, t=h) for a in (dst[:, n, :], src))
                yield (n, (dv[:, :, 0, :], sv[:, :, 0, :]), (dv[:, :, 1, :], sv[:, :, 1, :]),
                       sv[:, :, 0, h - 1:h].broadcast_to([P, S // (2 * h), h]))

        acc = ctx.enter_context(nc.psum_tensor("acc", [P, 2, M, CH], F32))
        tps = ctx.enter_context(nc.psum_tensor("tps", [P, 2, CH], F32))
        sps = ctx.enter_context(nc.psum_tensor("sps", [P, 2, CH], F32))

        gates = nc.dram_tensor("gates", (DEPTH * KT, P), F32, kind="Internal").ap()

        s_const = sem("s_const")
        s_x = sem("s_x")
        s_vec = sem("s_vec")
        s_pos = sem("s_pos")
        s_rb = sem("s_rb")
        vec_turned = sem("vec_turned")
        vec_ready = sem("vec_ready")
        c_ready = sem("c_ready")
        raw_landed = [sem(f"raw_landed{j}") for j in range(RAW)]
        hi_ready = sem("hi_ready")
        raw_read = sem("raw_read")
        split_used = sem("split_used")
        acc_taken = sem("acc_taken")
        dve_link = sem("dve_link")
        dve_passed = sem("dve_passed")
        act_link = sem("act_link")
        pool_link = sem("pool_link")
        mod_summed = sem("mod_summed")
        mod_taken = sem("mod_taken")
        gate_turned = sem("gate_turned")
        gate_rows = sem("gate_rows")
        gate_out = sem("gate_out")
        gate_bc = sem("gate_bc")
        onehot_ready = sem("onehot_ready")
        bias_product_ready = sem("bias_product_ready")
        bias_added = sem("bias_added")
        rot_ready = sem("rot_ready")
        sums_ready = sem("sums_ready")
        root_ready = sem("root_ready")
        rstd_ready = sem("rstd_ready")
        turn_in = sem("turn_in")
        turned = sem("turned")
        turn_hi = sem("turn_hi")
        turn_lo = sem("turn_lo")
        proj_ready = sem("proj_ready")
        x_ready = sem("x_ready")
        k_ready = sem("k_ready")
        k_turned = sem("k_turned")
        kt_ready = sem("kt_ready")
        qi_turned = sem("qi_turned")
        qit_ready = sem("qit_ready")
        dots_ready = sem("dots_ready")
        relu_ready = sem("relu_ready")
        dots_used = sem("dots_used")
        idx_ready = sem("idx_ready")
        idx_causal = sem("idx_causal")
        sel_ready = sem("sel_ready")
        mb_ready = sem("mb_ready")
        qn_ready = sem("qn_ready")
        qn_turned = sem("qn_turned")
        qt_ready = sem("qt_ready")
        lb_ready = sem("lb_ready")
        scores_ready = sem("scores_ready")
        logits_ready = sem("logits_ready")
        max_ready = sem("max_ready")
        probs_ready = sem("probs_ready")
        probs_turned = sem("probs_turned")
        pt_ready = sem("pt_ready")
        heads_out = sem("heads_out")
        y_ready = sem("y_ready")
        ga_ready = sem("ga_ready")
        rot_done = sem("rot_done")
        rqk_turned = sem("rqk_turned")
        rqt_ready = sem("rqt_ready")
        rs_ready = sem("rs_ready")
        rst_ready = sem("rst_ready")
        ret_out = sem("ret_out")
        ret_taken = sem("ret_taken")
        ret_var = sem("ret_var")
        ret_root = sem("ret_root")
        yb_ready = sem("yb_ready")
        act_acc = sem("act_acc")
        lb_stats = sem("lb_stats")
        lb_exp = sem("lb_exp")
        lbc_ready = sem("lbc_ready")
        hg_in = sem("hg_in")
        hg_turned = sem("hg_turned")
        hg_sig = sem("hg_sig")
        hg_f = sem("hg_f")
        hg_ln = sem("hg_ln")
        hg_w = sem("hg_w")
        hg_b = sem("hg_b")
        hg_d1 = sem("hg_d1")
        hg_d2 = sem("hg_d2")
        hg_x1 = sem("hg_x1")
        hg_x2 = sem("hg_x2")
        hg_rstd = sem("hg_rstd")
        hg_a = sem("hg_a")
        hg_at = sem("hg_at")
        hg_axr = sem("hg_axr")
        hg_o = sem("hg_o")
        hg_ss = sem("hg_ss")
        hg_y = sem("hg_y")
        cv_in = sem("cv_in")
        cv_turned = sem("cv_turned")
        cv_u = sem("cv_u")
        cv_c = sem("cv_c")
        cv_y = sem("cv_y")
        cv_hi = sem("cv_hi")
        cv_lo = sem("cv_lo")
        p_landed = sem("p_landed")
        fin_g = sem("fin_g")
        fin_ready = sem("fin_ready")
        s_out = sem("s_out")

        x_rows = x[0].rearrange("(m p) d -> p m d", p=P)
        out_rows = out[0].rearrange("(m p) d -> p m d", p=P)

        def ktiles(w):
            return w.rearrange("(k p) n -> p k n", p=P)

        wm = [ktiles(w_mod[l]) for l in range(DEPTH)]
        wi = [ktiles(w_in[l]) for l in range(DEPTH)]
        wo = [ktiles(w_out[l]) for l in range(DEPTH)]
        wi2 = ktiles(w_in_2[0])
        wa2, wb2, wo2 = ktiles(w_a_out_2[0]), ktiles(w_b_out_2[0]), ktiles(w_o_2[0])
        wg2, wp2 = ktiles(w_ple_gate_2[0]), ktiles(w_ple_proj_2[0])

        def full(w):
            return lambda j, col, n: w[:, 4 * j:4 * j + 4, ds(col, n)]

        def two(j, col, n):
            return (wa2 if j < 2 else wb2)[:, 4 * (j % 2):4 * (j % 2) + 4, ds(col, n)]

        REC, GATES, CONV = 4096, 8192, 0
        W2_PARTS = [(REC, 8), (GATES, 8), (CONV, 2), (CONV + 1024, 6)]

        block = ctx.enter_context(nc.Block())

        @block.sync
        def _(sp):
            free = Seen(sp, raw_read)

            sp.dma_start(vcol[0:96, 0:P], b_mod.rearrange("l (k p) -> (l k) p", p=P)).then_inc(s_vec, 16)
            sp.dma_start(vcol[96:128, 0:P], norm_gain.rearrange("l (k p) -> (l k) p", p=P)).then_inc(s_vec, 16)
            for name, ap in (("c", c), ("norm_mix_g_2", norm_mix_g_2), ("hg_norm_g_2", hg_norm_g_2),
                             ("ple_norm_g_2", ple_norm_g_2), ("lb_param_2", lb_param_2),
                             ("ret_norm_gain", ret_norm_gain), ("q_norm_gain", q_norm_gain),
                             ("k_norm_gain", k_norm_gain)):
                o, k = V2[name]
                sp.dma_start(xn[o:o + k, 0, 0, :], ap.rearrange("l (k p) -> (l k) p", p=P)).then_inc(s_vec, 16)
            o, k = V2["conv_w_2"]
            sp.dma_start(xn[o:o + k, 0, 0, :], conv_w_2[0].rearrange("t (k p) -> (t k) p", p=P)).then_inc(s_vec, 16)
            sp.dma_start(kst[:, :], consts).then_inc(s_const, 16)
            sp.dma_start(scr[:, 5376:6016], levels.rearrange("p n t -> p (n t)")).then_inc(s_const, 16)

            def pieces(src, col, n, width=CH, kts=4):
                for j in range(RAW):
                    sp.wait_ge(raw_read, free.next(2))
                    sp.dma_start(raw[:, j, 0:kts, 0:width], src(j, col, width)).then_inc(raw_landed[j], 16)

            def with_mod(src, col, mod, mod_col):
                for j in range(4):
                    for n, (w, at) in enumerate(((src, col), (mod, mod_col))):
                        slot = (2 * j + n) % RAW
                        sp.wait_ge(raw_read, free.next(2))
                        sp.dma_start(raw[:, slot, :, :], w(j, at, CH)).then_inc(raw_landed[slot], 16)

            with loop(sp, 8, {free: 8}) as i:
                pieces(full(wm[0]), i * CH, CH)
            with loop(sp, 4, {free: 16}) as i:
                with_mod(full(wi[0]), i * -CH + 6 * CH, full(wm[0]), 2 * D + i * CH)
            with loop(sp, 2, {free: 16}) as i:
                with_mod(full(wi[0]), i * -CH + 2 * CH, full(wm[1]), i * CH)
            pieces(full(wi[0]), 0, CH)
            with loop(sp, 5, {free: 8}) as i:
                pieces(full(wi[0]), 7 * CH + i * CH, CH)
            with loop(sp, 2, {free: 16}) as i:
                with_mod(full(wi[0]), 12 * CH + i * CH, full(wm[1]), 2 * CH + i * CH)
            pieces(full(wi[0]), NCH * CH, CH, width=TAIL)
            with loop(sp, 4, {free: 16}) as i:
                with_mod(full(wo[0]), i * CH, full(wm[1]), 4 * CH + i * CH)
            with loop(sp, 4, {free: 16}) as i:
                with_mod(full(wi[1]), i * -CH + 6 * CH, full(wm[1]), 2 * D + i * CH)
            with loop(sp, 3, {free: 8}) as i:
                pieces(full(wi[1]), i * -CH + 2 * CH, CH)
            with loop(sp, 7, {free: 8}) as i:
                pieces(full(wi[1]), 7 * CH + i * CH, CH)
            pieces(full(wi[1]), NCH * CH, CH, width=TAIL)
            with loop(sp, 4, {free: 8}) as i:
                pieces(full(wo[1]), i * CH, CH)
            for col, n in W2_PARTS:
                with loop(sp, n, {free: 8}) as i:
                    pieces(full(wi2), col + i * CH, CH)
            with loop(sp, 4, {free: 8}) as i:
                pieces(two, i * CH, CH)
            with loop(sp, 4, {free: 8}) as i:
                pieces(full(wo2), i * CH, CH)
            with loop(sp, 4, {free: 8}) as i:
                pieces(full(wg2), i * CH, CH)
            for j in range(RAW):
                sp.wait_ge(raw_read, free.next(2))
                sp.dma_start(raw[:, j, 0:2, :], wp2[:, :, j * CH:(j + 1) * CH]).then_inc(raw_landed[j], 16)
            sp.wait_ge(fin_ready, 2)
            sp.dma_start(out_rows, proj[:, :, 0:D]).then_inc(s_out, 16)
            sp.wait_ge(s_out, 16)

        @block.tensor
        def _(pe):
            pe.sem_inc(split_used, SPL)
            pe.sem_inc(turned, 2)
            pe.sem_inc(mod_summed, 2)
            pe.sem_inc(qn_turned, 2)
            pe.sem_inc(rqk_turned, 2)
            pe.sem_inc(hg_turned, 1)
            pe.sem_inc(cv_turned, 2)
            lo = Seen(pe, raw_read, 8)
            taken = Seen(pe, acc_taken)
            t_in, t_lo = Seen(pe, turn_in), Seen(pe, turn_lo)

            def gemm(turns, halves, group, width=CH, side=None, side_per=None, mods=0, drain=True):
                def body(t, first):
                    for x, (slot, kts) in enumerate(halves):
                        buf = x // group % 2
                        if x % group == 0:
                            pe.wait_ge(acc_taken, taken.next())
                        pe.wait_ge(raw_read, lo.next())
                        for u, kt in enumerate(kts):
                            for m in range(M):
                                hi_m, lo_m = (a[:, kt, m * P:(m + 1) * P] for a in (ht_hi, ht_lo))
                                start, stop = x % group == 0 and u == 0, x % group == group - 1 and u == len(kts) - 1
                                o = acc[:, buf, m, 0:width]
                                pe.matmul(o, hi_m, w_hi[:, slot, u, 0:width], start=start, stop=False)
                                pe.matmul(o, hi_m, w_lo[:, slot, u, 0:width], start=False, stop=False)
                                mm = pe.matmul(o, lo_m, w_hi[:, slot, u, 0:width], start=False, stop=stop)
                        mm.then_inc(split_used, 1)
                        if x // 8 < mods and x % 8 == 7:
                            pe.wait_ge(raw_read, lo.next(2))
                            mod_sums(x // 8 % 2)
                        elif x // 8 < mods and x % 2:
                            lo.skip(2)
                        if side:
                            side(t, x, first)
                if drain:
                    pe.wait_ge(acc_taken, taken.ahead(2))
                per = {taken: len(halves) // group, lo: len(halves) + 8 * mods}
                if mods:
                    per[m_taken] = mods
                if turns == 1:
                    body(0, True)
                elif side:
                    body(0, True)
                    with loop(pe, turns - 1, {**per, **side_per}) as i:
                        body(i + 1, False)
                else:
                    with loop(pe, turns, per) as i:
                        body(i, False)

            def chunk_halves(n):
                return [(h % SPL, (2 * h, 2 * h + 1)) for h in range(8)] * n

            def turn(n):
                with loop(pe, n, {t_in: 2, t_lo: 2}):
                    for b in range(2):
                        pe.wait_ge(turn_in, t_in.next())
                        pe.wait_ge(turn_lo, t_lo.next())
                        for m in range(M):
                            tr = pe.transpose(tps[:, b, m * P:(m + 1) * P], xn[:, b, m, :], ident)
                        tr.then_inc(turned, 1)

            pe.wait_ge(s_vec, 16 * 11)
            pe.wait_ge(s_const, 32)
            pe.transpose(tps[:, 0, 0:P], vcol[:, 0:P], ident)
            pe.transpose(tps[:, 0, P:P + NV2], xn[0:NV2, 0, 0, :], ident[0:NV2, 0:NV2]).then_inc(vec_turned, 1)

            m_taken = Seen(pe, mod_taken)

            def mod_sums(b):
                pe.wait_ge(mod_taken, m_taken.next())
                for j in range(4):
                    for e in range(2):
                        mm = pe.matmul(tps[:, 1, j:j + 1], macc[:, b, e, j * P:(j + 1) * P], ones,
                                       start=e == 0, stop=e == 1)
                mm.then_inc(mod_summed, 1)

            with loop(pe, 4, {lo: 16, m_taken: 2}):
                for b in range(2):
                    pe.wait_ge(raw_read, lo.next(8))
                    mod_sums(b)

            ktt, dots = Seen(pe, kt_ready), Seen(pe, dots_used, 0)
            qit = Seen(pe, qit_ready)
            qn, qtr, prb, ptr, yr = (Seen(pe, s) for s in (qn_ready, qt_ready, probs_ready, pt_ready, y_ready))
            rq, rs, rt = (Seen(pe, s) for s in (rqt_ready, rst_ready, ret_taken))
            rd = Seen(pe, rot_done, 2)
            kr, gt = Seen(pe, k_ready), Seen(pe, gate_rows)

            def index_queries(g):
                for b in range(2):
                    for m in range(M):
                        o = QI + (2 * g + b) * P
                        tr = pe.transpose(tps[:, 0, b * S + m * P:b * S + (m + 1) * P], proj[:, m, o:o + P], ident)
                tr.then_inc(qi_turned, 1)

            def index_dots(b):
                for e in range(2):
                    pe.wait_ge(dots_used, dots.next())
                    r = slice(64 * e, 64 * e + 64)
                    pe.matmul(sps[:, e, 0:P], qt[r, b, 0:P], kit[r, 0:P], start=True, stop=True)
                    pe.matmul(sps[:, e, P:P + S], qt[r, b, P:S], kit[r, :], start=True,
                              stop=True).then_inc(dots_ready, 1)

            def index_start(t, x, first):
                if x == 12:
                    pe.wait_ge(acc_taken, taken.ahead(1))
                    pe.wait_ge(k_ready, kr.next())
                    for m in range(M):
                        tr = pe.transpose(tps[:, 0, m * P:(m + 1) * P], xn[:, 0, m, :], ident)
                    tr.then_inc(k_turned, 1)
                if x == 14:
                    pe.wait_ge(kt_ready, ktt.next())
                    index_queries(0)

            def index(t, x, first):
                if x % 2 == 0:
                    k = x // 2
                    if k % 2 == 0:
                        pe.wait_ge(qit_ready, qit.next())
                    index_dots(k % 2)
                    if k % 2 and k < 7:
                        index_queries(k // 2 + 1)

            def sparse_keys(t, x, first):
                if x == 10:
                    pe.wait_ge(k_ready, kr.next())
                    for m in range(M):
                        tr = pe.transpose(tps[:, 0, S + m * P:S + (m + 1) * P], xn[:, 1, m, :], ident)
                    tr.then_inc(k_turned, 1)

            def heads(t, x, first):
                if first and x == 0:
                    pe.wait_ge(kt_ready, ktt.next())
                    pe.wait_ge(mod_taken, m_taken.ahead(1))
                for b in range(2):
                    if x % 8 == 0:
                        pe.wait_ge(qn_ready, qn.next())
                        for m in range(M):
                            tr = pe.transpose(tps[:, b, m * P:(m + 1) * P], xn[:, b, m, :], ident)
                        tr.then_inc(qn_turned, 1)
                    if x % 8 == 2:
                        pe.wait_ge(qt_ready, qtr.next())
                        pe.wait_ge(y_ready, yr.next())
                        pe.matmul(sps[:, b, 0:P], qt[:, b, 0:P], ktile[:, 0:P], start=True, stop=True)
                        pe.matmul(sps[:, b, P:P + S], qt[:, b, P:S], ktile, start=True,
                                  stop=True).then_inc(scores_ready, 1)
                    if x % 8 == 5:
                        pe.wait_ge(probs_ready, prb.next())
                        for n in range(3):
                            tr = pe.transpose(tps[:, b, n * P:(n + 1) * P], lg[:, b, n * P:(n + 1) * P], ident)
                        tr.then_inc(probs_turned, 1)
                    if x % 8 == 7:
                        pe.wait_ge(pt_ready, ptr.next())
                        v = [proj[:, m, VA:VA + HD] for m in range(M)]
                        pe.matmul(sps[:, b, 0:P], pt[:, b, 0:P], v[0], start=True, stop=True)
                        pe.matmul(sps[:, b, P:S], pt[:, b, P:S], v[0], start=True, stop=False)
                        pe.matmul(sps[:, b, P:S], pt[:, b, S:S + P], v[1], start=False,
                                  stop=True).then_inc(heads_out, 1)

            def retention():
                with loop(pe, 4, {rd: 2, rq: 2, rs: 2, rt: 2}) as i:
                    for b in range(2):
                        pe.wait_ge(rot_done, rd.next())
                        for w in range(2):
                            for m in range(M):
                                tr = pe.transpose(tps[:, b, w * S + m * P:w * S + (m + 1) * P], rqk[:, b, w, m, :], ident)
                        tr.then_inc(rqk_turned, 1)
                    for b in range(2):
                        pe.wait_ge(rqt_ready, rq.next())
                        pe.wait_ge(ret_taken, rt.next())
                        pe.matmul(sps[:, b, 0:S], rqt[:, b, 1, 0:P], rqt[:, b, 0, :], start=True, stop=True)
                        pe.matmul(sps[:, b, S:S + P], rqt[:, b, 1, P:S], rqt[:, b, 0, P:S], start=True,
                                  stop=True).then_inc(rs_ready, 1)
                    for b in range(2):
                        pe.wait_ge(rst_ready, rs.next())
                        v = [proj[:, m, ds(VB + (2 * i + b) * HD, HD)] for m in range(M)]
                        pe.matmul(sps[:, b, 0:P], rst[:, b, 0:P], v[0], start=True, stop=True)
                        pe.matmul(sps[:, b, P:S], rst[:, b, P:S], v[0], start=True, stop=False)
                        pe.matmul(sps[:, b, P:S], rst[:, b, S:S + P], v[1], start=False,
                                  stop=True).then_inc(ret_out, 1)

            for l in range(DEPTH):
                turn(KT // 2)
                pe.wait_ge(turn_lo, t_lo.ahead(2))
                gemm(1, chunk_halves(2), 8, mods=2)
                gemm(1, chunk_halves(2), 8, mods=2, side=index_start, drain=False)
                gemm(1, chunk_halves(2), 8, mods=2 * (l == 0), side=index, drain=False)
                gemm(1, chunk_halves(2), 8, side=sparse_keys, drain=False)
                gemm(2, chunk_halves(2), 8, side=heads, side_per={a: 4 for a in (qn, qtr, prb, ptr, yr)}, drain=False)
                gemm(1, chunk_halves(2), 8, mods=2 * (l == 0), drain=False)
                gemm(1, chunk_halves(1), 8, width=TAIL, drain=False)
                pe.wait_ge(mod_taken, m_taken.ahead(1))
                pe.wait_ge(acc_taken, taken.ahead(2))
                pe.transpose(tps[0:KT, 0, 0:P], modc[:, l * 48 + 32:l * 48 + 48], ident).then_inc(gate_turned, 1)
                pe.wait_ge(gate_rows, gt.next())
                retention()
                pe.wait_ge(ret_taken, rt.ahead(2))
                turn(KT // 2)
                pe.wait_ge(turn_lo, t_lo.ahead(2))
                gemm(2, chunk_halves(2), 8, mods=2 * (l == 0))

            hin, hx1, hx2, hat_r, haxr, hyr = (Seen(pe, s) for s in (hg_in, hg_x1, hg_x2, hg_at, hg_axr, hg_y))

            def hgrn_scores():
                pe.wait_ge(hg_x1, hx1.next())
                pe.wait_ge(hg_x2, hx2.next())
                pe.wait_ge(hg_y, hyr.next())
                for m in range(M):
                    c0 = m * P

                    def score(lv, s0, t0, h, o):
                        return pe.matmul(o, wk[:, lv, c0 + s0:c0 + s0 + h], wk[:, lv, c0 + t0:c0 + t0 + h],
                                         start=True, stop=True)
                    region = [sps[:, r // 2, (r % 2 * 2 + m) * P:(r % 2 * 2 + m + 1) * P] for r in range(4)]
                    for r in range(4):
                        score(3 + r, 0, 0, P, region[r])
                    for lv in range(3):
                        h = 64 >> lv
                        for s0 in range(0, P, 2 * h):
                            score(lv, s0, s0 + h, h, region[0][s0:s0 + h, s0 + h:s0 + 2 * h])
                    pe.matmul(tps[:, 1, c0:c0 + P], hk[:, c0:c0 + P], hq[:, c0:c0 + P], start=True, stop=True)
                pe.matmul(tps[:, 0, 0:P], wk[:, LEVELS, 0:P], wk[:, LEVELS, P:S], start=True,
                          stop=True).then_inc(hg_a, 1)

            def hgrn_out(g):
                pe.wait_ge(hg_at, hat_r.next())
                v = [proj[:, m, ds(2048 + g * HD, HD)] for m in range(M)]
                pe.matmul(tps[:, 1, S:S + P], hat[:, 0, :], v[0], start=True, stop=True)
                pe.matmul(tps[:, 1, S + P:2 * S], hat[:, 1, :], v[1], start=True, stop=False)
                pe.matmul(tps[:, 1, S + P:2 * S], hax, v[0], start=False, stop=True).then_inc(hg_o, 1)

            def hgrn(t, x, first):
                g, n = 2 * t + x // 8, x % 8
                begin = first and x < 8
                if n == 0 and not begin:
                    hgrn_scores()
                if n == 1:
                    if not begin:
                        pe.wait_ge(hg_axr, haxr.next())
                    pe.wait_ge(hg_in, hin.next())
                    for b in range(2):
                        for m in range(M):
                            tr = pe.transpose(tps[:, 0, b * S + m * P:b * S + (m + 1) * P], xn[:, b, m, :], ident)
                    tr.then_inc(hg_turned, 1)
                if n == 4 and not begin:
                    hgrn_out(g - 1)
            cin, cy = Seen(pe, cv_in), Seen(pe, cv_y)

            def conv():
                with loop(pe, 4, {cin: 2, cy: 2}):
                    for b in range(2):
                        pe.wait_ge(cv_in, cin.next())
                        pe.wait_ge(cv_y, cy.next())
                        for m in range(M):
                            pe.transpose(tps[:, b, m * P:(m + 1) * P], xn[:, b, m, :], ident)
                            tr = pe.transpose(tps[:, b, S + m * P:S + (m + 1) * P], lgc[:, b, m, :], ident)
                        tr.then_inc(cv_turned, 1)

            lgc = scr[:, 3584:4096].rearrange("p (b m d) -> p b m d", b=2, m=M)

            turn(KT // 2)
            pe.wait_ge(turn_lo, t_lo.ahead(2))
            for col, n in W2_PARTS:
                if col == GATES:
                    gemm(n // 2, chunk_halves(2), 8, side=hgrn,
                         side_per={s: 2 for s in (hin, hx1, hx2, hat_r, haxr, hyr)})
                    hgrn_scores()
                    pe.wait_ge(hg_axr, haxr.next())
                    hgrn_out(NH - 1)
                else:
                    gemm(n // 2, chunk_halves(2), 8)
            conv()
            pe.wait_ge(cv_y, cy.ahead(2))
            turn(NH // 2)
            pe.wait_ge(turn_lo, t_lo.ahead(2))
            pe.wait_ge(cv_lo, 2 + 8)
            gemm(4, chunk_halves(1), 4)
            turn(KT // 2)
            pe.wait_ge(turn_lo, t_lo.ahead(2))
            gemm(2, chunk_halves(2), 8)
            turn(KT // 2)
            pe.wait_ge(turn_lo, t_lo.ahead(2))
            gemm(2, chunk_halves(2), 8)
            turn(1)
            pe.wait_ge(turn_lo, t_lo.ahead(2))
            gemm(1, [(j, (0, 1)) for j in range(4)], 1)


        @block.scalar
        def _(act):
            act.sem_inc(acc_taken, 2)
            act.sem_inc(ret_taken, 2)
            act.dma_start(prow_i, positions.partition_broadcast(P)).then_inc(s_pos, 16)
            for m in range(M):
                act.dma_start(pcol_i[:, m:m + 1], positions[0].rearrange("(m p o) -> m p o", p=P, o=1)[m])\
                   .then_inc(s_pos, 16)
            act.dma_start(rbt, rel_bias.rearrange("b h -> (b h)").partition_broadcast(P)).then_inc(s_rb, 16)

            act.dma_start(xres[:, :, :], x_rows).then_inc(s_x, 16)
            landed = [Seen(act, s, 16 * 8) for s in raw_landed]
            slot_free = Seen(act, split_used)
            results = Seen(act, split_used, SPL)
            t_out = Seen(act, turned, 2)

            def link(ins):
                ins.then_inc(act_link, 1)
                act.wait_ge(act_link, linked.next())

            linked = Seen(act, act_link)

            def split(turns, nh, group, width=CH, halves=2, evac=None, side=None, side_per=None, mods=0,
                      prior=None, flush=True):
                gb = nh // group

                def take(g, b):
                    act.wait_ge(split_used, results.next(group))
                    evac(g, b)

                def body(t, first):
                    for x in range(nh):
                        j = x // halves % RAW
                        if x // 8 < mods:
                            j = 2 * j % RAW
                            if x % halves == 0:
                                landed[j + 1].skip(16)
                        if x % halves == 0:
                            act.wait_ge(raw_landed[j], landed[j].next(16))
                        act.wait_ge(split_used, slot_free.next())
                        act.activation(w_hi[:, x % SPL, :, 0:width],
                                       raw[:, j, 2 * (x % halves):2 * (x % halves) + 2, 0:width],
                                       ACT.Copy).then_inc(hi_ready, 1)
                        if x % group == min(3, group - 1):
                            g = x // group - 1
                            if evac and not (first and x < group):
                                take(t * gb + g, g % 2)
                            if first and x < group and prior:
                                at, n = prior
                                act.wait_ge(split_used, results.next(8))
                                at(n, n % 2)
                        if side:
                            side(t, x, first)

                body(0, True)
                if turns > 1:
                    per = {slot_free: nh, results: nh if evac else 0, **(side_per or {})}
                    per.update({s: 16 * nh // (RAW * halves) + 16 * mods for s in landed})
                    with loop(act, turns - 1, per) as i:
                        body(i + 1, False)
                if not evac:
                    results.skip(turns * nh)
                elif flush:
                    take(turns * gb - 1, (turns * gb - 1) % 2)

            def turn(n, kt0=0, scale=None, bias=None):
                with loop(act, n, {t_out: 2}) as i:
                    for b in range(2):
                        act.wait_ge(turned, t_out.next())
                        o = ht_hi[:, ds(kt0 + 2 * i + b, 1), :].rearrange("p a t -> p (a t)")
                        kw = {}
                        if scale is not None:
                            kw["scale"] = scale[:, ds(2 * i + b, 1)]
                        if bias is not None:
                            kw["bias"] = bias[:, ds(2 * i + b, 1)]
                        act.activation(o, tps[:, b, 0:S], ACT.Copy if bias is None else ACT.Identity,
                                       **kw).then_inc(turn_hi, 1)

            xr = Seen(act, x_ready, 2)

            def row_sums(n_x):
                for m in range(M):
                    act.activation(proj[:, m, 0:D], xres[:, m, :], ACT.Square, accum_out=st[:, m:m + 1])\
                       .then_inc(act_link, 1)
                act.wait_ge(act_link, linked.next(2))
                act.activation(st[:, 2:4], st[:, 0:2], ACT.Sqrt, bias=eps, scale=1.0 / D).then_inc(root_ready, 1)

            act.wait_ge(vec_turned, 1)
            link(act.activation(vcol[:, :], tps[:, 0, 0:P + NV2], ACT.Copy))
            act.activation(v2("c", 0, KT), v2("c", 0, KT), ACT.Silu).then_inc(vec_ready, 1)
            act.wait_ge(rot_ready, 1)
            act.activation(cs[:, 1, :, :], ang, ACT.Sin).then_inc(rot_done, 1)
            act.activation(cs[:, 0, :, :], ang_n, ACT.Sin, bias=kst[:, C_HPI:C_HPI + 1]).then_inc(rot_done, 1)
            act.wait_ge(lb_stats, 1)
            act.activation(lb_t[:, 1, :], lb_t[:, 0, :], ACT.Exp).then_inc(lb_exp, 1)

            oh, added = Seen(act, onehot_ready), Seen(act, bias_added)

            def bias_product(bucket_at, h):
                if h == 0:
                    act.wait_ge(onehot_ready, oh.next())
                if h % 4 == 0:
                    act.wait_ge(bias_added, added.next())
                r = act.activation(btmp[:, h // 4, h % 4, :], onehot[:, ds(bucket_at, 1), :].rearrange("p a k -> p (a k)"),
                                   ACT.Copy, scale=rbt[:, ds(bucket_at * NH + h, 1)])
                if h % 4 == 3:
                    r.then_inc(bias_product_ready, 1)

            act.wait_ge(s_rb, 16)
            with loop(act, B_FIRST, {oh: 1, added: 2}) as i:
                for h in range(NH):
                    bias_product(i, h)

            def bias_beside(first, n, x, steps):
                for k in range(x * n * NH // steps, (x + 1) * n * NH // steps):
                    bias_product(first + k // NH, k % NH)

            rr, ktn, qtn, dr = (Seen(act, s) for s in (sums_ready, k_turned, qi_turned, dots_ready))
            qnt, mx, pbt = Seen(act, qn_turned, 2), Seen(act, max_ready), Seen(act, probs_turned)
            rqt_t, rout, rvar = Seen(act, rqk_turned, 2), Seen(act, ret_out), Seen(act, ret_var)

            gtu, grd, gout = Seen(act, gate_turned), Seen(act, gate_rows), Seen(act, gate_out)

            def bias_done():
                act.wait_ge(bias_added, 2 + 2 * NB)

            def to_proj(width=CH, func=ACT.Copy, base=0, step=CH, wait=None):
                def evac(g, b):
                    if wait:
                        wait()
                    act.activation(proj[:, :, ds(base + g * step, width)], acc[:, b, :, 0:width], func)\
                       .then_inc(acc_taken, 1)
                return evac

            for l in range(DEPTH):
                if l == 0:
                    act.wait_ge(s_x, 16)
                else:
                    act.wait_ge(x_ready, xr.next(4))
                row_sums(l)
                turn(KT // 2, scale=acol[:, l * KT:(l + 1) * KT], bias=modc[:, l * 48:l * 48 + KT])
                first_acc = 2 + (NCH + 1 + 4) * l

                def bias_a1(t, x, first):
                    if l == 0:
                        bias_beside(B_FIRST, B_BESIDE, x, 32)

                def index_keys(t, x, first):
                    if l == 0:
                        bias_beside(B_FIRST, B_BESIDE, 16 + x, 32)
                    if x == 15:
                        act.wait_ge(k_turned, ktn.next())
                        act.activation(kit, tps[:, 0, 0:S], ACT.Copy).then_inc(kt_ready, 1)

                def index_relu():
                    for e in range(2):
                        act.wait_ge(dots_ready, dr.next())
                        act.activation(sps[:, e, 0:384], sps[:, e, 0:384], ACT.Relu).then_inc(relu_ready, 1)

                def index_queries():
                    act.wait_ge(qi_turned, qtn.next())
                    act.activation(qt, tps[:, 0, :].rearrange("p (b t) -> p b t", b=2), ACT.Copy).then_inc(qit_ready, 1)

                def index(t, x, first):
                    if l == 0:
                        bias_beside(B_FIRST + B_BESIDE, NB - B_FIRST - B_BESIDE, x, 16)
                    if x >= 4 and x % 2 == 0:
                        index_relu()
                    if x % 4 == 2:
                        index_queries()

                def norms(t, x, first):
                    if x == 0 or x == 2:
                        index_relu()
                    if x == 4 or x == 13:
                        a, z = (4, 9) if x == 4 else (0, 4)
                        act.wait_ge(sums_ready, rr.next())
                        act.activation(st[:, 24:42].rearrange("p (m h) -> p m h", m=M)[:, :, a:z],
                                       st[:, 4:22].rearrange("p (m h) -> p m h", m=M)[:, :, a:z],
                                       ACT.Sqrt, bias=eps, scale=1.0 / HD).then_inc(root_ready, 1)
                    if x == 8:
                        act.wait_ge(acc_taken, first_acc + 5)
                        act.activation(proj[:, :, GA:GA + DA], proj[:, :, GA:GA + DA], ACT.Silu).then_inc(ga_ready, 1)
                    if x == 14:
                        act.wait_ge(k_turned, ktn.next())
                        act.activation(ktile, tps[:, 0, S:2 * S], ACT.Copy, scale=v2("k_norm_gain", l)).then_inc(kt_ready, 1)

                def probs_columns():
                    for b in range(2):
                        act.wait_ge(probs_turned, pbt.next())
                        act.activation(pt[:, b, :], tps[:, b, 0:384], ACT.Copy).then_inc(pt_ready, 1)

                def heads(t, x, first):
                    n = x % 8
                    if n == 1 and not (first and x < 8):
                        probs_columns()
                    if n == 4:
                        for b in range(2):
                            act.wait_ge(qn_turned, qnt.next())
                            act.activation(qt[:, b, :], tps[:, b, 0:S], ACT.Copy, scale=v2("q_norm_gain", l))\
                               .then_inc(qt_ready, 1)
                    if n == 7:
                        for b in range(2):
                            act.wait_ge(max_ready, mx.next())
                            act.activation(lg[:, b, 0:P], lg[:, b, 0:P], ACT.Exp, bias=st[:, 44 + 2 * b:45 + 2 * b],
                                           accum_out=st[:, 48 + 2 * b:49 + 2 * b])
                            act.activation(lg[:, b, P:384], lg[:, b, P:384], ACT.Exp, bias=st[:, 45 + 2 * b:46 + 2 * b],
                                           accum_out=st[:, 49 + 2 * b:50 + 2 * b]).then_inc(probs_ready, 1)

                down6, down4, down2 = (to_proj(base=a * CH, step=-CH) for a in (6, 4, 2))
                ends = to_proj(base=0, step=7 * CH)
                up8, up12 = to_proj(base=8 * CH, wait=bias_done if l == 0 else None), to_proj(base=12 * CH)
                split(1, 16, 8, evac=down6, mods=2, side=bias_a1, flush=False)
                split(1, 16, 8, evac=down4, mods=2, side=index_keys, prior=(down6, 1), flush=False)
                split(1, 16, 8, evac=down2, mods=2 * (l == 0), side=index, prior=(down4, 1), flush=False)
                split(1, 16, 8, evac=ends, side=norms, prior=(down2, 1), flush=False)
                split(2, 16, 8, evac=up8, side=heads, side_per={qnt: 4, mx: 4, pbt: 4}, prior=(ends, 1), flush=False)
                probs_columns()
                split(1, 16, 8, evac=up12, mods=2 * (l == 0), prior=(up8, 3), flush=False)
                split(1, 8, 8, width=TAIL, evac=to_proj(TAIL, base=NCH * CH), prior=(up12, 1))
                act.wait_ge(gate_turned, gtu.next())
                act.activation(ttmp[0:KT, 0:P], tps[0:KT, 0, 0:P], ACT.Copy).then_inc(gate_rows, 1)
                act.wait_ge(gate_rows, grd.next())
                act.dma_start(gates[l * KT:(l + 1) * KT, :], ttmp[0:KT, 0:P]).then_inc(gate_out, 16)
                act.wait_ge(acc_taken, first_acc + NCH + 1)
                act.activation(proj[:, :, GB:GB + DA], proj[:, :, GB:GB + DA], ACT.Silu).then_inc(ga_ready, 1)
                with loop(act, 4, {rqt_t: 2, rout: 2, rvar: 1}) as i:
                    for b in range(2):
                        act.wait_ge(rqk_turned, rqt_t.next())
                        act.activation(rqt[:, b, :, :], tps[:, b, :].rearrange("p (w t) -> p w t", w=2), ACT.Copy)\
                           .then_inc(rqt_ready, 1)
                    for b in range(2):
                        act.wait_ge(ret_out, rout.next())
                        for m in range(M):
                            r = act.activation(ro[:, b, m, :], sps[:, b, m * P:(m + 1) * P], ACT.Copy,
                                               scale=kst[:, ds(C_QG + m * NH + 2 * i + b, 1)])
                        r.then_inc(ret_taken, 1)
                    act.wait_ge(ret_var, rvar.next())
                    act.activation(st[:, 0:4], mv[:, :, 1], ACT.Sqrt, bias=eps).then_inc(ret_root, 1)
                turn(NH // 2)
                turn(NH // 2, kt0=NH, scale=v2("ret_norm_gain", l * NH, NH))
                act.wait_ge(gate_out, gout.next(16))
                act.dma_start(proj[:, 0, 0:D], gates[l * KT:(l + 1) * KT, :].rearrange("k p -> (k p)")
                              .partition_broadcast(P)).then_inc(gate_bc, 16)
                split(2, 16, 8, mods=2 * (l == 0))

            act.wait_ge(x_ready, xr.next(4))
            row_sums(2)
            turn(KT // 2, scale=v2("norm_mix_g_2", 0, KT))
            hgt, hgf, hgd1, hgd2, hga, hgo = (Seen(act, s) for s in (hg_turned, hg_f, hg_d1, hg_d2, hg_a, hg_o))
            hgt.skip(1)

            def hgrn_cross():
                act.wait_ge(hg_a, hga.next())
                act.activation(hax, tps[:, 0, 0:P], ACT.Copy).then_inc(hg_axr, 1)

            def hgrn_squares():
                act.wait_ge(hg_o, hgo.next())
                for m in range(M):
                    act.activation(hy[:, m, :], tps[:, 1, S + m * P:S + (m + 1) * P], ACT.Square,
                                   scale=HD ** -0.5, accum_out=st[:, m:m + 1]).then_inc(hg_ss, 1)

            def hgrn(t, x, first):
                n = x % 8
                begin = first and x < 8
                if n == 2 and not begin:
                    hgrn_cross()
                if n == 3:
                    act.wait_ge(hg_turned, hgt.next())
                    act.activation(hs[:, 0:S], tps[:, 0, S:2 * S], ACT.Sigmoid)
                    act.activation(hk, tps[:, 0, S:2 * S], ACT.Sigmoid, scale=-1.0)
                    act.activation(hq, tps[:, 0, 0:S], ACT.Copy).then_inc(hg_sig, 1)
                if n == 4:
                    act.wait_ge(hg_f, hgf.next())
                    act.activation(hs, hs, ACT.Ln).then_inc(hg_ln, 1)
                if n == 5:
                    act.wait_ge(hg_d1, hgd1.next())
                    act.wait_ge(hg_d2, hgd2.next())
                    act.activation(wk, wk, ACT.Exp).then_inc(hg_w, 1)
                if n == 6 and not begin:
                    hgrn_squares()
            ngroups = 2 + DEPTH * (NCH + 1 + 4)
            for col, n in W2_PARTS:
                if col == CONV:
                    def evac(g, b):
                        act.activation(cg2[:, :, ds(g * CH, CH)], acc[:, b, :, :], ACT.Copy).then_inc(acc_taken, 1)
                else:
                    evac = to_proj(func=ACT.Sigmoid if col == GATES else ACT.Copy, base=4096 if col == GATES else 0)
                if col == GATES:
                    split(n // 2, 16, 8, evac=evac, side=hgrn, side_per={s: 2 for s in (hgt, hgf, hgd1, hgd2, hga, hgo)})
                    hgrn_cross()
                    hgrn_squares()
                else:
                    split(n // 2, 16, 8, evac=evac)
                ngroups += n
                if col == REC:
                    act.wait_ge(acc_taken, ngroups)
                    act.activation(proj[:, :, 0:1024], proj[:, :, 0:1024], ACT.Silu).then_inc(ga_ready, 1)
                    act.activation(proj[:, :, 3072:4096], proj[:, :, 3072:4096], ACT.Silu).then_inc(ga_ready, 1)
            act.wait_ge(acc_taken, ngroups)
            act.activation(proj[:, :, 2048:3072], proj[:, :, 2048:3072], ACT.Silu).then_inc(ga_ready, 1)
            cvt, cvc = Seen(act, cv_turned, 2), Seen(act, cv_y, 2)
            act.wait_ge(cv_hi, 1)
            with loop(act, 4, {cvt: 2, cvc: 2}) as i:
                for b in range(2):
                    act.wait_ge(cv_turned, cvt.next())
                    act.activation(ut[:, b, 2:258], tps[:, b, 0:S], ACT.Copy).then_inc(cv_u, 1)
                for b in range(2):
                    act.wait_ge(cv_y, cvc.next())
                    act.activation(ht_hi[:, ds(2 * i + b, 1), :].rearrange("p a t -> p (a t)"), ct[:, b, :],
                                   ACT.Copy).then_inc(cv_hi, 1)
            turn(NH // 2, kt0=NH, scale=v2("hg_norm_g_2", 0, NH))
            split(4, 8, 4)
            turn(KT // 2)
            act.dma_start(proj[:, :, 6144:6400], p_2[0, 0].rearrange("(m p) d -> p m d", p=P)).then_inc(p_landed, 16)
            act.dma_start(proj[:, 0, 4096:6144], final_norm_g_2.partition_broadcast(P)).then_inc(fin_g, 16)
            split(2, 16, 8)
            act.wait_ge(acc_taken, ngroups + 8 + 4)
            row_sums(3)
            turn(KT // 2, scale=v2("ple_norm_g_2", 0, KT))
            split(2, 16, 8, evac=to_proj(func=ACT.Sigmoid))
            turn(1)
            split(1, 4, 1, halves=1, evac=to_proj(base=2048))
            act.wait_ge(x_ready, 2 + 8 + 1)
            for m in range(M):
                act.activation(proj[:, m, 0:D], xres[:, m, :], ACT.Square, accum_out=st[:, m:m + 1]).then_inc(act_link, 1)
            act.wait_ge(act_link, linked.next(2))
            act.activation(st[:, 2:4], st[:, 0:2], ACT.Sqrt, bias=eps, scale=1.0 / D).then_inc(root_ready, 1)

        @block.vector
        def _(dve):
            dve.sem_inc(raw_read, 8)
            dve.sem_inc(mod_taken, 1)
            dve.sem_inc(turn_lo, 2)
            dve.sem_inc(dots_used, 2)
            dve.sem_inc(y_ready, 2)
            dve.sem_inc(logits_ready, 2)
            dve.sem_inc(yb_ready, 2)
            dve.sem_inc(hg_y, 1)
            dve.sem_inc(cv_y, 2)
            dve.sem_inc(cv_lo, 2)
            linked = Seen(dve, dve_link)

            def link(ins):
                ins.then_inc(dve_link, 1)
                dve.wait_ge(dve_link, linked.next())

            hi = Seen(dve, hi_ready)
            results = Seen(dve, split_used, SPL)
            t_hi, t_lo = Seen(dve, turn_hi), Seen(dve, turn_lo)

            def split(turns, nh, group, width=CH, halves=2, evac=None, side=None, side_per=None, mods=0,
                      prior_mod=False, keep_mod=False):
                gb = nh // group

                def take(g, b):
                    dve.wait_ge(split_used, results.next(group))
                    evac(g, b)

                def body(t, first):
                    for x in range(nh):
                        j = x // halves % RAW
                        if x // 8 < mods:
                            j = 2 * j % RAW
                        dve.wait_ge(hi_ready, hi.next())
                        dve.tensor_tensor(w_lo[:, x % SPL, :, 0:width],
                                          raw[:, j, 2 * (x % halves):2 * (x % halves) + 2, 0:width],
                                          w_hi[:, x % SPL, :, 0:width].bitcast(F32), ALU.subtract).then_inc(raw_read, 1)
                        own.skip(1)
                        if x % halves == 0:
                            m_land[j].skip(16)
                        if mods and x % 8 == 3 and not (first and x < 8):
                            mod_take(t * mods + x // 8 - 1 + mod_at[0])
                        if prior_mod and first and x == 3:
                            mod_take(mod_at[0] - 1)
                        if x // 8 < mods and x % 2:
                            mod_piece(x // 8 % 2, x % 8 // 2, j + 1)
                        if evac and x % group == min(3, group - 1) and not (first and x < group):
                            g = x // group - 1
                            take(t * gb + g, g % 2)
                        if side:
                            side(t, x, first)

                body(0, True)
                if turns > 1:
                    per = {hi: nh, results: nh if evac else 0, **(side_per or {})}
                    if evac in owners:
                        per.update(owners[evac])
                    per.update({s: 16 * nh // (RAW * halves) + 16 * mods for s in m_land})
                    per[own] = nh + 8 * mods
                    if mods:
                        per.update({m_free: mods, m_sum: mods})
                    with loop(dve, turns - 1, per) as i:
                        body(i + 1, False)
                if evac:
                    take(turns * gb - 1, (turns * gb - 1) % 2)
                else:
                    results.skip(turns * nh)
                mod_at[0] += turns * mods
                if mods and not keep_mod:
                    mod_take(mod_at[0] - 1)

            owners = {}

            def turn(n, kt0=0, scale=None, bias=None):
                per = {t_hi: 2}
                if bias is not None:
                    per.update({linked: 2, t_lo: 2})
                else:
                    t_lo.skip(2 * n)
                with loop(dve, n, per) as i:
                    for b in range(2):
                        dve.wait_ge(turn_hi, t_hi.next())
                        at = ds(kt0 + 2 * i + b, 1)
                        h = ht_hi[:, at, :].rearrange("p a t -> p (a t)").bitcast(F32)
                        o = ht_lo[:, at, :].rearrange("p a t -> p (a t)")
                        if bias is not None:
                            dve.wait_ge(turn_lo, t_lo.next())
                            link(dve.tensor_scalar(ttmp2[:, b, :], tps[:, b, 0:S], scale[:, ds(2 * i + b, 1)],
                                                   bias[:, ds(2 * i + b, 1)], ALU.mult, ALU.add))
                            r = dve.tensor_tensor(o, ttmp2[:, b, :], h, ALU.subtract)
                        elif scale is not None:
                            r = dve.scalar_tensor_tensor(o, tps[:, b, 0:S], scale[:, ds(2 * i + b, 1)], h,
                                                         ALU.mult, ALU.subtract)
                        else:
                            r = dve.tensor_tensor(o, tps[:, b, 0:S], h, ALU.subtract)
                        r.then_inc(turn_lo, 1)

            dve.wait_ge(s_pos, 48)
            dve.wait_ge(s_const, 32)
            dve.tensor_copy(lvm[:, :, :], scr[:, 5376:6016].rearrange("p (n t) -> p n t", t=P))
            dve.tensor_copy(prow, prow_i)
            link(dve.tensor_copy(pcol, pcol_i))
            for m in range(M):
                r = dve.tensor_scalar(ang[:, m, :], kst[:, C_INV:C_INV + HD // 2], pcol[:, m:m + 1], None, ALU.mult)
            link(r)
            big = 1.5 * 2 ** 23
            link(dve.tensor_scalar(ang_n, ang, 1.0 / (2 * math.pi), big, ALU.mult, ALU.add))
            link(dve.tensor_scalar(ang_n, ang_n, -big, None, ALU.add))
            c1 = 6.28125
            c2 = float(np.float32(2 * math.pi - c1).view(np.uint32) & np.uint32(0xfffff000))
            c2 = float(np.uint32(np.float32(2 * math.pi - c1).view(np.uint32) & np.uint32(0xfffff000)).view(np.float32))
            c3 = 2 * math.pi - c1 - c2
            for cc in (c1, c2, c3):
                link(dve.scalar_tensor_tensor(ang, ang_n, -cc, ang, ALU.mult, ALU.add))
            link(dve.tensor_scalar(ang, ang, 3.1415925, -3.1415925, ALU.min, ALU.max))
            link(dve.tensor_scalar(ang_n, ang, -1.0, None, ALU.mult))
            dve.tensor_tensor(ang_n, ang, ang_n, ALU.min).then_inc(rot_ready, 1)
            for m in range(M):
                o = slice(0, P) if m == 0 else slice(P, 384)
                r = dve.tensor_scalar(rel[:, o], prow[:, 0:(m + 1) * P], pcol[:, m:m + 1], -1.0, ALU.subtract, ALU.mult)
            link(r)
            link(dve.tensor_scalar(bucket, rel, 0.0, float(EXACT), ALU.max, ALU.min))
            for j in range(1, NB - EXACT):
                thr = math.ceil(EXACT * (MAXD / EXACT) ** (j / (NB - EXACT)))
                link(dve.scalar_tensor_tensor(bucket, rel, float(thr), bucket, ALU.is_ge, ALU.add))
            dve.wait_ge(vec_ready, 1)
            lp = v2("lb_param_2", 0, NH)
            dve.tensor_tensor(lb_t[:, 0, :], lp, lp, ALU.subtract).then_inc(lb_stats, 1)
            dve.wait_ge(lb_exp, 1)
            link(dve.reciprocal(lb_t[:, 0, :], lb_t[:, 1, :]))
            link(dve.tensor_tensor(lb_t[:, 0, :], lb_t[:, 0, :], lb_t[:, 1, :], ALU.mult))
            link(dve.tensor_tensor(lb_t[:, 1, :], lb_t[:, 0, :], lb_t[:, 0, :], ALU.subtract))
            link(dve.tensor_scalar(lb_t[:, 1, :], lb_t[:, 1, :], 0.0, 1.0 - 1e-6, ALU.max, ALU.min))
            dve.tensor_scalar(lbc[:, 0:NH], lb_t[:, 1, :], -1.0, 1.0, ALU.mult, ALU.add)
            link(dve.tensor_scalar(lbc[:, NH:2 * NH], lb_t[:, 1, :], 1e-30, None, ALU.max))

            m_free, m_sum = Seen(dve, mod_summed), Seen(dve, mod_summed, 2)
            m_land = [Seen(dve, s) for s in raw_landed]
            own = Seen(dve, raw_read, 8)
            mod_at = [8]

            def mod_piece(b, q, slot):
                if q == 0:
                    dve.wait_ge(mod_summed, m_free.next())
                dve.wait_ge(raw_landed[slot], m_land[slot].next(16))
                for u in range(2):
                    if q or u:
                        dve.wait_ge(raw_read, own.ahead(0))
                    for e in range(2):
                        kt = 4 * q + 2 * u + e
                        if q == 0 and u == 0:
                            r = dve.tensor_scalar(macc[:, b, e, :], raw[:, slot, 2 * u + e, :], v2("c", kt), None, ALU.mult)
                        else:
                            r = dve.scalar_tensor_tensor(macc[:, b, e, :], raw[:, slot, 2 * u + e, :], v2("c", kt),
                                                         macc[:, b, e, :], ALU.mult, ALU.add)
                    r.then_inc(raw_read, 1)
                    own.skip(1)

            def mod_take(cm):
                dve.wait_ge(mod_summed, m_sum.next())
                dve.tensor_tensor(modc[:, ds(cm * 4, 4)], tps[:, 1, 0:4], vcol[:, ds(V1["b_mod"][0] + cm * 4, 4)],
                                  ALU.add).then_inc(mod_taken, 1)

            def onehots(first):
                for k in range(4):
                    dve.tensor_tensor(onehot[:, ds(first + k, 1), :].rearrange("p a k -> p (a k)"), bucket,
                                      kst[:, ds(C_B + first + k, 1)].broadcast_to([P, 384]), ALU.is_equal)\
                       .then_inc(onehot_ready, 1)

            def mod_turn(i, first):
                for b in range(2):
                    for q in range(4):
                        mod_piece(b, q, q)
                        if q == 1 and not (first and b == 0):
                            mod_take(2 * i + b - 1)
                    onehots(i * 8 + 4 * b)

            mod_turn(0, True)
            with loop(dve, 3, {m_free: 2, m_sum: 2, own: 16, **{s: 32 for s in m_land}}) as i:
                mod_turn(i + 1, False)
            mod_take(7)

            root, accs = Seen(dve, root_ready), Seen(dve, acc_taken, 2)
            rl, sc, lbr, prb, ho = (Seen(dve, s) for s in (relu_ready, scores_ready, lb_ready, probs_ready, heads_out))
            du, rsr, rtk, rrt = Seen(dve, dots_used, 1), Seen(dve, rs_ready), Seen(dve, ret_taken, 2), Seen(dve, ret_root)
            gar, xfree, mbr = Seen(dve, ga_ready), Seen(dve, x_ready), Seen(dve, idx_causal)
            mbd = Seen(dve, mb_ready)

            def row_scale():
                dve.wait_ge(root_ready, root.next())
                dve.reciprocal(st[:, 22:24], st[:, 2:4]).then_inc(rstd_ready, 1)

            mtk = Seen(dve, mod_taken, 1)
            for l in range(DEPTH):
                dve.wait_ge(mod_taken, mtk.next(8 if l == 0 else 12))
                link(dve.scalar_tensor_tensor(acol[:, l * KT:(l + 1) * KT], modc[:, l * 48 + KT:l * 48 + 2 * KT], 1.0,
                                              v1("norm_gain", l * KT, KT), ALU.add, ALU.mult))
                row_scale()
                turn(KT // 2, scale=acol[:, l * KT:(l + 1) * KT], bias=modc[:, l * 48:l * 48 + KT])

                def index_sum(k):
                    for e in range(2):
                        dve.wait_ge(relu_ready, rl.next())
                        dve.wait_ge(dots_used, du.next())
                        for m in range(M):
                            o = slice(0, P) if m == 0 else slice(P, 384)
                            w = WI + 2 * k + e
                            r = dve.scalar_tensor_tensor(idx[:, o], sps[:, e, o], proj[:, m, w:w + 1], idx[:, o],
                                                         ALU.mult, ALU.add)
                        r.then_inc(dots_used, 1)

                def index(t, x, first):
                    if x == 4:
                        dve.wait_ge(acc_taken, accs.next(3))
                    if x >= 4 and x % 2 == 0:
                        index_sum(x // 2 - 2)

                def squares(a, z):
                    for m in range(M):
                        w = sq[:, 0:(z - a) * HD]
                        h = proj[:, m, a * HD:z * HD]
                        link(dve.tensor_tensor(w, h, h, ALU.mult))
                        r = dve.tensor_reduce(st[:, 4 + 9 * m + a:4 + 9 * m + z], w.rearrange("p (h d) -> p h d", d=HD),
                                              AX, ALU.add)
                        if m == 0:
                            link(r)
                    r.then_inc(sums_ready, 1)

                def scales(a, z):
                    dve.wait_ge(root_ready, root.next())
                    dve.reciprocal(st[:, 4:22].rearrange("p (m h) -> p m h", m=M)[:, :, a:z],
                                   st[:, 24:42].rearrange("p (m h) -> p m h", m=M)[:, :, a:z]).then_inc(rstd_ready, 1)

                tiles = [idx[:, 0:P], idx[:, P:384]]

                def norms_and_selection(t, x, first):
                    if x == 0 or x == 2:
                        index_sum(6 + x // 2)
                    if x == 2:
                        dve.wait_ge(dots_used, du.ahead(1))
                        dve.sem_inc(idx_ready, 1)
                    if x == 4:
                        dve.wait_ge(acc_taken, accs.next(3))
                        squares(4, 9)
                    if x == 5:
                        scales(4, 9)
                        dve.wait_ge(idx_causal, mbr.next(2))
                    if 5 <= x < 5 + TOPK // 8:
                        for m in range(M):
                            r = dve.max(tmp8[:, m, :], tiles[m])
                        link(r)
                        for m in range(M):
                            r = dve.match_replace(tiles[m], tmp8[:, m, :], tiles[m], -3.4e38)
                        link(r)
                    if x == 4 + TOPK // 8:
                        dve.tensor_scalar(mb, idx, -3.2e38, -1e30, ALU.is_ge, ALU.mult).then_inc(sel_ready, 1)
                    if x == 13:
                        dve.wait_ge(acc_taken, accs.next())
                        squares(0, 4)
                    if x == 14:
                        scales(0, 4)

                def outputs(col):
                    for b in range(2):
                        dve.wait_ge(probs_ready, prb.next())
                        link(dve.reciprocal(st[:, 52 + 2 * b:54 + 2 * b], st[:, 48 + 2 * b:50 + 2 * b]))
                        dve.wait_ge(heads_out, ho.next())
                        for m in range(M):
                            g = proj[:, m, ds(col + b * HD, HD)]
                            r = dve.scalar_tensor_tensor(g, sps[:, b, m * P:(m + 1) * P], st[:, 52 + 2 * b + m:53 + 2 * b + m],
                                                         g, ALU.mult, ALU.mult)
                        r.then_inc(y_ready, 1)

                def heads(t, x, first):
                    if x % 8 == 3 and not (first and x < 8):
                        outputs(t * (-4 * HD) + (GA + (4 if x > 8 else 10) * HD))
                    if x % 8 == 6:
                        for b in range(2):
                            dve.wait_ge(scores_ready, sc.next())
                            dve.wait_ge(lb_ready, lbr.next())
                            link(dve.scalar_tensor_tensor(lg[:, b, :], sps[:, b, 0:384], SCALE, lb_s[:, b, :],
                                                          ALU.mult, ALU.add))
                            dve.tensor_reduce(st[:, 44 + 2 * b:45 + 2 * b], lg[:, b, 0:P], AX, ALU.max, negate=True)\
                               .then_inc(logits_ready, 1)
                            dve.tensor_reduce(st[:, 45 + 2 * b:46 + 2 * b], lg[:, b, P:384], AX, ALU.max, negate=True)\
                               .then_inc(max_ready, 1)

                mods = 2 * (l == 0)
                split(1, 16, 8, mods=2, keep_mod=True)
                split(1, 16, 8, mods=2, prior_mod=True, keep_mod=True)
                link(dve.memset(idx, 0.0))
                split(1, 16, 8, mods=mods, side=index, prior_mod=True, keep_mod=True)
                split(1, 16, 8, side=norms_and_selection, prior_mod=l == 0)
                dve.wait_ge(ga_ready, gar.next())
                split(2, 16, 8, side=heads, side_per={sc: 4, lbr: 4, prb: 4, ho: 4, linked: 8})
                outputs(GA + 2 * HD)
                split(1, 16, 8, mods=mods, keep_mod=True)
                split(1, 8, 8, width=TAIL, prior_mod=l == 0)
                dve.wait_ge(acc_taken, accs.next(8))
                dve.wait_ge(ga_ready, gar.next())
                with loop(dve, 4, {rsr: 2, rtk: 2, rrt: 1, linked: 3}) as i:
                    for b in range(2):
                        dve.wait_ge(rs_ready, rsr.next())
                        dve.scalar_tensor_tensor(rst[:, b, 0:S], sps[:, b, 0:S], kst[:, ds(C_KG + 2 * i + b, 1)], maskt,
                                                 ALU.mult, ALU.mult)
                        dve.scalar_tensor_tensor(rst[:, b, S:S + P], sps[:, b, S:S + P], kst[:, ds(C_KG + NH + 2 * i + b, 1)],
                                                 maskt[:, 0:P], ALU.mult, ALU.mult).then_inc(rst_ready, 1)
                    for b in range(2):
                        dve.wait_ge(ret_taken, rtk.next())
                        for m in range(M):
                            r = dve.bn_stats(bns[:, 2 * b + m, :], ro[:, b, m, :])
                    link(r)
                    dve.sem_inc(dve_passed, 1)
                    for n in range(4):
                        r = dve.bn_aggr(mv[:, n, :], bns[:, n, :])
                    r.then_inc(ret_var, 1)
                    dve.wait_ge(ret_root, rrt.next())
                    link(dve.reciprocal(st[:, 4:8], st[:, 0:4]))
                    for n in range(4):
                        r = dve.tensor_scalar(ro[:, n // 2, n % 2, :], ro[:, n // 2, n % 2, :], mv[:, n, 0:1],
                                              st[:, 4 + n:5 + n], ALU.subtract, ALU.mult)
                    link(r)
                    for b in range(2):
                        g = proj[:, :, ds(GB + (2 * i + b) * HD, HD)]
                        r = dve.tensor_tensor(g, g, ro[:, b, :, :], ALU.mult)
                        r.then_inc(yb_ready, 1)
                turn(NH // 2)
                turn(NH // 2, kt0=NH, scale=v2("ret_norm_gain", l * NH, NH))
                dve.wait_ge(gate_bc, 16 * (l + 1))

                def gated(g, b):
                    dve.wait_ge(x_ready, xfree.next())
                    dve.tensor_tensor(proj[:, 1, b * 1024:(b + 1) * 1024].rearrange("p (m n) -> p m n", m=M),
                                      acc[:, b, :, :],
                                      proj[:, 0, ds(g * CH, CH)].unsqueeze(1).broadcast_to([P, M, CH]),
                                      ALU.mult).then_inc(acc_taken, 1)
                owners[gated] = {xfree: 2}
                split(2, 16, 8, evac=gated, mods=2 * (l == 0))
                accs.skip(4)

            row_scale()
            turn(KT // 2, scale=v2("norm_mix_g_2", 0, KT))
            hsg, hln, hwr, har, hrt = (Seen(dve, s) for s in (hg_sig, hg_ln, hg_w, hg_a, hg_rstd))
            bsc = hb.rearrange("p (m t) -> p m t", m=M)
            lfs = hs[:, 0:S].rearrange("p (m t) -> p m t", m=M)

            def hgrn_merge():
                dve.wait_ge(hg_a, har.next())
                for r in range(5):
                    dve.sem_inc(dve_passed, 1)
                    src = (sps[:, r // 2, r % 2 * S:(r % 2 + 1) * S] if r < 4 else tps[:, 1, 0:S])\
                        .rearrange("p (m t) -> p m t", m=M)
                    o = dve.copy_predicated(hat, lvm[:, r, :].unsqueeze(1).broadcast_to([P, M, P]), src)
                    if r < 4:
                        link(o)
                o.then_inc(hg_at, 1)

            def hgrn_y(g):
                dve.wait_ge(hg_rstd, hrt.next())
                for m in range(M):
                    og = proj[:, m, ds(3072 + g * HD, HD)]
                    r = dve.scalar_tensor_tensor(og, tps[:, 1, S + m * P:S + (m + 1) * P], st[:, 4 + m:5 + m], og,
                                                 ALU.mult, ALU.mult)
                r.then_inc(hg_y, 1)

            def hgrn(t, x, first):
                g, n = 2 * t + x // 8, x % 8
                begin = first and x < 8
                if n == 2 and not begin:
                    hgrn_merge()
                if n == 3:
                    dve.wait_ge(hg_sig, hsg.next())
                    one_lb, floor = lbc[:, ds(g, 1)], lbc[:, ds(NH + g, 1)]
                    dve.tensor_scalar(hk, hk, one_lb, None, ALU.mult)
                    link(dve.tensor_scalar(hb, hs[:, 0:S], one_lb, floor, ALU.mult, ALU.add))
                    dve.tensor_scalar(hs[:, 0:S], hb, 2.0 ** -60, None, ALU.max)
                    dve.tensor_scalar(hs[:, S:2 * S], hb, 2.0 ** -60, 2.0 ** 60, ALU.min, ALU.mult).then_inc(hg_f, 1)
                if n == 4:
                    dve.wait_ge(hg_ln, hln.next())
                    link(dve.tensor_tensor(hs[:, 0:S], hs[:, 0:S], hs[:, S:2 * S], ALU.add))
                    for m in range(M):
                        r = dve.tensor_tensor_scan(bsc[:, m, :], ones128, lfs[:, m, :], 0.0, ALU.mult, ALU.add)
                    r.then_inc(hg_b, 1)
                    dve.wait_ge(hg_b, hbd.next())
                    for _, first_half, second, mid in level_views(wk, hb):
                        dve.tensor_tensor(second[0], second[1], mid, ALU.subtract)
                    dve.tensor_copy(wk[:, LEVELS, P:S], hb[:, P:S]).then_inc(hg_d2, 1)
                if n == 6:
                    dve.wait_ge(hg_w, hwr.next())
                    for _, first_half, second, mid in level_views(wk, hq):
                        dve.tensor_tensor(second[0], second[0], second[1], ALU.mult)
                    dve.tensor_tensor(wk[:, LEVELS, P:S], wk[:, LEVELS, P:S], hq[:, P:S], ALU.mult).then_inc(hg_x2, 1)
                if n == 7 and not begin:
                    hgrn_y(g - 1)

            hbd = Seen(dve, hg_b)
            for col, n in W2_PARTS:
                accs.skip(n)
                if col == GATES:
                    dve.wait_ge(ga_ready, gar.next(2))
                    link(dve.memset(hat, 0.0))
                    split(n // 2, 16, 8, side=hgrn,
                          side_per={hsg: 2, hln: 2, hwr: 2, har: 2, hrt: 2, hbd: 2, linked: 12})
                    hgrn_merge()
                    hgrn_y(NH - 1)
                else:
                    split(n // 2, 16, 8)
            dve.memset(ut, 0.0).then_inc(cv_hi, 1)
            cuu, chh, cll = Seen(dve, cv_u), Seen(dve, cv_hi, 1), Seen(dve, cv_lo)
            cw = v2("conv_w_2", 0, 24)
            with loop(dve, 4, {cuu: 2, chh: 2, cll: 2, linked: 6}) as i:
                for b in range(2):
                    dve.wait_ge(cv_lo, cll.next())
                    dve.wait_ge(cv_u, cuu.next())
                    k = 2 * i + b
                    link(dve.tensor_scalar(ct[:, b, :], ut[:, b, 2:258], cw[:, ds(16 + k, 1)], None, ALU.mult))
                    link(dve.scalar_tensor_tensor(ct[:, b, :], ut[:, b, 1:257], cw[:, ds(8 + k, 1)], ct[:, b, :],
                                                  ALU.mult, ALU.add))
                    link(dve.scalar_tensor_tensor(ct[:, b, :], ut[:, b, 0:256], cw[:, ds(k, 1)], ct[:, b, :],
                                                  ALU.mult, ALU.add))
                    dve.tensor_tensor(ct[:, b, :], ct[:, b, :], tps[:, b, S:2 * S], ALU.mult).then_inc(cv_y, 1)
                for b in range(2):
                    dve.wait_ge(cv_hi, chh.next())
                    at = ds(2 * i + b, 1)
                    dve.tensor_tensor(ht_lo[:, at, :].rearrange("p a t -> p (a t)"), ct[:, b, :],
                                      ht_hi[:, at, :].rearrange("p a t -> p (a t)").bitcast(F32),
                                      ALU.subtract).then_inc(cv_lo, 1)
            turn(NH // 2, kt0=NH, scale=v2("hg_norm_g_2", 0, NH))

            def merge(g, b):
                gt = proj[:, :, ds(4096 + b * 2048 + (g - b) * (CH // 2), CH)]
                dve.tensor_tensor(gt, acc[:, b, :, :], gt, ALU.mult).then_inc(acc_taken, 1)
            split(4, 8, 4, evac=merge)
            turn(KT // 2)

            def add_x(g, b):
                xs = xres[:, :, ds(g * CH, CH)]
                dve.tensor_tensor(xs, acc[:, b, :, :], xs, ALU.add).then_inc(acc_taken, 1)
            split(2, 16, 8, evac=add_x)
            row_scale()
            turn(KT // 2, scale=v2("ple_norm_g_2", 0, KT))
            accs.skip(8 + 4)
            split(2, 16, 8)
            turn(1)
            split(1, 4, 1, halves=1)
            dve.wait_ge(acc_taken, accs.next(8))
            link(dve.tensor_tensor(proj[:, :, 0:D], proj[:, :, 0:D], proj[:, :, D:2 * D], ALU.mult))
            dve.tensor_tensor(xres[:, :, :], xres[:, :, :], proj[:, :, 0:D], ALU.add).then_inc(x_ready, 1)
            dve.wait_ge(root_ready, root.next())
            link(dve.reciprocal(st[:, 22:24], st[:, 2:4]))
            dve.wait_ge(fin_g, 16)
            for m in range(M):
                dve.scalar_tensor_tensor(proj[:, m, 0:D], xres[:, m, :], st[:, 22 + m:23 + m], proj[:, 0, 4096:6144],
                                         ALU.mult, ALU.mult).then_inc(fin_ready, 1)

        @block.gpsimd
        def _(pool):
            pool.sem_inc(x_ready, 2)
            pool.sem_inc(bias_added, 2)
            linked = Seen(pool, pool_link)

            def link(ins):
                ins.then_inc(pool_link, 1)
                pool.wait_ge(pool_link, linked.next())

            prod, badd = Seen(pool, bias_product_ready), Seen(pool, bias_added)

            def bias_sum(n):
                with loop(pool, n, {prod: 2, badd: 2}):
                    for b in range(2):
                        pool.wait_ge(bias_product_ready, prod.next())
                        pool.wait_ge(bias_added, badd.next())
                        o = bias[:, 4 * b:4 * b + 4, :]
                        pool.tensor_tensor(o, o, btmp[:, b, :, :], ALU.add).then_inc(bias_added, 1)

            link(pool.memset(scr[:, 0:3072], 0.0))
            bias_sum(B_FIRST)

            xfree = Seen(pool, turned)
            rstd, accs = Seen(pool, rstd_ready), Seen(pool, acc_taken, 2)
            qnf, lbf, rqf = (Seen(pool, s) for s in (qn_turned, logits_ready, rqk_turned))
            idr, slr, yr, ybr = Seen(pool, idx_ready), Seen(pool, sel_ready), Seen(pool, y_ready, 2), Seen(pool, yb_ready, 2)
            rdone = Seen(pool, rot_done, 2)
            mbr = Seen(pool, mb_ready)
            ktn = Seen(pool, k_turned)

            def turn(n, make):
                with loop(pool, n, {xfree: 2}) as i:
                    for b in range(2):
                        pool.wait_ge(turned, xfree.next())
                        make(xn[:, b, :, :], 2 * i + b).then_inc(turn_in, 1)

            def x_tile(o, k):
                return pool.tensor_tensor(o, xres[:, :, ds(k * P, P)], bc(st[:, 22:24], P), ALU.mult)

            def proj_tile(col):
                return lambda o, k: pool.tensor_copy(o, proj[:, :, ds(col + k * P, P)])

            def causal(t, fill, done):
                for m in range(M):
                    o = t[:, 0:P] if m == 0 else t[:, P:384]
                    pool.affine_select(out=o, in_=o, compare_op=ALU.is_ge, fill=fill, base=m * P,
                                       pattern=[[-1, (m + 1) * P]], channel_multiplier=1).then_inc(done, 1)

            xs = Seen(pool, acc_taken, 2)
            for l in range(DEPTH):
                pool.wait_ge(rstd_ready, rstd.next())
                turn(KT // 2, x_tile)
                if l == 0:
                    bias_sum(B_BESIDE - 2)
                pool.wait_ge(acc_taken, accs.next(3))
                pool.wait_ge(turned, xfree.ahead(2))
                for e in range(2):
                    r = pool.tensor_copy(xn[:, 0, :, 64 * e:64 * e + 64], proj[:, :, KI:KI + ID])
                r.then_inc(k_ready, 1)
                if l == 0:
                    bias_sum(NB - B_FIRST - B_BESIDE + 2)
                pool.wait_ge(idx_ready, idr.next())
                causal(idx, -3e38, idx_causal)
                pool.wait_ge(acc_taken, accs.next(3))
                pool.wait_ge(rstd_ready, rstd.next())
                rs9 = st[:, 4:22].rearrange("p (m h) -> p m h", m=M)
                pool.tensor_tensor(xn[:, 1, :, :], proj[:, :, KA:KA + HD], bc(rs9[:, :, 8], HD), ALU.mult)\
                    .then_inc(k_ready, 1)
                pool.wait_ge(sel_ready, slr.next())
                causal(mb, -1e30, mb_ready)
                pool.wait_ge(acc_taken, accs.next())
                pool.wait_ge(rstd_ready, rstd.next())
                pool.wait_ge(mb_ready, mbr.next(2))
                pool.wait_ge(k_turned, ktn.next(2))
                with loop(pool, 2, {qnf: 4, lbf: 4}) as i:
                    for n in range(4):
                        h, b = i * -4 + (4 + n), n % 2
                        pool.wait_ge(qn_turned, qnf.next())
                        pool.tensor_tensor(xn[:, b, :, :], proj[:, :, ds(i * (-4 * HD) + (QA + (4 + n) * HD), HD)],
                                           rs9[:, :, ds(h, 1)].broadcast_to([P, M, HD]), ALU.mult).then_inc(qn_ready, 1)
                        pool.wait_ge(logits_ready, lbf.next())
                        pool.tensor_tensor(lb_s[:, b, :], bias[:, ds(h, 1), :].rearrange("p a k -> p (a k)"), mb,
                                           ALU.add).then_inc(lb_ready, 1)
                pool.wait_ge(y_ready, yr.next(8))
                if l == 0:
                    pool.wait_ge(mod_taken, 1 + 16)
                pool.wait_ge(acc_taken, accs.next(8))
                t4 = [rtmp[:, a, :, :].rearrange("p (w m) d -> p w m d", w=2) for a in range(4)]
                qk = proj[:, :, QB:QB + 2 * DA].rearrange("p m (w n) -> p w m n", w=2)
                cos, sin = (cs[:, a, :, :].unsqueeze(1).broadcast_to([P, 2, M, HD // 2]) for a in range(2))
                half = HD // 2
                with loop(pool, 4, {rqf: 2, linked: 2, rdone: 2}) as i:
                    for b in range(2):
                        h = 2 * i + b
                        pool.wait_ge(rqk_turned, rqf.next())
                        x1, x2 = qk[:, :, :, ds(h * HD, half)], qk[:, :, :, ds(h * HD + half, half)]
                        pool.tensor_tensor(t4[0], x1, cos, ALU.mult)
                        pool.tensor_tensor(t4[1], x2, sin, ALU.mult)
                        pool.tensor_tensor(t4[2], x1, sin, ALU.mult)
                        link(pool.tensor_tensor(t4[3], x2, cos, ALU.mult))
                        pool.tensor_tensor(rqk[:, b, :, :, 0:half], t4[0], t4[1], ALU.subtract)
                        pool.tensor_tensor(rqk[:, b, :, :, half:HD], t4[2], t4[3], ALU.add).then_inc(rot_done, 1)
                        pool.wait_ge(rot_done, rdone.next())
                pool.wait_ge(yb_ready, ybr.next(8))
                turn(NH // 2, proj_tile(GA))
                turn(NH // 2, proj_tile(GB))
                for g in range(4):
                    pool.wait_ge(acc_taken, accs.next())
                    b = g % 2
                    t = xres[:, :, g * CH:(g + 1) * CH]
                    pool.tensor_tensor(t, t, proj[:, 1, b * 1024:(b + 1) * 1024].rearrange("p (m n) -> p m n", m=M),
                                       ALU.add).then_inc(x_ready, 1)

            pool.wait_ge(rstd_ready, rstd.next())
            turn(KT // 2, x_tile)
            hin, hbr, hwr, hss = (Seen(pool, s) for s in (hg_turned, hg_b, hg_w, hg_ss))
            accs.skip(16)
            pool.wait_ge(ga_ready, 2 * DEPTH + 2)

            def hgrn_scale():
                pool.wait_ge(hg_ss, hss.next(2))
                link(pool.tensor_tensor(st[:, 2:4], st[:, 0:2], eps.broadcast_to([P, M]), ALU.add))
                pool.tensor_tensor(st[:, 4:6], st[:, 2:4], kst[:, C_PW:C_PW + 2], ALU.pow).then_inc(hg_rstd, 1)

            def hgrn(g, first):
                pool.wait_ge(hg_turned, hin.next())
                pool.tensor_copy(xn[:, 0, :, :], proj[:, :, ds(g * HD, HD)])
                pool.tensor_copy(xn[:, 1, :, :], proj[:, :, ds(1024 + g * HD, HD)]).then_inc(hg_in, 1)
                pool.wait_ge(hg_b, hbr.next())
                for _, first_half, second, mid in level_views(wk, hb):
                    pool.tensor_tensor(first_half[0], mid, first_half[1], ALU.subtract)
                pool.tensor_tensor(wk[:, LEVELS, 0:P], hb[:, P - 1:P].broadcast_to([P, P]), hb[:, 0:P],
                                   ALU.subtract).then_inc(hg_d1, 1)
                pool.wait_ge(hg_w, hwr.next())
                for _, first_half, second, mid in level_views(wk, hk):
                    pool.tensor_tensor(first_half[0], first_half[0], first_half[1], ALU.mult)
                pool.tensor_tensor(wk[:, LEVELS, 0:P], wk[:, LEVELS, 0:P], hk[:, 0:P], ALU.mult).then_inc(hg_x1, 1)
                if not first:
                    hgrn_scale()

            hgrn(0, True)
            with loop(pool, NH - 1, {hin: 1, hbr: 1, hwr: 1, hss: 2, linked: 1}) as i:
                hgrn(i + 1, False)
            hgrn_scale()
            accs.skip(8)
            pool.wait_ge(ga_ready, 2 * DEPTH + 3)
            cvf = Seen(pool, cv_turned)
            lgc = scr[:, 3584:4096].rearrange("p (b m d) -> p b m d", b=2, m=M)
            with loop(pool, 4, {cvf: 2}) as i:
                for b in range(2):
                    k = 2 * i + b
                    pool.wait_ge(cv_turned, cvf.next())
                    pool.tensor_tensor(xn[:, b, :, :], cg2[:, :, ds(k * P, P)], proj[:, :, ds(1024 + k * P, P)], ALU.mult)
                    pool.tensor_tensor(lgc[:, b, :, :], proj[:, :, ds(k * P, P)], proj[:, :, ds(2048 + k * P, P)],
                                       ALU.mult).then_inc(cv_in, 1)
            pool.wait_ge(cv_turned, cvf.ahead(2))
            turn(NH // 2, proj_tile(3072))
            pool.wait_ge(acc_taken, accs.next(8))
            turn(KT // 2, lambda o, k: pool.tensor_tensor(o, proj[:, :, ds(4096 + k * P, P)], proj[:, :, ds(6144 + k * P, P)],
                                                          ALU.add))
            pool.wait_ge(rstd_ready, rstd.next())
            turn(KT // 2, x_tile)
            pool.wait_ge(p_landed, 16)
            turn(1, proj_tile(6144))


_INS = ["x", "c", "positions", "rel_bias", "norm_gain", "w_mod", "b_mod", "w_in", "q_norm_gain", "k_norm_gain",
        "ret_norm_gain", "w_out", "p_2", "norm_mix_g_2", "w_in_2", "conv_w_2", "lb_param_2", "hg_norm_g_2",
        "w_a_out_2", "w_b_out_2", "w_o_2", "ple_norm_g_2", "w_ple_gate_2", "w_ple_proj_2", "final_norm_g_2"]


def kernel(**inputs):
    import concourse.bacc as bacc
    from concourse.bass_utils import run_bass_kernel_spmd

    nc = bacc.Bacc("TRN2", target_bir_lowering=False, num_devices=1)
    arrays, args = {}, []
    consts, levels = constants()
    for name, a in [(n, np.ascontiguousarray(inputs[n])) for n in _INS] + [("consts", consts), ("levels", levels)]:
        arrays["in_" + name] = a
        args.append(nc.dram_tensor("in_" + name, a.shape, mybir.dt.from_np(a.dtype), kind="ExternalInput").ap())
    out = nc.dram_tensor("out_0", (1, S, D), F32, kind="ExternalOutput").ap()
    build(nc, *args, out)
    r = run_bass_kernel_spmd(nc, [arrays], core_ids=[0])
    return r.results[0]["out_0"]
```

```python
from contextlib import ExitStack, contextmanager
import math

import numpy as np
import concourse.bass as bass
from concourse import mybir

F32 = mybir.dt.float32
F32R = mybir.dt.float32r
I32 = mybir.dt.int32
U8 = mybir.dt.uint8
ALU = mybir.AluOpType
ACT = mybir.ActivationFunctionType
AX = mybir.AxisListType.X
ds = bass.ds

P = 128
D = 2048
S = 256
M = S // P
KT = D // P
DEPTH = 2
HD = 128
NH = 8
DA = NH * HD
IH, ID = 16, 64
TOPK = min(256, S // 4)
NB = 32
EXACT, MAXD = 16, 128
EPS = 1e-6
SCALE = HD ** -0.5
CH = 512

QA = 0
KA = QA + DA
VA = KA + HD
GA = VA + HD
QI = GA + DA
KI = QI + IH * ID
WI = KI + ID
QB = WI + IH
KB = QB + DA
VB = KB + DA
GB = VB + DA
N_IN = GB + DA
NCH = N_IN // CH
TAIL = N_IN - NCH * CH
IN2 = 6 * D

C_ID = 0
C_MASK = C_ID + P
C_INV = C_MASK + 2 * P
C_QG = C_INV + HD // 2
C_KG = C_QG + M * NH
C_B = C_KG + M * NH
C_EPS = C_B + NB
C_HPI = C_EPS + 1
C_PW = C_HPI + 1
C_N = C_PW + 2

V1 = {"b_mod": (0, 96), "norm_gain": (96, 32)}
V2, _at = {}, 0
for _n, _k in (("c", 16), ("norm_mix_g_2", 16), ("hg_norm_g_2", 8), ("ple_norm_g_2", 16), ("conv_w_2", 24),
               ("lb_param_2", 8), ("ret_norm_gain", 16), ("q_norm_gain", 2), ("k_norm_gain", 2)):
    V2[_n] = (_at, _k)
    _at += _k
NV2 = _at
LEVELS = 7

B_FIRST, B_A, B_B = 13, 10, 6
B_C = NB - B_FIRST - B_A - B_B
RAW = 4
SPL = 4


def constants():
    k = np.zeros((P, C_N), np.float32)
    k[:, C_ID:C_ID + P] = np.eye(P)
    r = np.arange(P)
    k[:, C_MASK:C_MASK + P] = (r[None, :] >= r[:, None])
    k[:, C_MASK + P:C_MASK + 2 * P] = 1.0
    half = HD // 2
    k[:, C_INV:C_INV + half] = np.float32(10000.0) ** (-np.arange(half, dtype=np.float32) / np.float32(half))
    lg = np.log1p(-np.exp2(-5.0 - np.arange(NH)))
    for m in range(M):
        t = (m * P + r)[:, None]
        k[:, C_QG + m * NH:C_QG + (m + 1) * NH] = np.exp(lg[None, :] * t)
        k[:, C_KG + m * NH:C_KG + (m + 1) * NH] = np.exp(-lg[None, :] * t) * SCALE
    k[:, C_B:C_B + NB] = np.arange(NB)
    k[:, C_EPS] = EPS
    k[:, C_HPI] = math.pi / 2
    k[:, C_PW:C_PW + 2] = -0.5
    lv = np.zeros((P, 5, P), np.float32)
    for n in range(LEVELS):
        b = 64 >> n
        lv[:, max(n - 3, 0)] += ((r[:, None] // (2 * b) == r[None, :] // (2 * b)) & (r[:, None] // b % 2 == 0)
                                 & (r[None, :] // b % 2 == 1))
    lv[:, 4] = np.eye(P)
    return k, lv


class Seen:

    def __init__(self, eng, sem, start=0):
        self.eng, self.sem, self.n, self.i, self.per, self.base = eng, sem, start, None, 0, 0

    def next(self, more=1):
        self.n += more
        return self.n + self.base if self.i is None else self.i * self.per + (self.base + self.n)

    def skip(self, n):
        self.n += n

    def ahead(self, n):
        v = self.next(n)
        self.n -= n
        return v


@contextmanager
def loop(eng, turns, per):
    with eng.Fori(0, turns) as i:
        for s, n in per.items():
            s.i, s.per, s.base, s.n = i, n, s.n, 0
        yield i
        for s, n in per.items():
            assert s.n == n, (s.sem, s.n, n)
            s.i, s.n, s.base = None, s.base + turns * n, 0


def bc(ap, n):
    return ap.unsqueeze(len(ap.shape)).broadcast_to([*ap.shape, n])


def build(nc, x, c, positions, rel_bias, norm_gain, w_mod, b_mod, w_in, q_norm_gain, k_norm_gain, ret_norm_gain,
          w_out, p_2, norm_mix_g_2, w_in_2, conv_w_2, lb_param_2, hg_norm_g_2, w_a_out_2, w_b_out_2, w_o_2,
          ple_norm_g_2, w_ple_gate_2, w_ple_proj_2, final_norm_g_2, consts, levels, out):
    ctx = ExitStack()
    with ctx:
        def sb(name, shape, dt=F32):
            return ctx.enter_context(nc.sbuf_tensor(name, shape, dt))

        def sem(name):
            return ctx.enter_context(nc.semaphore(name))

        xres = sb("xres", [P, M, D])
        ht_hi = sb("ht_hi", [P, KT, S], F32R)
        ht_lo = sb("ht_lo", [P, KT, S], F32R)
        proj = sb("proj", [P, M, 8192])
        raw = sb("raw", [P, RAW, 4, CH])
        w_hi = sb("w_hi", [P, SPL, 2, CH], F32R)
        w_lo = sb("w_lo", [P, SPL, 2, CH], F32R)
        scr = sb("scr", [P, 6144])
        kst = sb("kst", [P, C_N])
        lvm = sb("lvm", [P, 5, P], U8)
        vcol = sb("vcol", [P, P + NV2])
        modc = sb("modc", [P, DEPTH * 48])
        acol = sb("acol", [P, DEPTH * KT])
        lbc = sb("lbc", [P, 3 * NH])
        cs = proj[:, 1, N_IN + 384:N_IN + 640].rearrange("p (a m d) -> p a m d", a=2, m=M)
        xn = sb("xn", [P, 2, M, P])
        ktile = proj[:, 0, N_IN:N_IN + S]
        mb = proj[:, 1, N_IN:N_IN + 384]
        st = sb("st", [P, 64])
        tmp8 = proj[:, 0, N_IN + 256:N_IN + 272].rearrange("p (m k) -> p m k", m=M)
        bns = proj[:, 0, N_IN + 272:N_IN + 296].rearrange("p (n k) -> p n k", n=4)
        mv = proj[:, 0, N_IN + 296:N_IN + 304].rearrange("p (n k) -> p n k", n=4)

        ident = kst[:, C_ID:C_ID + P]
        maskt = kst[:, C_MASK:C_MASK + 2 * P]
        eps = kst[:, C_EPS:C_EPS + 1]
        ones = kst[:, C_MASK + P:C_MASK + P + 1]
        ones128 = kst[:, C_MASK + P:C_MASK + 2 * P]

        macc = scr[:, 3072:5120].rearrange("p (b e n) -> p b e n", b=2, e=2)
        rbt = scr[:, 5120:5376]
        onehot = proj[:, 1, QB + 1024:N_IN].bitcast(U8).rearrange("p (b k) -> p b k", b=NB)
        btmp = proj[:, 0, QB + 1024:N_IN].rearrange("p (b h k) -> p b h k", b=2, h=NH // 2)
        bucket = proj[:, 0, 2048:2432]
        rel = proj[:, 0, 2432:2816]
        prow_i = proj[:, 1, 2048:2304].bitcast(I32)
        prow = proj[:, 1, 2304:2560]
        pcol_i = proj[:, 1, 2560:2562].bitcast(I32)
        pcol = proj[:, 1, 2562:2564]
        ang = proj[:, 1, 2564:2692].rearrange("p (m d) -> p m d", m=M)
        ang_n = proj[:, 1, 2692:2820].rearrange("p (m d) -> p m d", m=M)
        lb_t = proj[:, 1, 2820:2836].rearrange("p (a h) -> p a h", a=2)

        def one(ap, k):
            return ap[:, k:k + 1]

        def v1(n, i=0, k=1):
            return vcol[:, V1[n][0] + i:V1[n][0] + i + k]

        def v2(n, i=0, k=1):
            return vcol[:, P + V2[n][0] + i:P + V2[n][0] + i + k]

        bias = scr[:, 0:3072].rearrange("p (h k) -> p h k", h=NH)
        lb_s = scr[:, 3072:3840].rearrange("p (b k) -> p b k", b=2)
        lg = scr[:, 3840:4608].rearrange("p (b k) -> p b k", b=2)
        pt = scr[:, 4608:5376].rearrange("p (b k) -> p b k", b=2)
        qt = scr[:, 5376:5888].rearrange("p (b k) -> p b k", b=2)
        ttmp = scr[:, 5888:6144]
        ttmp2 = scr[:, 5632:6144].rearrange("p (b t) -> p b t", b=2)
        idx = proj[:, 0, N_IN + 304:N_IN + 688]
        kit = scr[:, 5888:6144]
        sq = scr[:, 5376:6016]
        rqt = scr[:, 4096:5120].rearrange("p (b w t) -> p b w t", b=2, w=2)
        rst = scr[:, 5120:5888].rearrange("p (b k) -> p b k", b=2)
        ro = proj[:, 0, 0:512].rearrange("p (b m d) -> p b m d", b=2, m=M)
        rtmp = proj[:, 1, 0:1024].rearrange("p (a w d) -> p a w d", a=4, w=4)
        wk = scr[:, 0:2048].rearrange("p (n t) -> p n t", t=S)
        wq = scr[:, 2048:4096].rearrange("p (n t) -> p n t", t=S)
        hq = scr[:, 4096:4352]
        hk = scr[:, 4352:4608]
        hs = scr[:, 4608:5120]
        hb = scr[:, 5120:5376]
        hat = scr[:, 5376:5632].rearrange("p (m t) -> p m t", m=M)
        hax = scr[:, 5632:5760]
        hy = scr[:, 5888:6144].rearrange("p (m d) -> p m d", m=M)
        cg2 = scr[:, 0:2048].rearrange("p (m n) -> p m n", m=M)
        ut = scr[:, 2048:2048 + 2 * 258].rearrange("p (b t) -> p b t", b=2)
        ct = scr[:, 2560 + 8:2560 + 8 + 512].rearrange("p (b t) -> p b t", b=2)

        def level_views(dst, src):
            for n in range(LEVELS):
                h = 64 >> n
                dv, sv = (a.rearrange("p (n two t) -> p n two t", two=2, t=h) for a in (dst[:, n, :], src))
                yield (n, (dv[:, :, 0, :], sv[:, :, 0, :]), (dv[:, :, 1, :], sv[:, :, 1, :]),
                       sv[:, :, 0, h - 1:h].broadcast_to([P, S // (2 * h), h]))

        def of_layer(l):
            return lambda k: (one(acol, l * KT + k), one(modc, l * 48 + k))

        def of_outputs(l):
            return lambda k: (None if k < NH else v2("ret_norm_gain", l * NH + k - NH), None)

        acc = ctx.enter_context(nc.psum_tensor("acc", [P, 2, M, CH], F32))
        tps = ctx.enter_context(nc.psum_tensor("tps", [P, 2, CH], F32))
        sps = ctx.enter_context(nc.psum_tensor("sps", [P, 2, CH], F32))

        gates = nc.dram_tensor("gates", (DEPTH * KT, P), F32, kind="Internal").ap()

        s_const = sem("s_const")
        s_x = sem("s_x")
        s_vec = sem("s_vec")
        s_pos = sem("s_pos")
        s_rb = sem("s_rb")
        vec_turned = sem("vec_turned")
        vec_ready = sem("vec_ready")
        c_ready = sem("c_ready")
        raw_landed = [sem(f"raw_landed{j}") for j in range(RAW)]
        hi_ready = sem("hi_ready")
        raw_read = sem("raw_read")
        split_used = sem("split_used")
        acc_taken = sem("acc_taken")
        dve_link = sem("dve_link")
        dve_passed = sem("dve_passed")
        act_link = sem("act_link")
        pool_link = sem("pool_link")
        pool_passed = sem("pool_passed")
        mod_summed = sem("mod_summed")
        mod_taken = sem("mod_taken")
        scale_ready = sem("scale_ready")
        gate_turned = sem("gate_turned")
        gate_rows = sem("gate_rows")
        gate_out = sem("gate_out")
        gate_bc = sem("gate_bc")
        onehot_ready = sem("onehot_ready")
        bias_product_ready = sem("bias_product_ready")
        bias_added = sem("bias_added")
        rot_ready = sem("rot_ready")
        sums_ready = sem("sums_ready")
        squares_ready = sem("squares_ready")
        row_summed = sem("row_summed")
        root_ready = sem("root_ready")
        rstd_ready = sem("rstd_ready")
        turn_in = sem("turn_in")
        turned = sem("turned")
        turn_hi = sem("turn_hi")
        turn_lo = sem("turn_lo")
        proj_ready = sem("proj_ready")
        x_ready = sem("x_ready")
        k_ready = sem("k_ready")
        k_turned = sem("k_turned")
        kt_ready = sem("kt_ready")
        qi_turned = sem("qi_turned")
        qit_ready = sem("qit_ready")
        dots_ready = sem("dots_ready")
        relu_ready = sem("relu_ready")
        dots_used = sem("dots_used")
        idx_ready = sem("idx_ready")
        idx_causal = sem("idx_causal")
        sel_ready = sem("sel_ready")
        mb_ready = sem("mb_ready")
        qn_ready = sem("qn_ready")
        qn_turned = sem("qn_turned")
        qt_ready = sem("qt_ready")
        lb_ready = sem("lb_ready")
        scores_ready = sem("scores_ready")
        logits_ready = sem("logits_ready")
        max_ready = sem("max_ready")
        probs_ready = sem("probs_ready")
        probs_turned = sem("probs_turned")
        pt_ready = sem("pt_ready")
        heads_out = sem("heads_out")
        y_ready = sem("y_ready")
        ga_ready = sem("ga_ready")
        rot_done = sem("rot_done")
        rqk_turned = sem("rqk_turned")
        rqt_ready = sem("rqt_ready")
        rs_ready = sem("rs_ready")
        rst_ready = sem("rst_ready")
        ret_out = sem("ret_out")
        ret_taken = sem("ret_taken")
        ret_var = sem("ret_var")
        ret_root = sem("ret_root")
        yb_ready = sem("yb_ready")
        act_acc = sem("act_acc")
        lb_stats = sem("lb_stats")
        lb_exp = sem("lb_exp")
        lbc_ready = sem("lbc_ready")
        hg_in = sem("hg_in")
        hg_turned = sem("hg_turned")
        hg_sig = sem("hg_sig")
        hg_f = sem("hg_f")
        hg_ln = sem("hg_ln")
        hg_w = sem("hg_w")
        hg_b = sem("hg_b")
        hg_d1 = sem("hg_d1")
        hg_d2 = sem("hg_d2")
        hg_x1 = sem("hg_x1")
        hg_x2 = sem("hg_x2")
        hg_rstd = sem("hg_rstd")
        hg_a = sem("hg_a")
        hg_at = sem("hg_at")
        hg_axr = sem("hg_axr")
        hg_o = sem("hg_o")
        hg_ss = sem("hg_ss")
        hg_y = sem("hg_y")
        cv_in = sem("cv_in")
        cv_turned = sem("cv_turned")
        cv_u = sem("cv_u")
        cv_c = sem("cv_c")
        cv_y = sem("cv_y")
        cv_hi = sem("cv_hi")
        cv_lo = sem("cv_lo")
        p_landed = sem("p_landed")
        fin_g = sem("fin_g")
        fin_ready = sem("fin_ready")
        s_out = sem("s_out")

        x_rows = x[0].rearrange("(m p) d -> p m d", p=P)
        out_rows = out[0].rearrange("(m p) d -> p m d", p=P)

        def ktiles(w):
            return w.rearrange("(k p) n -> p k n", p=P)

        wm = [ktiles(w_mod[l]) for l in range(DEPTH)]
        wi = [ktiles(w_in[l]) for l in range(DEPTH)]
        wo = [ktiles(w_out[l]) for l in range(DEPTH)]
        wi2 = ktiles(w_in_2[0])
        wa2, wb2, wo2 = ktiles(w_a_out_2[0]), ktiles(w_b_out_2[0]), ktiles(w_o_2[0])
        wg2, wp2 = ktiles(w_ple_gate_2[0]), ktiles(w_ple_proj_2[0])

        def full(w):
            return lambda j, col, n: w[:, 4 * j:4 * j + 4, ds(col, n)]

        def two(j, col, n):
            return (wa2 if j < 2 else wb2)[:, 4 * (j % 2):4 * (j % 2) + 4, ds(col, n)]

        REC, GATES, CONV = 4096, 8192, 0
        W2_PARTS = [(REC, 8), (GATES, 8), (CONV, 2), (CONV + 1024, 6)]

        block = ctx.enter_context(nc.Block())

        @block.sync
        def _(sp):
            free = Seen(sp, raw_read)

            sp.dma_start(vcol[0:96, 0:P], b_mod.rearrange("l (k p) -> (l k) p", p=P)).then_inc(s_vec, 16)
            sp.dma_start(vcol[96:128, 0:P], norm_gain.rearrange("l (k p) -> (l k) p", p=P)).then_inc(s_vec, 16)
            for name, ap in (("c", c), ("norm_mix_g_2", norm_mix_g_2), ("hg_norm_g_2", hg_norm_g_2),
                             ("ple_norm_g_2", ple_norm_g_2), ("lb_param_2", lb_param_2),
                             ("ret_norm_gain", ret_norm_gain), ("q_norm_gain", q_norm_gain),
                             ("k_norm_gain", k_norm_gain)):
                o, k = V2[name]
                sp.dma_start(xn[o:o + k, 0, 0, :], ap.rearrange("l (k p) -> (l k) p", p=P)).then_inc(s_vec, 16)
            o, k = V2["conv_w_2"]
            sp.dma_start(xn[o:o + k, 0, 0, :], conv_w_2[0].rearrange("t (k p) -> (t k) p", p=P)).then_inc(s_vec, 16)
            sp.dma_start(kst[:, :], consts).then_inc(s_const, 16)
            sp.dma_start(scr[:, 5376:6016], levels.rearrange("p n t -> p (n t)")).then_inc(s_const, 16)

            def pieces(src, col, n, width=CH, kts=4):
                for j in range(RAW):
                    sp.wait_ge(raw_read, free.next(2))
                    sp.dma_start(raw[:, j, 0:kts, 0:width], src(j, col, width)).then_inc(raw_landed[j], 16)

            def with_mod(src, col, mod, mod_col):
                for j in range(4):
                    for n, (w, at) in enumerate(((src, col), (mod, mod_col))):
                        slot = (2 * j + n) % RAW
                        sp.wait_ge(raw_read, free.next(2))
                        sp.dma_start(raw[:, slot, :, :], w(j, at, CH)).then_inc(raw_landed[slot], 16)

            with loop(sp, 8, {free: 8}) as i:
                pieces(full(wm[0]), i * CH, CH)
            with loop(sp, 4, {free: 16}) as i:
                with_mod(full(wi[0]), i * -CH + 6 * CH, full(wm[0]), 2 * D + i * CH)
            with loop(sp, 2, {free: 16}) as i:
                with_mod(full(wi[0]), i * -CH + 2 * CH, full(wm[1]), i * CH)
            with loop(sp, 2, {free: 16}) as i:
                with_mod(full(wi[0]), i * (7 * CH), full(wm[1]), 2 * CH + i * CH)
            with loop(sp, 6, {free: 8}) as i:
                pieces(full(wi[0]), 8 * CH + i * CH, CH)
            pieces(full(wi[0]), NCH * CH, CH, width=TAIL)
            with loop(sp, 4, {free: 16}) as i:
                with_mod(full(wo[0]), i * CH, full(wm[1]), 4 * CH + i * CH)
            with loop(sp, 4, {free: 16}) as i:
                with_mod(full(wi[1]), i * -CH + 6 * CH, full(wm[1]), 2 * D + i * CH)
            with loop(sp, 3, {free: 8}) as i:
                pieces(full(wi[1]), i * -CH + 2 * CH, CH)
            with loop(sp, 7, {free: 8}) as i:
                pieces(full(wi[1]), 7 * CH + i * CH, CH)
            pieces(full(wi[1]), NCH * CH, CH, width=TAIL)
            with loop(sp, 4, {free: 8}) as i:
                pieces(full(wo[1]), i * CH, CH)
            for col, n in W2_PARTS:
                with loop(sp, n, {free: 8}) as i:
                    pieces(full(wi2), col + i * CH, CH)
            with loop(sp, 4, {free: 8}) as i:
                pieces(two, i * CH, CH)
            with loop(sp, 4, {free: 8}) as i:
                pieces(full(wo2), i * CH, CH)
            with loop(sp, 4, {free: 8}) as i:
                pieces(full(wg2), i * CH, CH)
            for j in range(RAW):
                sp.wait_ge(raw_read, free.next(2))
                sp.dma_start(raw[:, j, 0:2, :], wp2[:, :, j * CH:(j + 1) * CH]).then_inc(raw_landed[j], 16)
            for m in range(M):
                sp.wait_ge(fin_ready, m + 1)
                sp.dma_start(out_rows[:, m, :], proj[:, m, 0:D]).then_inc(s_out, 16)
            sp.wait_ge(s_out, 16 * M)

        @block.tensor
        def _(pe):
            pe.sem_inc(split_used, SPL)
            pe.sem_inc(turned, 2)
            pe.sem_inc(mod_summed, 2)
            pe.sem_inc(qn_turned, 2)
            pe.sem_inc(hg_turned, 1)
            pe.sem_inc(cv_turned, 2)
            lo = Seen(pe, raw_read, 8)
            taken = Seen(pe, acc_taken)
            t_in, t_lo = Seen(pe, turn_in), Seen(pe, turn_lo)

            def gemm(turns, halves, group, width=CH, side=None, side_per=None, mods=0, drain=True,
                     turning=None):
                def turn_pair(p):
                    for k in (2 * p, 2 * p + 1):
                        pe.wait_ge(turn_in, t_in.next())
                        pe.wait_ge(turn_lo, t_lo.next())
                        for m in range(M):
                            tr = pe.transpose(tps[:, k % 2, m * P:(m + 1) * P], xn[:, k % 2, m, :], ident)
                        tr.then_inc(turned, 1)

                def body(t, first):
                    for x, (slot, kts) in enumerate(halves):
                        buf = x // group % 2
                        if turning is not None and first and x < 8:
                            if x == 0 and turning == 0:
                                turn_pair(0)
                            if x < 7 and 2 * x + 2 >= turning:
                                turn_pair(x + 1)
                            if x == 7:
                                pe.wait_ge(turn_lo, t_lo.ahead(2))
                        if x % group == 0:
                            pe.wait_ge(acc_taken, taken.next())
                        pe.wait_ge(raw_read, lo.next())
                        for u, kt in enumerate(kts):
                            for m in range(M):
                                hi_m, lo_m = (a[:, kt, m * P:(m + 1) * P] for a in (ht_hi, ht_lo))
                                start, stop = x % group == 0 and u == 0, x % group == group - 1 and u == len(kts) - 1
                                o = acc[:, buf, m, 0:width]
                                pe.matmul(o, hi_m, w_hi[:, slot, u, 0:width], start=start, stop=False)
                                pe.matmul(o, hi_m, w_lo[:, slot, u, 0:width], start=False, stop=False)
                                mm = pe.matmul(o, lo_m, w_hi[:, slot, u, 0:width], start=False, stop=stop)
                        mm.then_inc(split_used, 1)
                        if x // 8 < mods and x % 8 == 7:
                            pe.wait_ge(raw_read, lo.next(2))
                            mod_sums(x // 8 % 2)
                        elif x // 8 < mods and x % 2:
                            lo.skip(2)
                        if side:
                            side(t, x, first)
                if drain:
                    pe.wait_ge(acc_taken, taken.ahead(2))
                per = {taken: len(halves) // group, lo: len(halves) + 8 * mods}
                if mods:
                    per[m_taken] = mods
                if turns == 1:
                    body(0, True)
                elif side or turning is not None:
                    body(0, True)
                    with loop(pe, turns - 1, {**per, **(side_per or {})}) as i:
                        body(i + 1, False)
                else:
                    with loop(pe, turns, per) as i:
                        body(i, False)

            def chunk_halves(n):
                return [(h % SPL, (2 * h, 2 * h + 1)) for h in range(8)] * n

            def turn(n):
                with loop(pe, n, {t_in: 2, t_lo: 2}):
                    for b in range(2):
                        pe.wait_ge(turn_in, t_in.next())
                        pe.wait_ge(turn_lo, t_lo.next())
                        for m in range(M):
                            tr = pe.transpose(tps[:, b, m * P:(m + 1) * P], xn[:, b, m, :], ident)
                        tr.then_inc(turned, 1)

            pe.wait_ge(s_vec, 16 * 11)
            pe.wait_ge(s_const, 32)
            pe.transpose(tps[:, 0, 0:P], vcol[:, 0:P], ident)
            pe.transpose(tps[:, 0, P:P + NV2], xn[0:NV2, 0, 0, :], ident[0:NV2, 0:NV2]).then_inc(vec_turned, 1)

            m_taken = Seen(pe, mod_taken)

            def mod_sums(b):
                pe.wait_ge(mod_taken, m_taken.next())
                for j in range(4):
                    for e in range(2):
                        mm = pe.matmul(tps[:, 1, j:j + 1], macc[:, b, e, j * P:(j + 1) * P], ones,
                                       start=e == 0, stop=e == 1)
                mm.then_inc(mod_summed, 1)

            with loop(pe, 4, {lo: 16, m_taken: 2}):
                for b in range(2):
                    pe.wait_ge(raw_read, lo.next(8))
                    mod_sums(b)

            ktt, dots = Seen(pe, kt_ready), Seen(pe, dots_used, 0)
            qit = Seen(pe, qit_ready)
            qn, qtr, prb, ptr, yr = (Seen(pe, s) for s in (qn_ready, qt_ready, probs_ready, pt_ready, y_ready))
            rq, rs, rt = (Seen(pe, s) for s in (rqt_ready, rst_ready, ret_taken))
            rd = Seen(pe, rot_done, 2)
            kr, gt = Seen(pe, k_ready), Seen(pe, gate_rows)

            def index_queries(g):
                for b in range(2):
                    for m in range(M):
                        o = QI + (2 * g + b) * P
                        tr = pe.transpose(tps[:, 0, b * S + m * P:b * S + (m + 1) * P], proj[:, m, o:o + P], ident)
                tr.then_inc(qi_turned, 1)

            def index_dots(b):
                for e in range(2):
                    pe.wait_ge(dots_used, dots.next())
                    r = slice(64 * e, 64 * e + 64)
                    pe.matmul(sps[:, e, 0:P], qt[r, b, 0:P], kit[r, 0:P], start=True, stop=True)
                    pe.matmul(sps[:, e, P:P + S], qt[r, b, P:S], kit[r, :], start=True,
                              stop=True).then_inc(dots_ready, 1)

            def index_start(t, x, first):
                if x == 12:
                    pe.wait_ge(acc_taken, taken.ahead(1))
                    pe.wait_ge(k_ready, kr.next())
                    for m in range(M):
                        tr = pe.transpose(tps[:, 0, m * P:(m + 1) * P], xn[:, 0, m, :], ident)
                    tr.then_inc(k_turned, 1)
                if x == 14:
                    pe.wait_ge(kt_ready, ktt.next())
                    index_queries(0)

            def index(t, x, first):
                if x % 2 == 0:
                    k = x // 2
                    if k % 2 == 0:
                        pe.wait_ge(qit_ready, qit.next())
                    index_dots(k % 2)
                    if k % 2 and k < 7:
                        index_queries(k // 2 + 1)

            def gate_and_keys(l, x):
                if x == 4:
                    pe.wait_ge(mod_taken, 1 + 12 * (l + 1))
                    pe.transpose(tps[0:KT, 0, 0:P], modc[:, l * 48 + 32:l * 48 + 48], ident).then_inc(gate_turned, 1)
                if x == 10:
                    pe.wait_ge(gate_rows, gt.next())
                    pe.wait_ge(k_ready, kr.next())
                    for m in range(M):
                        tr = pe.transpose(tps[:, 0, S + m * P:S + (m + 1) * P], xn[:, 1, m, :], ident)
                    tr.then_inc(k_turned, 1)

            def heads(t, x, first):
                if first and x == 0:
                    pe.wait_ge(kt_ready, ktt.next())
                    pe.wait_ge(mod_taken, m_taken.ahead(1))
                for b in range(2):
                    if x % 8 == 0:
                        pe.wait_ge(qn_ready, qn.next())
                        for m in range(M):
                            tr = pe.transpose(tps[:, b, m * P:(m + 1) * P], xn[:, b, m, :], ident)
                        tr.then_inc(qn_turned, 1)
                    if x % 8 == 2:
                        pe.wait_ge(qt_ready, qtr.next())
                        pe.wait_ge(y_ready, yr.next())
                        pe.matmul(sps[:, b, 0:P], qt[:, b, 0:P], ktile[:, 0:P], start=True, stop=True)
                        pe.matmul(sps[:, b, P:P + S], qt[:, b, P:S], ktile, start=True,
                                  stop=True).then_inc(scores_ready, 1)
                    if x % 8 == 5:
                        pe.wait_ge(probs_ready, prb.next())
                        for n in range(3):
                            tr = pe.transpose(tps[:, b, n * P:(n + 1) * P], lg[:, b, n * P:(n + 1) * P], ident)
                        tr.then_inc(probs_turned, 1)
                    if x % 8 == 7:
                        pe.wait_ge(pt_ready, ptr.next())
                        v = [proj[:, m, VA:VA + HD] for m in range(M)]
                        pe.matmul(sps[:, b, 0:P], pt[:, b, 0:P], v[0], start=True, stop=True)
                        pe.matmul(sps[:, b, P:S], pt[:, b, P:S], v[0], start=True, stop=False)
                        pe.matmul(sps[:, b, P:S], pt[:, b, S:S + P], v[1], start=False,
                                  stop=True).then_inc(heads_out, 1)

            def retention(l, u):
                p, n = u // 6, u % 6
                for b in range(2):
                    h = 2 * p + b
                    if n == 0:
                        pe.wait_ge(rot_done, rd.next())
                        for w, col in enumerate((QB, KB)):
                            for m in range(M):
                                tr = pe.transpose(tps[:, b, w * S + m * P:w * S + (m + 1) * P],
                                                  proj[:, m, col + h * HD:col + (h + 1) * HD], ident)
                        tr.then_inc(rqk_turned, 1)
                    if n == 2:
                        if p == 0:
                            pe.wait_ge(y_ready, yr.ahead(2))
                        pe.wait_ge(rqt_ready, rq.next())
                        pe.wait_ge(ret_taken, rt.next())
                        pe.matmul(sps[:, b, 0:S], rqt[:, b, 1, 0:P], rqt[:, b, 0, :], start=True, stop=True)
                        pe.matmul(sps[:, b, S:S + P], rqt[:, b, 1, P:S], rqt[:, b, 0, P:S], start=True,
                                  stop=True).then_inc(rs_ready, 1)
                    if n == 4:
                        pe.wait_ge(rst_ready, rs.next())
                        pe.wait_ge(acc_taken, 2 + (NCH + 1 + 4) * l + (12 if p < 2 else 13))
                        v = [proj[:, m, VB + h * HD:VB + (h + 1) * HD] for m in range(M)]
                        pe.matmul(sps[:, b, 0:P], rst[:, b, 0:P], v[0], start=True, stop=True)
                        pe.matmul(sps[:, b, P:S], rst[:, b, P:S], v[0], start=True, stop=False)
                        pe.matmul(sps[:, b, P:S], rst[:, b, S:S + P], v[1], start=False,
                                  stop=True).then_inc(ret_out, 1)

            for l in range(DEPTH):
                pe.wait_ge(mod_taken, m_taken.ahead(1))
                gemm(1, chunk_halves(2), 8, mods=2, turning=0)
                gemm(1, chunk_halves(2), 8, mods=2, side=index_start, drain=False)
                gemm(1, chunk_halves(2), 8, mods=2 * (l == 0), side=index, drain=False)
                gemm(1, chunk_halves(2), 8, mods=2 * (l == 0), side=lambda t, x, first: gate_and_keys(l, x), drain=False)
                gemm(2, chunk_halves(2), 8, side=heads, side_per={a: 4 for a in (qn, qtr, prb, ptr, yr)}, drain=False)
                gemm(1, chunk_halves(2), 8, side=lambda t, x, first: retention(l, x), drain=False)
                gemm(1, chunk_halves(1), 8, width=TAIL, side=lambda t, x, first: retention(l, 16 + x), drain=False)
                gemm(2, chunk_halves(2), 8, mods=2 * (l == 0), turning=0)

            hin, hx1, hx2, hat_r, haxr, hyr = (Seen(pe, s) for s in (hg_in, hg_x1, hg_x2, hg_at, hg_axr, hg_y))

            def hgrn_scores():
                pe.wait_ge(hg_x1, hx1.next())
                pe.wait_ge(hg_x2, hx2.next())
                pe.wait_ge(hg_y, hyr.next())
                for m in range(M):
                    c0 = m * P

                    def score(lv, s0, t0, h, o):
                        return pe.matmul(o, wk[:, lv, c0 + s0:c0 + s0 + h], wk[:, lv, c0 + t0:c0 + t0 + h],
                                         start=True, stop=True)
                    region = [sps[:, r // 2, (r % 2 * 2 + m) * P:(r % 2 * 2 + m + 1) * P] for r in range(4)]
                    for r in range(4):
                        score(3 + r, 0, 0, P, region[r])
                    for lv in range(3):
                        h = 64 >> lv
                        for s0 in range(0, P, 2 * h):
                            score(lv, s0, s0 + h, h, region[0][s0:s0 + h, s0 + h:s0 + 2 * h])
                    pe.matmul(tps[:, 1, c0:c0 + P], hk[:, c0:c0 + P], hq[:, c0:c0 + P], start=True, stop=True)
                pe.matmul(tps[:, 0, 0:P], wk[:, LEVELS, 0:P], wk[:, LEVELS, P:S], start=True,
                          stop=True).then_inc(hg_a, 1)

            def hgrn_out(g):
                pe.wait_ge(hg_at, hat_r.next())
                v = [proj[:, m, ds(2048 + g * HD, HD)] for m in range(M)]
                pe.matmul(tps[:, 1, S:S + P], hat[:, 0, :], v[0], start=True, stop=True)
                pe.matmul(tps[:, 1, S + P:2 * S], hat[:, 1, :], v[1], start=True, stop=False)
                pe.matmul(tps[:, 1, S + P:2 * S], hax, v[0], start=False, stop=True).then_inc(hg_o, 1)

            def hgrn(t, x, first):
                g, n = 2 * t + x // 8, x % 8
                begin = first and x < 8
                if n == 0 and not begin:
                    hgrn_scores()
                if n == 1:
                    if not begin:
                        pe.wait_ge(hg_axr, haxr.next())
                    pe.wait_ge(hg_in, hin.next())
                    for b in range(2):
                        for m in range(M):
                            tr = pe.transpose(tps[:, 0, b * S + m * P:b * S + (m + 1) * P], xn[:, b, m, :], ident)
                    tr.then_inc(hg_turned, 1)
                if n == 4 and not begin:
                    hgrn_out(g - 1)
            cin, cy = Seen(pe, cv_in), Seen(pe, cv_y)

            def conv():
                with loop(pe, 4, {cin: 2, cy: 2}):
                    for b in range(2):
                        pe.wait_ge(cv_in, cin.next())
                        pe.wait_ge(cv_y, cy.next())
                        for m in range(M):
                            pe.transpose(tps[:, b, m * P:(m + 1) * P], xn[:, b, m, :], ident)
                            tr = pe.transpose(tps[:, b, S + m * P:S + (m + 1) * P], lgc[:, b, m, :], ident)
                        tr.then_inc(cv_turned, 1)

            lgc = scr[:, 3584:4096].rearrange("p (b m d) -> p b m d", b=2, m=M)

            for col, n in W2_PARTS:
                if col == GATES:
                    gemm(n // 2, chunk_halves(2), 8, side=hgrn,
                         side_per={s: 2 for s in (hin, hx1, hx2, hat_r, haxr, hyr)})
                    hgrn_scores()
                    pe.wait_ge(hg_axr, haxr.next())
                    hgrn_out(NH - 1)
                else:
                    gemm(n // 2, chunk_halves(2), 8, turning=0 if col == REC else None)
            conv()
            pe.wait_ge(cv_y, cy.ahead(2))
            pe.wait_ge(cv_lo, 2 + 8)
            gemm(4, chunk_halves(1), 4, turning=NH)
            gemm(2, chunk_halves(2), 8, turning=0)
            gemm(2, chunk_halves(2), 8, turning=0)
            turn(1)
            pe.wait_ge(turn_lo, t_lo.ahead(2))
            gemm(1, [(j, (0, 1)) for j in range(4)], 1)


        @block.scalar
        def _(act):
            act.sem_inc(acc_taken, 2)
            act.sem_inc(ret_taken, 2)
            act.dma_start(prow_i, positions.partition_broadcast(P)).then_inc(s_pos, 16)
            for m in range(M):
                act.dma_start(pcol_i[:, m:m + 1], positions[0].rearrange("(m p o) -> m p o", p=P, o=1)[m])\
                   .then_inc(s_pos, 16)
            act.dma_start(rbt, rel_bias.rearrange("b h -> (b h)").partition_broadcast(P)).then_inc(s_rb, 16)

            act.dma_start(xres[:, :, :], x_rows).then_inc(s_x, 16)
            landed = [Seen(act, s, 16 * 8) for s in raw_landed]
            slot_free = Seen(act, split_used)
            results = Seen(act, split_used, SPL)
            t_out = Seen(act, turned, 2)

            def link(ins):
                ins.then_inc(act_link, 1)
                act.wait_ge(act_link, linked.next())

            linked = Seen(act, act_link)

            def split(turns, nh, group, width=CH, halves=2, evac=None, side=None, side_per=None, mods=0,
                      prior=None, flush=True, turning=None, scales=None):
                gb = nh // group

                def take(g, b):
                    act.wait_ge(split_used, results.next(group))
                    evac(g, b)

                def body(t, first):
                    for x in range(nh):
                        j = x // halves % RAW
                        if x // 8 < mods:
                            j = 2 * j % RAW
                            if x % halves == 0:
                                landed[j + 1].skip(16)
                        if x % halves == 0:
                            act.wait_ge(raw_landed[j], landed[j].next(16))
                        act.wait_ge(split_used, slot_free.next())
                        act.activation(w_hi[:, x % SPL, :, 0:width],
                                       raw[:, j, 2 * (x % halves):2 * (x % halves) + 2, 0:width],
                                       ACT.Copy).then_inc(hi_ready, 1)
                        if turning is not None and first and turning <= 2 * x < 16:
                            for k in (2 * x, 2 * x + 1):
                                turn_tile(k, *(scales(k) if scales else (None, None)))
                        if x % group == min(3, group - 1):
                            g = x // group - 1
                            if evac and not (first and x < group):
                                take(t * gb + g, g % 2)
                            if first and x < group and prior:
                                at, n = prior
                                act.wait_ge(split_used, results.next(8))
                                at(n, n % 2)
                        if side:
                            side(t, x, first)

                body(0, True)
                if turns > 1:
                    per = {slot_free: nh, results: nh if evac else 0, **(side_per or {})}
                    per.update({s: 16 * nh // (RAW * halves) + 16 * mods for s in landed})
                    with loop(act, turns - 1, per) as i:
                        body(i + 1, False)
                if not evac:
                    results.skip(turns * nh)
                elif flush:
                    take(turns * gb - 1, (turns * gb - 1) % 2)

            def turn_tile(k, scale, bias):
                act.wait_ge(turned, t_out.next())
                kw = {n: v for n, v in (("scale", scale), ("bias", bias)) if v is not None}
                act.activation(ht_hi[:, k, :], tps[:, k % 2, 0:S], ACT.Copy if bias is None else ACT.Identity,
                               **kw).then_inc(turn_hi, 1)

            xr = Seen(act, x_ready, 2)

            rsum = Seen(act, row_summed)

            def row_squares(g, at):
                for m in range(M):
                    act.activation(proj[:, m, at + g * CH:at + (g + 1) * CH], xres[:, m, g * CH:(g + 1) * CH], ACT.Square,
                                   accum_out=st[:, 56 + 4 * m + g:57 + 4 * m + g]).then_inc(squares_ready, 1)

            def row_root():
                act.wait_ge(row_summed, rsum.next())
                act.activation(st[:, 2:4], st[:, 0:2], ACT.Sqrt, bias=eps, scale=1.0 / D).then_inc(root_ready, 1)

            act.wait_ge(vec_turned, 1)
            link(act.activation(vcol[:, :], tps[:, 0, 0:P + NV2], ACT.Copy))
            act.activation(v2("c", 0, KT), v2("c", 0, KT), ACT.Silu).then_inc(vec_ready, 1)
            act.wait_ge(lb_stats, 1)
            act.activation(lb_t[:, 1, :], lb_t[:, 0, :], ACT.Exp).then_inc(lb_exp, 1)

            act.wait_ge(s_x, 16)
            for g in range(4):
                row_squares(g, 0)
            row_root()
            oh, added = Seen(act, onehot_ready), Seen(act, bias_added)

            def bias_product(bucket_at, h):
                if h == 0:
                    act.wait_ge(onehot_ready, oh.next())
                if h % 4 == 0:
                    act.wait_ge(bias_added, added.next())
                r = act.activation(btmp[:, h // 4, h % 4, :], onehot[:, ds(bucket_at, 1), :].rearrange("p a k -> p (a k)"),
                                   ACT.Copy, scale=rbt[:, ds(bucket_at * NH + h, 1)])
                if h % 4 == 3:
                    r.then_inc(bias_product_ready, 1)

            act.wait_ge(s_rb, 16)
            with loop(act, B_FIRST, {oh: 1, added: 2}) as i:
                for h in range(NH):
                    bias_product(i, h)
            act.wait_ge(rot_ready, 1)
            act.activation(cs[:, 1, :, :], ang, ACT.Sin).then_inc(rot_done, 1)
            act.activation(cs[:, 0, :, :], ang_n, ACT.Sin, bias=kst[:, C_HPI:C_HPI + 1]).then_inc(rot_done, 1)

            def bias_beside(first, n, x, steps):
                for k in range(x * n * NH // steps, (x + 1) * n * NH // steps):
                    bias_product(first + k // NH, k % NH)

            rr, ktn, qtn, dr = (Seen(act, s) for s in (sums_ready, k_turned, qi_turned, dots_ready))
            qnt, mx, pbt = Seen(act, qn_turned, 2), Seen(act, max_ready), Seen(act, probs_turned)
            rqt_t, rout, rvar = Seen(act, rqk_turned), Seen(act, ret_out), Seen(act, ret_var)

            gtu, grd, gout = Seen(act, gate_turned), Seen(act, gate_rows), Seen(act, gate_out)

            def bias_done():
                act.wait_ge(bias_added, 2 + 2 * NB)

            def to_proj(width=CH, func=ACT.Copy, base=0, step=CH, wait=None):
                def evac(g, b):
                    if wait:
                        wait()
                    act.activation(proj[:, :, ds(base + g * step, width)], acc[:, b, :, 0:width], func)\
                       .then_inc(acc_taken, 1)
                return evac

            for l in range(DEPTH):
                if l:
                    for g in range(4):
                        act.wait_ge(x_ready, xr.next())
                        row_squares(g, D)
                    row_root()
                first_acc = 2 + (NCH + 1 + 4) * l

                def bias_a1(t, x, first):
                    if l == 0:
                        if x >= 8:
                            bias_beside(B_FIRST, B_A, x - 8, 24)

                def index_keys(t, x, first):
                    if l == 0:
                        bias_beside(B_FIRST, B_A, 8 + x, 24)
                    if x == 15:
                        act.wait_ge(k_turned, ktn.next())
                        act.activation(kit, tps[:, 0, 0:S], ACT.Copy).then_inc(kt_ready, 1)

                def index_relu():
                    for e in range(2):
                        act.wait_ge(dots_ready, dr.next())
                        act.activation(sps[:, e, 0:384], sps[:, e, 0:384], ACT.Relu).then_inc(relu_ready, 1)

                def index_queries():
                    act.wait_ge(qi_turned, qtn.next())
                    act.activation(qt, tps[:, 0, :].rearrange("p (b t) -> p b t", b=2), ACT.Copy).then_inc(qit_ready, 1)

                def index(t, x, first):
                    if l == 0:
                        bias_beside(B_FIRST + B_A, B_B, x, 16)
                    if x >= 4 and x % 2 == 0:
                        index_relu()
                    if x % 4 == 2:
                        index_queries()

                def norms(t, x, first):
                    if l == 0 and 6 <= x < 14:
                        bias_beside(B_FIRST + B_A + B_B, B_C, x - 6, 8)
                    if x == 0 or x == 2:
                        index_relu()
                    if x == 4 or x == 13:
                        a, z = (4, 9) if x == 4 else (0, 4)
                        act.wait_ge(sums_ready, rr.next())
                        act.activation(st[:, 24:42].rearrange("p (m h) -> p m h", m=M)[:, :, a:z],
                                       st[:, 4:22].rearrange("p (m h) -> p m h", m=M)[:, :, a:z],
                                       ACT.Sqrt, bias=eps, scale=1.0 / HD).then_inc(root_ready, 1)
                    if x == 8:
                        act.wait_ge(gate_turned, gtu.next())
                        act.activation(ttmp[0:KT, P:2 * P], tps[0:KT, 0, 0:P], ACT.Copy).then_inc(gate_rows, 1)
                    if x == 9:
                        act.wait_ge(gate_rows, grd.next())
                        act.dma_start(gates[l * KT:(l + 1) * KT, :], ttmp[0:KT, P:2 * P]).then_inc(gate_out, 16)
                        act.wait_ge(acc_taken, first_acc + 5)
                        act.activation(proj[:, :, GA:GA + DA], proj[:, :, GA:GA + DA], ACT.Silu).then_inc(ga_ready, 1)
                    if x == 14:
                        act.wait_ge(k_turned, ktn.next())
                        act.activation(ktile, tps[:, 0, S:2 * S], ACT.Copy, scale=v2("k_norm_gain", l)).then_inc(kt_ready, 1)

                def probs_columns():
                    for b in range(2):
                        act.wait_ge(probs_turned, pbt.next())
                        act.activation(pt[:, b, :], tps[:, b, 0:384], ACT.Copy).then_inc(pt_ready, 1)

                def heads(t, x, first):
                    n = x % 8
                    if n == 1 and not (first and x < 8):
                        probs_columns()
                    if n == 4:
                        for b in range(2):
                            act.wait_ge(qn_turned, qnt.next())
                            act.activation(qt[:, b, :], tps[:, b, 0:S], ACT.Copy, scale=v2("q_norm_gain", l))\
                               .then_inc(qt_ready, 1)
                    if n == 7:
                        for b in range(2):
                            act.wait_ge(max_ready, mx.next())
                            act.activation(lg[:, b, 0:P], lg[:, b, 0:P], ACT.Exp, bias=st[:, 44 + 2 * b:45 + 2 * b],
                                           accum_out=st[:, 48 + 2 * b:49 + 2 * b])
                            act.activation(lg[:, b, P:384], lg[:, b, P:384], ACT.Exp, bias=st[:, 45 + 2 * b:46 + 2 * b],
                                           accum_out=st[:, 49 + 2 * b:50 + 2 * b]).then_inc(probs_ready, 1)

                def retention(u):
                    if u % 6 == 4 and u < 24:
                        for b in range(2):
                            act.wait_ge(rqk_turned, rqt_t.next())
                            act.activation(rqt[:, b, :, :], tps[:, b, :].rearrange("p (w t) -> p w t", w=2), ACT.Copy)\
                               .then_inc(rqt_ready, 1)
                    if u % 6 == 2 and u >= 8:
                        for b in range(2):
                            act.wait_ge(ret_out, rout.next())
                            for m in range(M):
                                q = C_QG + m * NH + 2 * (u // 6 - 1) + b
                                r = act.activation(ro[:, b, m, :], sps[:, b, m * P:(m + 1) * P], ACT.Copy,
                                                   scale=kst[:, q:q + 1])
                            r.then_inc(ret_taken, 1)
                    if u % 6 == 3 and u >= 9:
                        act.wait_ge(ret_var, rvar.next())
                        act.activation(st[:, 0:4], mv[:, :, 1], ACT.Sqrt, bias=eps).then_inc(ret_root, 1)

                down6, down4, down2 = (to_proj(base=a * CH, step=-CH) for a in (6, 4, 2))
                ends = to_proj(base=0, step=7 * CH)
                up8, up12 = to_proj(base=8 * CH, wait=bias_done if l == 0 else None), to_proj(base=12 * CH)
                act.wait_ge(scale_ready, l + 1)
                split(1, 16, 8, evac=down6, mods=2, side=bias_a1, flush=False, turning=0, scales=of_layer(l))
                split(1, 16, 8, evac=down4, mods=2, side=index_keys, prior=(down6, 1), flush=False)
                split(1, 16, 8, evac=down2, mods=2 * (l == 0), side=index, prior=(down4, 1), flush=False)
                split(1, 16, 8, evac=ends, mods=2 * (l == 0), side=norms, prior=(down2, 1), flush=False)
                split(2, 16, 8, evac=up8, side=heads, side_per={qnt: 4, mx: 4, pbt: 4}, prior=(ends, 1), flush=False)
                probs_columns()
                split(1, 16, 8, evac=up12, side=lambda t, x, first: retention(x), prior=(up8, 3), flush=False)
                split(1, 8, 8, width=TAIL, evac=to_proj(TAIL, base=NCH * CH), side=lambda t, x, first: retention(16 + x),
                      prior=(up12, 1))

                def last_pair_and_gates(t, x, first):
                    if first and x == 0:
                        retention(26)
                        act.wait_ge(acc_taken, first_acc + NCH + 1)
                        act.activation(proj[:, :, GB:GB + DA], proj[:, :, GB:GB + DA], ACT.Silu).then_inc(ga_ready, 1)
                    if first and x == 1:
                        retention(27)
                    if first and x == 4:
                        act.wait_ge(gate_out, gout.next(16))
                        act.dma_start(proj[:, 0, 0:D], gates[l * KT:(l + 1) * KT, :].rearrange("k p -> (k p)")
                                      .partition_broadcast(P)).then_inc(gate_bc, 16)
                split(2, 16, 8, mods=2 * (l == 0), side=last_pair_and_gates, turning=0, scales=of_outputs(l))

            for g in range(4):
                act.wait_ge(x_ready, xr.next())
                row_squares(g, D)
            row_root()
            hgt, hgf, hgd1, hgd2, hga, hgo = (Seen(act, s) for s in (hg_turned, hg_f, hg_d1, hg_d2, hg_a, hg_o))
            hgt.skip(1)

            def hgrn_cross():
                act.wait_ge(hg_a, hga.next())
                act.activation(hax, tps[:, 0, 0:P], ACT.Copy).then_inc(hg_axr, 1)

            def hgrn_squares():
                act.wait_ge(hg_o, hgo.next())
                for m in range(M):
                    act.activation(hy[:, m, :], tps[:, 1, S + m * P:S + (m + 1) * P], ACT.Square,
                                   scale=HD ** -0.5, accum_out=st[:, m:m + 1]).then_inc(hg_ss, 1)

            def hgrn(t, x, first):
                n = x % 8
                begin = first and x < 8
                if n == 2 and not begin:
                    hgrn_cross()
                if n == 3:
                    act.wait_ge(hg_turned, hgt.next())
                    act.activation(hs[:, 0:S], tps[:, 0, S:2 * S], ACT.Sigmoid)
                    act.activation(hk, tps[:, 0, S:2 * S], ACT.Sigmoid, scale=-1.0)
                    act.activation(hq, tps[:, 0, 0:S], ACT.Copy).then_inc(hg_sig, 1)
                if n == 4:
                    act.wait_ge(hg_f, hgf.next())
                    act.activation(hs, hs, ACT.Ln).then_inc(hg_ln, 1)
                if n == 5:
                    act.wait_ge(hg_d1, hgd1.next())
                    act.wait_ge(hg_d2, hgd2.next())
                    act.activation(wk, wk, ACT.Exp).then_inc(hg_w, 1)
                if n == 6 and not begin:
                    hgrn_squares()
            ngroups = 2 + DEPTH * (NCH + 1 + 4)
            for col, n in W2_PARTS:
                if col == CONV:
                    def evac(g, b):
                        act.activation(cg2[:, :, ds(g * CH, CH)], acc[:, b, :, :], ACT.Copy).then_inc(acc_taken, 1)
                else:
                    evac = to_proj(func=ACT.Sigmoid if col == GATES else ACT.Copy, base=4096 if col == GATES else 0)
                if col == GATES:
                    split(n // 2, 16, 8, evac=evac, side=hgrn, side_per={s: 2 for s in (hgt, hgf, hgd1, hgd2, hga, hgo)})
                    hgrn_cross()
                    hgrn_squares()
                else:
                    split(n // 2, 16, 8, evac=evac, turning=0 if col == REC else None,
                          scales=lambda k: (v2("norm_mix_g_2", k), None))
                ngroups += n
                if col == REC:
                    act.wait_ge(acc_taken, ngroups)
                    act.activation(proj[:, :, 0:1024], proj[:, :, 0:1024], ACT.Silu).then_inc(ga_ready, 1)
                    act.activation(proj[:, :, 3072:4096], proj[:, :, 3072:4096], ACT.Silu).then_inc(ga_ready, 1)
            act.wait_ge(acc_taken, ngroups)
            act.activation(proj[:, :, 2048:3072], proj[:, :, 2048:3072], ACT.Silu).then_inc(ga_ready, 1)
            cvt, cvc = Seen(act, cv_turned, 2), Seen(act, cv_y, 2)
            act.wait_ge(cv_hi, 1)
            with loop(act, 4, {cvt: 2, cvc: 2}) as i:
                for b in range(2):
                    act.wait_ge(cv_turned, cvt.next())
                    act.activation(ut[:, b, 2:258], tps[:, b, 0:S], ACT.Copy).then_inc(cv_u, 1)
                for b in range(2):
                    act.wait_ge(cv_y, cvc.next())
                    act.activation(ht_hi[:, ds(2 * i + b, 1), :].rearrange("p a t -> p (a t)"), ct[:, b, :],
                                   ACT.Copy).then_inc(cv_hi, 1)
            split(4, 8, 4, turning=NH, scales=lambda k: (v2("hg_norm_g_2", k - NH), None))

            def last_inputs(t, x, first):
                if first and x == 8:
                    act.dma_start(proj[:, :, 6144:6400], p_2[0, 0].rearrange("(m p) d -> p m d", p=P))\
                       .then_inc(p_landed, 16)
                    act.dma_start(proj[:, 0, 4096:6144], final_norm_g_2.partition_broadcast(P)).then_inc(fin_g, 16)
            split(2, 16, 8, side=last_inputs, turning=0)
            for g in range(4):
                act.wait_ge(acc_taken, ngroups + 8 + g + 1)
                row_squares(g, D)
            row_root()
            split(2, 16, 8, evac=to_proj(func=ACT.Sigmoid), turning=0, scales=lambda k: (v2("ple_norm_g_2", k), None))
            for k in range(2):
                turn_tile(k, None, None)
            split(1, 4, 1, halves=1)
            for g in range(4):
                act.wait_ge(x_ready, 2 + 8 + g + 1)
                row_squares(g, D)
            row_root()

        @block.vector
        def _(dve):
            dve.sem_inc(raw_read, 8)
            dve.sem_inc(mod_taken, 1)
            dve.sem_inc(turn_lo, 2)
            dve.sem_inc(dots_used, 2)
            dve.sem_inc(y_ready, 2)
            dve.sem_inc(logits_ready, 2)
            dve.sem_inc(yb_ready, 2)
            dve.sem_inc(hg_y, 1)
            dve.sem_inc(cv_y, 2)
            dve.sem_inc(cv_lo, 2)
            linked = Seen(dve, dve_link)

            def link(ins):
                ins.then_inc(dve_link, 1)
                dve.wait_ge(dve_link, linked.next())

            hi = Seen(dve, hi_ready)
            results = Seen(dve, split_used, SPL)
            t_hi, t_lo = Seen(dve, turn_hi), Seen(dve, turn_lo)

            def split(turns, nh, group, width=CH, halves=2, evac=None, side=None, side_per=None, mods=0,
                      prior_mod=False, keep_mod=False, turning=None, scales=None):
                gb = nh // group

                def take(g, b):
                    dve.wait_ge(split_used, results.next(group))
                    evac(g, b)

                def body(t, first):
                    for x in range(nh):
                        j = x // halves % RAW
                        if x // 8 < mods:
                            j = 2 * j % RAW
                        dve.wait_ge(hi_ready, hi.next())
                        dve.tensor_tensor(w_lo[:, x % SPL, :, 0:width],
                                          raw[:, j, 2 * (x % halves):2 * (x % halves) + 2, 0:width],
                                          w_hi[:, x % SPL, :, 0:width].bitcast(F32), ALU.subtract).then_inc(raw_read, 1)
                        own.skip(1)
                        if turning is not None and first and turning <= 2 * x < 16:
                            for k in (2 * x, 2 * x + 1):
                                turn_tile(k, *(scales(k) if scales else (None, None)))
                        if x % halves == 0:
                            m_land[j].skip(16)
                        if mods and x % 8 == 3 and not (first and x < 8):
                            mod_take(t * mods + x // 8 - 1 + mod_at[0])
                        if prior_mod and first and x == 3:
                            mod_take(mod_at[0] - 1)
                        if x // 8 < mods and x % 2:
                            mod_piece(x // 8 % 2, x % 8 // 2, j + 1)
                        if evac and x % group == min(3, group - 1) and not (first and x < group):
                            g = x // group - 1
                            take(t * gb + g, g % 2)
                        if side:
                            side(t, x, first)

                body(0, True)
                if turns > 1:
                    per = {hi: nh, results: nh if evac else 0, **(side_per or {})}
                    if evac in owners:
                        per.update(owners[evac])
                    per.update({s: 16 * nh // (RAW * halves) + 16 * mods for s in m_land})
                    per[own] = nh + 8 * mods
                    if mods:
                        per.update({m_free: mods, m_sum: mods})
                    with loop(dve, turns - 1, per) as i:
                        body(i + 1, False)
                if evac:
                    take(turns * gb - 1, (turns * gb - 1) % 2)
                else:
                    results.skip(turns * nh)
                mod_at[0] += turns * mods
                if mods and not keep_mod:
                    mod_take(mod_at[0] - 1)

            owners = {}

            def turn_tile(k, scale, bias):
                dve.wait_ge(turn_hi, t_hi.next())
                b, h, o = k % 2, ht_hi[:, k, :].bitcast(F32), ht_lo[:, k, :]
                if bias is not None:
                    dve.wait_ge(turn_lo, t_lo.next())
                    link(dve.tensor_scalar(ttmp2[:, b, :], tps[:, b, 0:S], scale, bias, ALU.mult, ALU.add))
                    r = dve.tensor_tensor(o, ttmp2[:, b, :], h, ALU.subtract)
                elif scale is not None:
                    r = dve.scalar_tensor_tensor(o, tps[:, b, 0:S], scale, h, ALU.mult, ALU.subtract)
                else:
                    r = dve.tensor_tensor(o, tps[:, b, 0:S], h, ALU.subtract)
                if bias is None:
                    t_lo.skip(1)
                r.then_inc(turn_lo, 1)

            dve.wait_ge(s_pos, 48)
            dve.wait_ge(s_const, 32)
            dve.tensor_copy(lvm[:, :, :], scr[:, 5376:6016].rearrange("p (n t) -> p n t", t=P))
            dve.tensor_copy(prow, prow_i)
            link(dve.tensor_copy(pcol, pcol_i))
            for m in range(M):
                o = slice(0, P) if m == 0 else slice(P, 384)
                r = dve.tensor_scalar(rel[:, o], prow[:, 0:(m + 1) * P], pcol[:, m:m + 1], -1.0, ALU.subtract, ALU.mult)
            link(r)
            link(dve.tensor_scalar(bucket, rel, 0.0, float(EXACT), ALU.max, ALU.min))
            for j in range(1, NB - EXACT):
                thr = math.ceil(EXACT * (MAXD / EXACT) ** (j / (NB - EXACT)))
                link(dve.scalar_tensor_tensor(bucket, rel, float(thr), bucket, ALU.is_ge, ALU.add))
            dve.wait_ge(vec_ready, 1)
            lp = v2("lb_param_2", 0, NH)
            dve.tensor_tensor(lb_t[:, 0, :], lp, lp, ALU.subtract).then_inc(lb_stats, 1)
            m_free, m_sum = Seen(dve, mod_summed), Seen(dve, mod_summed, 2)
            m_land = [Seen(dve, s) for s in raw_landed]
            own = Seen(dve, raw_read, 8)
            mod_at = [8]

            def mod_piece(b, q, slot):
                if q == 0:
                    dve.wait_ge(mod_summed, m_free.next())
                dve.wait_ge(raw_landed[slot], m_land[slot].next(16))
                for u in range(2):
                    if q or u:
                        dve.wait_ge(raw_read, own.ahead(0))
                    for e in range(2):
                        kt = 4 * q + 2 * u + e
                        if q == 0 and u == 0:
                            r = dve.tensor_scalar(macc[:, b, e, :], raw[:, slot, 2 * u + e, :], v2("c", kt), None, ALU.mult)
                        else:
                            r = dve.scalar_tensor_tensor(macc[:, b, e, :], raw[:, slot, 2 * u + e, :], v2("c", kt),
                                                         macc[:, b, e, :], ALU.mult, ALU.add)
                    r.then_inc(raw_read, 1)
                    own.skip(1)

            def mod_take(cm):
                dve.wait_ge(mod_summed, m_sum.next())
                dve.tensor_tensor(modc[:, ds(cm * 4, 4)], tps[:, 1, 0:4], vcol[:, ds(V1["b_mod"][0] + cm * 4, 4)],
                                  ALU.add).then_inc(mod_taken, 1)

            def onehots(first, n):
                for k in range(n):
                    dve.tensor_tensor(onehot[:, ds(first + k, 1), :].rearrange("p a k -> p (a k)"), bucket,
                                      kst[:, ds(C_B + first + k, 1)].broadcast_to([P, 384]), ALU.is_equal)\
                       .then_inc(onehot_ready, 1)

            root, accs = Seen(dve, root_ready), Seen(dve, acc_taken, 2)
            sqr = Seen(dve, squares_ready)

            def row_scale():
                dve.wait_ge(squares_ready, sqr.next(8))
                dve.tensor_reduce(st[:, 0:2], st[:, 56:64].rearrange("p (m g) -> p m g", m=M), AX, ALU.add)\
                   .then_inc(row_summed, 1)
                dve.wait_ge(root_ready, root.next())
                dve.reciprocal(st[:, 22:24], st[:, 2:4]).then_inc(rstd_ready, 1)

            def angles():
                for m in range(M):
                    r = dve.tensor_scalar(ang[:, m, :], kst[:, C_INV:C_INV + HD // 2], pcol[:, m:m + 1], None, ALU.mult)
                link(r)
                big = 1.5 * 2 ** 23
                link(dve.tensor_scalar(ang_n, ang, 1.0 / (2 * math.pi), big, ALU.mult, ALU.add))
                link(dve.tensor_scalar(ang_n, ang_n, -big, None, ALU.add))
                c1 = 6.28125
                c2 = float(np.float32(2 * math.pi - c1).view(np.uint32) & np.uint32(0xfffff000))
                c2 = float(np.uint32(np.float32(2 * math.pi - c1).view(np.uint32) & np.uint32(0xfffff000)).view(np.float32))
                c3 = 2 * math.pi - c1 - c2
                for cc in (c1, c2, c3):
                    link(dve.scalar_tensor_tensor(ang, ang_n, -cc, ang, ALU.mult, ALU.add))
                link(dve.tensor_scalar(ang, ang, 3.1415925, -3.1415925, ALU.min, ALU.max))
                link(dve.tensor_scalar(ang_n, ang, -1.0, None, ALU.mult))
                dve.tensor_tensor(ang_n, ang, ang_n, ALU.min).then_inc(rot_ready, 1)

            def lower_bound():
                dve.wait_ge(lb_exp, 1)
                link(dve.reciprocal(lb_t[:, 0, :], lb_t[:, 1, :]))
                link(dve.tensor_tensor(lb_t[:, 0, :], lb_t[:, 0, :], lb_t[:, 1, :], ALU.mult))
                link(dve.tensor_tensor(lb_t[:, 1, :], lb_t[:, 0, :], lb_t[:, 0, :], ALU.subtract))
                link(dve.tensor_scalar(lb_t[:, 1, :], lb_t[:, 1, :], 0.0, 1.0 - 1e-6, ALU.max, ALU.min))
                dve.tensor_scalar(lbc[:, 0:NH], lb_t[:, 1, :], -1.0, 1.0, ALU.mult, ALU.add)
                link(dve.tensor_scalar(lbc[:, NH:2 * NH], lb_t[:, 1, :], 1e-30, None, ALU.max))


            def mod_turn(i, first=False, onehot=0):
                for b in range(2):
                    for q in range(4):
                        mod_piece(b, q, q)
                        if q == 1 and not (first and b == 0):
                            mod_take(2 * i + b - 1)
                    if onehot:
                        onehots(onehot + 4 * b, 4 if onehot + 4 * b < NB // 2 else 0)
                    if first and b == 0:
                        lower_bound()
                    if first and b == 1:
                        angles()
                        row_scale()

            onehots(0, 4)
            mod_turn(0, first=True, onehot=4)
            mod_turn(1, onehot=12)
            with loop(dve, 2, {m_free: 2, m_sum: 2, own: 16, **{s: 32 for s in m_land}}) as i:
                mod_turn(i + 2)
            mod_take(7)

            rl, sc, lbr, prb, ho = (Seen(dve, s) for s in (relu_ready, scores_ready, lb_ready, probs_ready, heads_out))
            du, rsr, rtk, rrt = Seen(dve, dots_used, 1), Seen(dve, rs_ready), Seen(dve, ret_taken, 2), Seen(dve, ret_root)
            gar, xfree, mbr = Seen(dve, ga_ready), Seen(dve, x_ready), Seen(dve, idx_causal)
            mbd = Seen(dve, mb_ready)

            mtk = Seen(dve, mod_taken, 1)
            for l in range(DEPTH):
                dve.wait_ge(mod_taken, mtk.next(8 if l == 0 else 12))
                dve.scalar_tensor_tensor(acol[:, l * KT:(l + 1) * KT], modc[:, l * 48 + KT:l * 48 + 2 * KT], 1.0,
                                         v1("norm_gain", l * KT, KT), ALU.add, ALU.mult).then_inc(scale_ready, 1)
                dve.wait_ge(scale_ready, l + 1)
                if l:
                    row_scale()

                def index_sum(k):
                    for e in range(2):
                        dve.wait_ge(relu_ready, rl.next())
                        dve.wait_ge(dots_used, du.next())
                        for m in range(M):
                            o = slice(0, P) if m == 0 else slice(P, 384)
                            w = WI + 2 * k + e
                            r = dve.scalar_tensor_tensor(idx[:, o], sps[:, e, o], proj[:, m, w:w + 1], idx[:, o],
                                                         ALU.mult, ALU.add)
                        r.then_inc(dots_used, 1)

                def index(t, x, first):
                    if x == 4:
                        dve.wait_ge(acc_taken, accs.next(3))
                    if x >= 4 and x % 2 == 0:
                        index_sum(x // 2 - 2)

                def squares(a, z):
                    for m in range(M):
                        w = sq[:, 0:(z - a) * HD]
                        h = proj[:, m, a * HD:z * HD]
                        link(dve.tensor_tensor(w, h, h, ALU.mult))
                        r = dve.tensor_reduce(st[:, 4 + 9 * m + a:4 + 9 * m + z], w.rearrange("p (h d) -> p h d", d=HD),
                                              AX, ALU.add)
                        if m == 0:
                            link(r)
                    r.then_inc(sums_ready, 1)

                def scales(a, z):
                    dve.wait_ge(root_ready, root.next())
                    dve.reciprocal(st[:, 4:22].rearrange("p (m h) -> p m h", m=M)[:, :, a:z],
                                   st[:, 24:42].rearrange("p (m h) -> p m h", m=M)[:, :, a:z]).then_inc(rstd_ready, 1)

                tiles = [idx[:, 0:P], idx[:, P:384]]

                def norms_and_selection(t, x, first):
                    if x == 0 or x == 2:
                        index_sum(6 + x // 2)
                    if x == 2:
                        dve.wait_ge(dots_used, du.ahead(1))
                        dve.sem_inc(idx_ready, 1)
                    if x == 4:
                        dve.wait_ge(acc_taken, accs.next(3))
                        squares(4, 9)
                    if x == 5:
                        scales(4, 9)
                        dve.wait_ge(idx_causal, mbr.next(2))
                    if 5 <= x < 5 + TOPK // 8:
                        for m in range(M):
                            r = dve.max(tmp8[:, m, :], tiles[m])
                        link(r)
                        for m in range(M):
                            r = dve.match_replace(tiles[m], tmp8[:, m, :], tiles[m], -3.4e38)
                        link(r)
                    if x == 4 + TOPK // 8:
                        dve.tensor_scalar(mb, idx, -3.2e38, -1e30, ALU.is_ge, ALU.mult).then_inc(sel_ready, 1)
                    if x == 13:
                        dve.wait_ge(acc_taken, accs.next())
                        squares(0, 4)
                    if x == 14:
                        scales(0, 4)

                def outputs(col):
                    for b in range(2):
                        dve.wait_ge(probs_ready, prb.next())
                        link(dve.reciprocal(st[:, 52 + 2 * b:54 + 2 * b], st[:, 48 + 2 * b:50 + 2 * b]))
                        dve.wait_ge(heads_out, ho.next())
                        for m in range(M):
                            g = proj[:, m, ds(col + b * HD, HD)]
                            r = dve.scalar_tensor_tensor(g, sps[:, b, m * P:(m + 1) * P], st[:, 52 + 2 * b + m:53 + 2 * b + m],
                                                         g, ALU.mult, ALU.mult)
                        r.then_inc(y_ready, 1)

                def heads(t, x, first):
                    if x % 8 == 3 and not (first and x < 8):
                        outputs(t * (-4 * HD) + (GA + (4 if x > 8 else 10) * HD))
                    if x % 8 == 6:
                        for b in range(2):
                            dve.wait_ge(scores_ready, sc.next())
                            dve.wait_ge(lb_ready, lbr.next())
                            link(dve.scalar_tensor_tensor(lg[:, b, :], sps[:, b, 0:384], SCALE, lb_s[:, b, :],
                                                          ALU.mult, ALU.add))
                            dve.tensor_reduce(st[:, 44 + 2 * b:45 + 2 * b], lg[:, b, 0:P], AX, ALU.max, negate=True)\
                               .then_inc(logits_ready, 1)
                            dve.tensor_reduce(st[:, 45 + 2 * b:46 + 2 * b], lg[:, b, P:384], AX, ALU.max, negate=True)\
                               .then_inc(max_ready, 1)

                def retention(u):
                    if u % 6 == 0 and u >= 6:
                        for b in range(2):
                            dve.wait_ge(rs_ready, rsr.next())
                            k = C_KG + 2 * (u // 6 - 1) + b
                            dve.scalar_tensor_tensor(rst[:, b, 0:S], sps[:, b, 0:S], kst[:, k:k + 1], maskt,
                                                     ALU.mult, ALU.mult)
                            dve.scalar_tensor_tensor(rst[:, b, S:S + P], sps[:, b, S:S + P], kst[:, k + NH:k + NH + 1],
                                                     maskt[:, 0:P], ALU.mult, ALU.mult).then_inc(rst_ready, 1)
                    if u % 6 == 2 and u >= 8:
                        for b in range(2):
                            dve.wait_ge(ret_taken, rtk.next())
                            for m in range(M):
                                r = dve.bn_stats(bns[:, 2 * b + m, :], ro[:, b, m, :])
                        link(r)
                        dve.sem_inc(dve_passed, 1)
                        for n in range(4):
                            r = dve.bn_aggr(mv[:, n, :], bns[:, n, :])
                        r.then_inc(ret_var, 1)
                    if u % 6 == 4 and u >= 10:
                        dve.wait_ge(ret_root, rrt.next())
                        link(dve.reciprocal(st[:, 4:8], st[:, 0:4]))
                        for n in range(4):
                            col = VB + (2 * (u // 6 - 1) + n // 2) * HD
                            r = dve.tensor_scalar(proj[:, n % 2, col:col + HD], ro[:, n // 2, n % 2, :], mv[:, n, 0:1],
                                                  st[:, 4 + n:5 + n], ALU.subtract, ALU.mult)
                        r.then_inc(yb_ready, 2)

                def last_onehots(t, x, first):
                    if l == 0 and x >= 8:
                        onehots(NB // 2 + 2 * (x - 8), 2)

                mods = 2 * (l == 0)
                split(1, 16, 8, mods=2, keep_mod=True, side=last_onehots, turning=0, scales=of_layer(l))
                split(1, 16, 8, mods=2, prior_mod=True, keep_mod=True)
                link(dve.memset(idx, 0.0))
                split(1, 16, 8, mods=mods, side=index, prior_mod=True, keep_mod=l == 0)
                split(1, 16, 8, mods=mods, side=norms_and_selection, prior_mod=l == 0, keep_mod=l == 0)
                dve.wait_ge(ga_ready, gar.next())
                split(2, 16, 8, side=heads, side_per={sc: 4, lbr: 4, prb: 4, ho: 4, linked: 8}, prior_mod=l == 0)
                outputs(GA + 2 * HD)
                split(1, 16, 8, side=lambda t, x, first: retention(x))
                split(1, 8, 8, width=TAIL, side=lambda t, x, first: retention(16 + x))
                retention(24)
                accs.skip(8)
                gar.skip(1)

                def gated(g, b):
                    dve.wait_ge(gate_bc, 16 * (l + 1))
                    dve.wait_ge(x_ready, xfree.next())
                    dve.tensor_tensor(proj[:, 1, b * 1024:(b + 1) * 1024].rearrange("p (m n) -> p m n", m=M),
                                      acc[:, b, :, :],
                                      proj[:, 0, ds(g * CH, CH)].unsqueeze(1).broadcast_to([P, M, CH]),
                                      ALU.mult).then_inc(acc_taken, 1)
                owners[gated] = {xfree: 2}

                def last_pair(t, x, first):
                    if first and x == 0:
                        retention(26)
                    if first and x == 1:
                        retention(28)
                split(2, 16, 8, evac=gated, mods=2 * (l == 0), side=last_pair, turning=0, scales=of_outputs(l))
                accs.skip(4)

            row_scale()
            hsg, hln, hwr, har, hrt = (Seen(dve, s) for s in (hg_sig, hg_ln, hg_w, hg_a, hg_rstd))
            bsc = hb.rearrange("p (m t) -> p m t", m=M)
            lfs = hs[:, 0:S].rearrange("p (m t) -> p m t", m=M)

            def hgrn_merge():
                dve.wait_ge(hg_a, har.next())
                for r in range(5):
                    dve.sem_inc(dve_passed, 1)
                    src = (sps[:, r // 2, r % 2 * S:(r % 2 + 1) * S] if r < 4 else tps[:, 1, 0:S])\
                        .rearrange("p (m t) -> p m t", m=M)
                    o = dve.copy_predicated(hat, lvm[:, r, :].unsqueeze(1).broadcast_to([P, M, P]), src)
                    if r < 4:
                        link(o)
                o.then_inc(hg_at, 1)

            def hgrn_y(g):
                dve.wait_ge(hg_rstd, hrt.next())
                for m in range(M):
                    og = proj[:, m, ds(3072 + g * HD, HD)]
                    r = dve.scalar_tensor_tensor(og, tps[:, 1, S + m * P:S + (m + 1) * P], st[:, 4 + m:5 + m], og,
                                                 ALU.mult, ALU.mult)
                r.then_inc(hg_y, 1)

            def hgrn(t, x, first):
                g, n = 2 * t + x // 8, x % 8
                begin = first and x < 8
                if n == 2 and not begin:
                    hgrn_merge()
                if n == 3:
                    dve.wait_ge(hg_sig, hsg.next())
                    one_lb, floor = lbc[:, ds(g, 1)], lbc[:, ds(NH + g, 1)]
                    dve.tensor_scalar(hk, hk, one_lb, None, ALU.mult)
                    link(dve.tensor_scalar(hb, hs[:, 0:S], one_lb, floor, ALU.mult, ALU.add))
                    dve.tensor_scalar(hs[:, 0:S], hb, 2.0 ** -60, None, ALU.max)
                    dve.tensor_scalar(hs[:, S:2 * S], hb, 2.0 ** -60, 2.0 ** 60, ALU.min, ALU.mult).then_inc(hg_f, 1)
                if n == 4:
                    dve.wait_ge(hg_ln, hln.next())
                    link(dve.tensor_tensor(hs[:, 0:S], hs[:, 0:S], hs[:, S:2 * S], ALU.add))
                    for m in range(M):
                        r = dve.tensor_tensor_scan(bsc[:, m, :], ones128, lfs[:, m, :], 0.0, ALU.mult, ALU.add)
                    r.then_inc(hg_b, 1)
                    dve.wait_ge(hg_b, hbd.next())
                    for _, first_half, second, mid in level_views(wk, hb):
                        dve.tensor_tensor(second[0], second[1], mid, ALU.subtract)
                    dve.tensor_copy(wk[:, LEVELS, P:S], hb[:, P:S]).then_inc(hg_d2, 1)
                if n == 6:
                    dve.wait_ge(hg_w, hwr.next())
                    for _, first_half, second, mid in level_views(wk, hq):
                        dve.tensor_tensor(second[0], second[0], second[1], ALU.mult)
                    dve.tensor_tensor(wk[:, LEVELS, P:S], wk[:, LEVELS, P:S], hq[:, P:S], ALU.mult).then_inc(hg_x2, 1)
                if n == 7 and not begin:
                    hgrn_y(g - 1)

            hbd = Seen(dve, hg_b)
            for col, n in W2_PARTS:
                accs.skip(n)
                if col == GATES:
                    dve.wait_ge(ga_ready, gar.next(2))
                    link(dve.memset(hat, 0.0))
                    split(n // 2, 16, 8, side=hgrn,
                          side_per={hsg: 2, hln: 2, hwr: 2, har: 2, hrt: 2, hbd: 2, linked: 12})
                    hgrn_merge()
                    hgrn_y(NH - 1)
                else:
                    split(n // 2, 16, 8, turning=0 if col == REC else None,
                          scales=lambda k: (v2("norm_mix_g_2", k), None))
            dve.memset(ut, 0.0).then_inc(cv_hi, 1)
            cuu, chh, cll = Seen(dve, cv_u), Seen(dve, cv_hi, 1), Seen(dve, cv_lo)
            cw = v2("conv_w_2", 0, 24)
            with loop(dve, 4, {cuu: 2, chh: 2, cll: 2, linked: 6}) as i:
                for b in range(2):
                    dve.wait_ge(cv_lo, cll.next())
                    dve.wait_ge(cv_u, cuu.next())
                    k = 2 * i + b
                    link(dve.tensor_scalar(ct[:, b, :], ut[:, b, 2:258], cw[:, ds(16 + k, 1)], None, ALU.mult))
                    link(dve.scalar_tensor_tensor(ct[:, b, :], ut[:, b, 1:257], cw[:, ds(8 + k, 1)], ct[:, b, :],
                                                  ALU.mult, ALU.add))
                    link(dve.scalar_tensor_tensor(ct[:, b, :], ut[:, b, 0:256], cw[:, ds(k, 1)], ct[:, b, :],
                                                  ALU.mult, ALU.add))
                    dve.tensor_tensor(ct[:, b, :], ct[:, b, :], tps[:, b, S:2 * S], ALU.mult).then_inc(cv_y, 1)
                for b in range(2):
                    dve.wait_ge(cv_hi, chh.next())
                    at = ds(2 * i + b, 1)
                    dve.tensor_tensor(ht_lo[:, at, :].rearrange("p a t -> p (a t)"), ct[:, b, :],
                                      ht_hi[:, at, :].rearrange("p a t -> p (a t)").bitcast(F32),
                                      ALU.subtract).then_inc(cv_lo, 1)

            def merge(g, b):
                gt = proj[:, :, ds(4096 + b * 2048 + (g - b) * (CH // 2), CH)]
                dve.tensor_tensor(gt, acc[:, b, :, :], gt, ALU.mult).then_inc(acc_taken, 1)
            split(4, 8, 4, evac=merge, turning=NH, scales=lambda k: (v2("hg_norm_g_2", k - NH), None))

            def add_x(g, b):
                xs = xres[:, :, ds(g * CH, CH)]
                dve.tensor_tensor(xs, acc[:, b, :, :], xs, ALU.add).then_inc(acc_taken, 1)
            split(2, 16, 8, evac=add_x, turning=0)
            row_scale()
            accs.skip(8 + 4)
            split(2, 16, 8, turning=0, scales=lambda k: (v2("ple_norm_g_2", k), None))
            for k in range(2):
                turn_tile(k, None, None)
            dve.wait_ge(acc_taken, accs.next(4))

            def embedding(g, b):
                e = proj[:, :, g * CH:(g + 1) * CH]
                ins = dve.tensor_tensor(e, acc[:, b, :, :], e, ALU.mult)
                ins.then_inc(acc_taken, 1)
                dve.wait_ge(acc_taken, accs.next())
                xs = xres[:, :, g * CH:(g + 1) * CH]
                dve.tensor_tensor(xs, xs, e, ALU.add).then_inc(x_ready, 1)
            split(1, 4, 1, halves=1, evac=embedding)
            row_scale()
            dve.wait_ge(rstd_ready, 3 * DEPTH + 3)
            dve.wait_ge(fin_g, 16)
            for m in range(M):
                dve.scalar_tensor_tensor(proj[:, m, 0:D], xres[:, m, :], st[:, 22 + m:23 + m], proj[:, 0, 4096:6144],
                                         ALU.mult, ALU.mult).then_inc(fin_ready, 1)

        @block.gpsimd
        def _(pool):
            pool.sem_inc(x_ready, 2)
            pool.sem_inc(bias_added, 2)
            linked = Seen(pool, pool_link)

            def link(ins):
                ins.then_inc(pool_link, 1)
                pool.wait_ge(pool_link, linked.next())

            prod, badd = Seen(pool, bias_product_ready), Seen(pool, bias_added)

            def bias_sum(n):
                with loop(pool, n, {prod: 2, badd: 2}):
                    for b in range(2):
                        pool.wait_ge(bias_product_ready, prod.next())
                        pool.wait_ge(bias_added, badd.next())
                        o = bias[:, 4 * b:4 * b + 4, :]
                        pool.tensor_tensor(o, o, btmp[:, b, :, :], ALU.add).then_inc(bias_added, 1)

            link(pool.memset(scr[:, 0:3072], 0.0))
            bias_sum(B_FIRST)

            xfree = Seen(pool, turned)
            rstd, accs = Seen(pool, rstd_ready), Seen(pool, acc_taken, 2)
            qnf, lbf = (Seen(pool, s) for s in (qn_turned, logits_ready))
            idr, slr, yr, ybr = Seen(pool, idx_ready), Seen(pool, sel_ready), Seen(pool, y_ready, 2), Seen(pool, yb_ready, 2)
            rdone = Seen(pool, rot_done, 2)
            mbr = Seen(pool, mb_ready)
            ktn = Seen(pool, k_turned)

            def turn(n, make):
                with loop(pool, n, {xfree: 2}) as i:
                    for b in range(2):
                        pool.wait_ge(turned, xfree.next())
                        make(xn[:, b, :, :], 2 * i + b).then_inc(turn_in, 1)

            def x_tile(o, k):
                return pool.tensor_tensor(o, xres[:, :, ds(k * P, P)], bc(st[:, 22:24], P), ALU.mult)

            def proj_tile(col):
                return lambda o, k: pool.tensor_copy(o, proj[:, :, ds(col + k * P, P)])

            def causal(t, fill, done):
                for m in range(M):
                    o = t[:, 0:P] if m == 0 else t[:, P:384]
                    pool.affine_select(out=o, in_=o, compare_op=ALU.is_ge, fill=fill, base=m * P,
                                       pattern=[[-1, (m + 1) * P]], channel_multiplier=1).then_inc(done, 1)

            xs = Seen(pool, acc_taken, 2)
            for l in range(DEPTH):
                pool.wait_ge(rstd_ready, rstd.next())
                turn(KT // 2, x_tile)
                if l == 0:
                    bias_sum(B_A - 2)
                pool.wait_ge(acc_taken, accs.next(3))
                pool.wait_ge(turned, xfree.ahead(2))
                for e in range(2):
                    r = pool.tensor_copy(xn[:, 0, :, 64 * e:64 * e + 64], proj[:, :, KI:KI + ID])
                r.then_inc(k_ready, 1)
                if l == 0:
                    bias_sum(B_B + 2)
                pool.wait_ge(idx_ready, idr.next())
                causal(idx, -3e38, idx_causal)
                pool.wait_ge(acc_taken, accs.next(3))
                pool.wait_ge(rstd_ready, rstd.next())
                rs9 = st[:, 4:22].rearrange("p (m h) -> p m h", m=M)
                pool.tensor_tensor(xn[:, 1, :, :], proj[:, :, KA:KA + HD], bc(rs9[:, :, 8], HD), ALU.mult)\
                    .then_inc(k_ready, 1)
                if l == 0:
                    bias_sum(B_C)
                pool.wait_ge(sel_ready, slr.next())
                causal(mb, -1e30, mb_ready)
                pool.wait_ge(acc_taken, accs.next())
                pool.wait_ge(rstd_ready, rstd.next())
                pool.wait_ge(mb_ready, mbr.next(2))
                pool.wait_ge(k_turned, ktn.next(2))
                if l == 0:
                    pool.wait_ge(mod_taken, 1 + 16)
                with loop(pool, 2, {qnf: 4, lbf: 4}) as i:
                    for n in range(4):
                        h, b = i * -4 + (4 + n), n % 2
                        pool.wait_ge(qn_turned, qnf.next())
                        pool.tensor_tensor(xn[:, b, :, :], proj[:, :, ds(i * (-4 * HD) + (QA + (4 + n) * HD), HD)],
                                           rs9[:, :, ds(h, 1)].broadcast_to([P, M, HD]), ALU.mult).then_inc(qn_ready, 1)
                        pool.wait_ge(logits_ready, lbf.next())
                        pool.tensor_tensor(lb_s[:, b, :], bias[:, ds(h, 1), :].rearrange("p a k -> p (a k)"), mb,
                                           ALU.add).then_inc(lb_ready, 1)
                pool.wait_ge(qn_turned, qnf.ahead(2))
                pool.wait_ge(acc_taken, accs.next(4))
                t4 = [rtmp[:, a, :, :].rearrange("p (w m) d -> p w m d", w=2) for a in range(4)]
                qk = proj[:, :, QB:QB + 2 * DA].rearrange("p m (w n) -> p w m n", w=2)
                cos, sin = (cs[:, a, :, :].unsqueeze(1).broadcast_to([P, 2, M, HD // 2]) for a in range(2))
                half = HD // 2
                with loop(pool, 4, {linked: 2, rdone: 2}) as i:
                    for b in range(2):
                        h = 2 * i + b
                        x1, x2 = qk[:, :, :, ds(h * HD, half)], qk[:, :, :, ds(h * HD + half, half)]
                        pool.tensor_tensor(t4[0], x1, cos, ALU.mult)
                        pool.tensor_tensor(t4[1], x2, sin, ALU.mult)
                        pool.tensor_tensor(t4[2], x1, sin, ALU.mult)
                        link(pool.tensor_tensor(t4[3], x2, cos, ALU.mult))
                        pool.sem_inc(pool_passed, 1)
                        pool.tensor_tensor(x1, t4[0], t4[1], ALU.subtract)
                        pool.tensor_tensor(x2, t4[2], t4[3], ALU.add).then_inc(rot_done, 1)
                        pool.wait_ge(rot_done, rdone.next())
                pool.wait_ge(y_ready, yr.next(8))
                turn(NH // 2, proj_tile(GA))
                pool.wait_ge(yb_ready, ybr.next(8))
                pool.wait_ge(ga_ready, 2 * (l + 1))
                pool.wait_ge(acc_taken, accs.next(4))
                turn(NH // 2, lambda o, k: pool.tensor_tensor(o, proj[:, :, ds(VB + k * P, P)], proj[:, :, ds(GB + k * P, P)],
                                                              ALU.mult))
                for g in range(4):
                    pool.wait_ge(acc_taken, accs.next())
                    b = g % 2
                    t = xres[:, :, g * CH:(g + 1) * CH]
                    pool.tensor_tensor(t, t, proj[:, 1, b * 1024:(b + 1) * 1024].rearrange("p (m n) -> p m n", m=M),
                                       ALU.add).then_inc(x_ready, 1)

            pool.wait_ge(rstd_ready, rstd.next())
            turn(KT // 2, x_tile)
            hin, hbr, hwr, hss = (Seen(pool, s) for s in (hg_turned, hg_b, hg_w, hg_ss))
            accs.skip(16)
            pool.wait_ge(ga_ready, 2 * DEPTH + 2)

            def hgrn_scale():
                pool.wait_ge(hg_ss, hss.next(2))
                link(pool.tensor_tensor(st[:, 2:4], st[:, 0:2], eps.broadcast_to([P, M]), ALU.add))
                pool.tensor_tensor(st[:, 4:6], st[:, 2:4], kst[:, C_PW:C_PW + 2], ALU.pow).then_inc(hg_rstd, 1)

            def hgrn(g, first):
                pool.wait_ge(hg_turned, hin.next())
                pool.tensor_copy(xn[:, 0, :, :], proj[:, :, ds(g * HD, HD)])
                pool.tensor_copy(xn[:, 1, :, :], proj[:, :, ds(1024 + g * HD, HD)]).then_inc(hg_in, 1)
                pool.wait_ge(hg_b, hbr.next())
                for _, first_half, second, mid in level_views(wk, hb):
                    pool.tensor_tensor(first_half[0], mid, first_half[1], ALU.subtract)
                pool.tensor_tensor(wk[:, LEVELS, 0:P], hb[:, P - 1:P].broadcast_to([P, P]), hb[:, 0:P],
                                   ALU.subtract).then_inc(hg_d1, 1)
                pool.wait_ge(hg_w, hwr.next())
                for _, first_half, second, mid in level_views(wk, hk):
                    pool.tensor_tensor(first_half[0], first_half[0], first_half[1], ALU.mult)
                pool.tensor_tensor(wk[:, LEVELS, 0:P], wk[:, LEVELS, 0:P], hk[:, 0:P], ALU.mult).then_inc(hg_x1, 1)
                if not first:
                    hgrn_scale()

            hgrn(0, True)
            with loop(pool, NH - 1, {hin: 1, hbr: 1, hwr: 1, hss: 2, linked: 1}) as i:
                hgrn(i + 1, False)
            hgrn_scale()
            accs.skip(8)
            pool.wait_ge(ga_ready, 2 * DEPTH + 3)
            cvf = Seen(pool, cv_turned)
            lgc = scr[:, 3584:4096].rearrange("p (b m d) -> p b m d", b=2, m=M)
            with loop(pool, 4, {cvf: 2}) as i:
                for b in range(2):
                    k = 2 * i + b
                    pool.wait_ge(cv_turned, cvf.next())
                    pool.tensor_tensor(xn[:, b, :, :], cg2[:, :, ds(k * P, P)], proj[:, :, ds(1024 + k * P, P)], ALU.mult)
                    pool.tensor_tensor(lgc[:, b, :, :], proj[:, :, ds(k * P, P)], proj[:, :, ds(2048 + k * P, P)],
                                       ALU.mult).then_inc(cv_in, 1)
            pool.wait_ge(cv_turned, cvf.ahead(2))
            turn(NH // 2, proj_tile(3072))
            pool.wait_ge(acc_taken, accs.next(8))
            turn(KT // 2, lambda o, k: pool.tensor_tensor(o, proj[:, :, ds(4096 + k * P, P)], proj[:, :, ds(6144 + k * P, P)],
                                                          ALU.add))
            pool.wait_ge(rstd_ready, rstd.next())
            turn(KT // 2, x_tile)
            pool.wait_ge(p_landed, 16)
            turn(1, proj_tile(6144))


_INS = ["x", "c", "positions", "rel_bias", "norm_gain", "w_mod", "b_mod", "w_in", "q_norm_gain", "k_norm_gain",
        "ret_norm_gain", "w_out", "p_2", "norm_mix_g_2", "w_in_2", "conv_w_2", "lb_param_2", "hg_norm_g_2",
        "w_a_out_2", "w_b_out_2", "w_o_2", "ple_norm_g_2", "w_ple_gate_2", "w_ple_proj_2", "final_norm_g_2"]


def kernel(**inputs):
    import concourse.bacc as bacc
    from concourse.bass_utils import run_bass_kernel_spmd

    nc = bacc.Bacc("TRN2", target_bir_lowering=False, num_devices=1)
    arrays, args = {}, []
    consts, levels = constants()
    for name, a in [(n, np.ascontiguousarray(inputs[n])) for n in _INS] + [("consts", consts), ("levels", levels)]:
        arrays["in_" + name] = a
        args.append(nc.dram_tensor("in_" + name, a.shape, mybir.dt.from_np(a.dtype), kind="ExternalInput").ap())
    out = nc.dram_tensor("out_0", (1, S, D), F32, kind="ExternalOutput").ap()
    build(nc, *args, out)
    r = run_bass_kernel_spmd(nc, [arrays], core_ids=[0])
    return r.results[0]["out_0"]
```
